# Optimizing a Trainium2 kernel written in Bass

```python
import math
import jax, jax.numpy as jnp
from jax import lax
import numpy as np

D_MODEL = 1024
BATCH = 1
SEQ = 256
DEPTH = 2
DEC_BATCH = 8
DEC_SEQ = 4
PAST_LEN = 2048
PAGE_SIZE = 128

N_GDN_HEADS = 4
GDN_HEAD_DIM = 128
GDN_WIDTH = N_GDN_HEADS * GDN_HEAD_DIM
GDN_CONV_WIDTH = 4
GDN_CHUNK = 64
CONF_WIDTH = D_MODEL - GDN_WIDTH
CONF_GROUPS = 4
CONF_KERNEL = 31
D_FF_DENSE = 2816
N_EXPERTS = 8
TOP_K = 2
D_FF_EXPERT = 3584
MOE_BLOCK = 128
N_DENSE_LAYERS = (DEPTH + 1) // 2
N_MOE_LAYERS = DEPTH // 2
N_MOD = 6
RMS_EPS = 1e-6
LN_EPS = 1e-5
QKV_WIDTH = 3 * GDN_WIDTH
IN_WIDTH = QKV_WIDTH + GDN_WIDTH + 2 * N_GDN_HEADS + 2 * CONF_WIDTH

kernel_name = "hybrid_gdn_conformer_adaln_moe_step"

def rms_norm(x, g):
    xf = x.astype(jnp.float32)
    y = xf * lax.rsqrt(jnp.mean(xf * xf, axis=-1, keepdims=True) + RMS_EPS)
    return (y * g.astype(jnp.float32)).astype(x.dtype)

def l2_normalize(x):
    return x * lax.rsqrt(jnp.sum(x * x, axis=-1, keepdims=True) + 1e-6)

def causal_depthwise_conv(x, buf, w):
    width = w.shape[0]
    xp = jnp.concatenate([buf.astype(x.dtype), x], axis=1)
    y = lax.conv_general_dilated(xp, w[:, None, :].astype(x.dtype), window_strides=(1,), padding="VALID",
                                 dimension_numbers=("NWC", "WIO", "NWC"), feature_group_count=x.shape[-1])
    return y, xp[:, xp.shape[1] - (width - 1):]

def gated_delta_rule(q, k, v, g, beta, s0):
    bsz, seq, nh, dk = q.shape
    dv = v.shape[-1]
    c = math.gcd(seq, GDN_CHUNK)
    n = seq // c

    def chunks(t):
        t = t.reshape((bsz, n, c, nh) + t.shape[3:])
        return jnp.moveaxis(t, 3, 1)

    q, k, v, g, beta = chunks(q), chunks(k), chunks(v), chunks(g), chunks(beta)
    gc = jnp.cumsum(g, axis=-1)
    incl = jnp.tril(jnp.ones((c, c), dtype=bool))
    strict = jnp.tril(jnp.ones((c, c), dtype=bool), -1)
    decay = jnp.exp(jnp.where(incl, gc[..., :, None] - gc[..., None, :], -jnp.inf))
    kb = k * beta[..., None]
    a_mat = jnp.where(strict, jnp.einsum("bhnid,bhnjd->bhnij", kb, k) * decay, 0.0)
    eye = jnp.eye(c, dtype=q.dtype)
    t_inv = lax.linalg.triangular_solve(eye + a_mat, jnp.broadcast_to(eye, a_mat.shape),
                                        left_side=True, lower=True, unit_diagonal=True)
    u = jnp.einsum("bhnij,bhnjd->bhnid", t_inv, v * beta[..., None])
    w = jnp.einsum("bhnij,bhnjd->bhnid", t_inv, kb * jnp.exp(gc)[..., None])
    qk = jnp.where(incl, jnp.einsum("bhnid,bhnjd->bhnij", q, k) * decay, 0.0)
    q_dec = q * jnp.exp(gc)[..., None]
    k_dec = k * jnp.exp(gc[..., -1:] - gc)[..., None]
    g_last = jnp.exp(gc[..., -1])

    def step(s, inp):
        w_n, u_n, qd_n, kd_n, qk_n, gl_n = inp
        v_new = u_n - jnp.einsum("bhik,bhkv->bhiv", w_n, s)
        o_n = jnp.einsum("bhik,bhkv->bhiv", qd_n, s) + jnp.einsum("bhij,bhjv->bhiv", qk_n, v_new)
        s = s * gl_n[..., None, None] + jnp.einsum("bhik,bhiv->bhkv", kd_n, v_new)
        return s, o_n

    xs = tuple(jnp.moveaxis(t, 2, 0) for t in (w, u, q_dec, k_dec, qk, g_last))
    s_final, o = lax.scan(step, s0, xs)
    o = jnp.moveaxis(o, 0, 2).reshape(bsz, nh, seq, dv)
    return jnp.moveaxis(o, 1, 2), s_final

def gdn_mixer(qkv_in, z, b_raw, a_raw, conv_buf, s0, w_conv, a_log, dt_bias, g_out):
    bsz, seq, _ = qkv_in.shape
    f32 = jnp.float32
    qkv, new_buf = causal_depthwise_conv(qkv_in, conv_buf, w_conv)
    qkv = jax.nn.silu(qkv.astype(f32)).reshape(bsz, seq, 3, N_GDN_HEADS, GDN_HEAD_DIM)
    q = l2_normalize(qkv[:, :, 0]) * (GDN_HEAD_DIM ** -0.5)
    k = l2_normalize(qkv[:, :, 1])
    v = qkv[:, :, 2]
    beta = jax.nn.sigmoid(b_raw.astype(f32))
    g = -jnp.exp(a_log.astype(f32)) * jax.nn.softplus(a_raw.astype(f32) + dt_bias.astype(f32))
    o, s = gated_delta_rule(q, k, v, g, beta, s0.astype(f32))
    o = rms_norm(o, g_out) * jax.nn.silu(z.astype(f32).reshape(bsz, seq, N_GDN_HEADS, GDN_HEAD_DIM))
    return o.reshape(bsz, seq, GDN_WIDTH).astype(qkv_in.dtype), new_buf, s.astype(s0.dtype)

def conformer_conv(u, gate, buf, w_dw, b_dw, g_ln, b_ln):
    bsz, seq, _ = u.shape
    h = u * jax.nn.sigmoid(gate)
    y, new_buf = causal_depthwise_conv(h, buf, w_dw)
    y = (y + b_dw).astype(jnp.float32).reshape(bsz, seq, CONF_GROUPS, CONF_WIDTH // CONF_GROUPS)
    mu = jnp.mean(y, axis=-1, keepdims=True)
    var = jnp.mean(jnp.square(y - mu), axis=-1, keepdims=True)
    y = ((y - mu) * lax.rsqrt(var + LN_EPS)).reshape(bsz, seq, CONF_WIDTH) * g_ln.astype(jnp.float32) + b_ln.astype(jnp.float32)
    return jax.nn.silu(y).astype(u.dtype), new_buf

def swiglu(x, wg, wu, wd):
    return (jax.nn.silu(x @ wg) * (x @ wu)) @ wd

def moe_swiglu(h, w_r, b_r, wg, wu, wd):
    n_tok, dm = h.shape
    logits = h.astype(jnp.float32) @ w_r.astype(jnp.float32) + b_r.astype(jnp.float32)
    probs = jax.nn.softmax(logits, axis=-1)
    top_p, top_e = lax.top_k(probs, TOP_K)
    top_p = top_p / jnp.sum(top_p, axis=-1, keepdims=True)
    n_asg = n_tok * TOP_K
    flat_e = top_e.reshape(n_asg)
    flat_p = top_p.reshape(n_asg)
    flat_tok = jnp.arange(n_asg, dtype=jnp.int32) // TOP_K
    order = jnp.argsort(flat_e)
    se, stok, sp = flat_e[order], flat_tok[order], flat_p[order]
    counts = jnp.bincount(flat_e, length=N_EXPERTS)
    padded = (counts + MOE_BLOCK - 1) // MOE_BLOCK * MOE_BLOCK
    pad_end = jnp.cumsum(padded)
    pad_start = pad_end - padded
    start = jnp.cumsum(counts) - counts
    dest = pad_start[se] + jnp.arange(n_asg) - start[se]
    n_blocks = (n_asg + MOE_BLOCK - 1) // MOE_BLOCK + N_EXPERTS
    n_slots = n_blocks * MOE_BLOCK
    slot_tok = jnp.full((n_slots,), n_tok, jnp.int32).at[dest].set(stok)
    block_e = jnp.minimum(jnp.searchsorted(pad_end, jnp.arange(n_blocks) * MOE_BLOCK, side="right"), N_EXPERTS - 1)
    h_pad = jnp.concatenate([h, jnp.zeros((1, dm), h.dtype)], axis=0)
    xb = h_pad[slot_tok].reshape(n_blocks, MOE_BLOCK, dm)

    def expert_block(args):
        xblk, e = args
        return swiglu(xblk, wg[e], wu[e], wd[e])

    yb = lax.map(expert_block, (xb, block_e)).reshape(n_slots, dm)
    contrib = yb[dest] * sp[:, None].astype(h.dtype)
    return jax.ops.segment_sum(contrib, stok, num_segments=n_tok)

def decoder_trunk(x, c, gdn_conv0, gdn_state0, conf_conv0, params):
    (w_ada, b_ada, g_norm1, g_norm2, w_in, w_gdn_conv, a_log, dt_bias, g_gdn_out,
     w_conf_dw, b_conf_dw, g_conf_ln, b_conf_ln, w_out,
     w_ff_gate, w_ff_up, w_ff_down, w_router, b_router, w_exp_gate, w_exp_up, w_exp_down, g_final) = params
    bsz, seq, _ = x.shape
    o1 = QKV_WIDTH
    o2 = o1 + GDN_WIDTH
    o3 = o2 + N_GDN_HEADS
    o4 = o3 + N_GDN_HEADS
    o5 = o4 + CONF_WIDTH
    new_s, new_conv, new_conf = [], [], []
    for layer in range(DEPTH):
        mod = (jax.nn.silu(c) @ w_ada[layer] + b_ada[layer])[:, None, :]
        shift1, scale1, gate1, shift2, scale2, gate2 = jnp.split(mod, N_MOD, axis=-1)
        h = rms_norm(x, g_norm1[layer]) * (1 + scale1) + shift1
        proj = h @ w_in[layer]
        qkv_in, z, b_raw, a_raw, glu_u, glu_g = jnp.split(proj, [o1, o2, o3, o4, o5], axis=-1)
        o_a, buf_a, s_a = gdn_mixer(qkv_in, z, b_raw, a_raw, gdn_conv0[layer], gdn_state0[layer],
                                    w_gdn_conv[layer], a_log[layer], dt_bias[layer], g_gdn_out[layer])
        o_b, buf_b = conformer_conv(glu_u, glu_g, conf_conv0[layer], w_conf_dw[layer], b_conf_dw[layer],
                                    g_conf_ln[layer], b_conf_ln[layer])
        x = x + gate1 * (jnp.concatenate([o_a, o_b], axis=-1) @ w_out[layer])
        h = rms_norm(x, g_norm2[layer]) * (1 + scale2) + shift2
        idx = layer // 2
        if layer % 2 == 0:
            f = swiglu(h, w_ff_gate[idx], w_ff_up[idx], w_ff_down[idx])
        else:
            f = moe_swiglu(h.reshape(bsz * seq, D_MODEL), w_router[idx], b_router[idx],
                           w_exp_gate[idx], w_exp_up[idx], w_exp_down[idx]).reshape(bsz, seq, D_MODEL)
        x = x + gate2 * f
        new_s.append(s_a)
        new_conv.append(buf_a)
        new_conf.append(buf_b)
    return rms_norm(x, g_final), jnp.stack(new_s), jnp.stack(new_conv), jnp.stack(new_conf)

def setup_inputs(seed: int = 0) -> dict:
    key = jax.random.key(seed)
    ks = jax.random.split(key, 32)
    f32 = jnp.float32
    D = D_MODEL

    def nrm(i, shape, scale):
        return jax.random.normal(ks[i], shape, f32) * scale

    dt = jnp.exp(jax.random.uniform(ks[14], (DEPTH, N_GDN_HEADS), f32, math.log(1e-3), math.log(1e-1)))
    return {
        "x_prompt": nrm(0, (BATCH, SEQ, D), 1.0),
        "x_sample": nrm(1, (DEC_BATCH, DEC_SEQ, D), 1.0),
        "c_prompt": nrm(2, (BATCH, D), 1.0),
        "c_sample": nrm(3, (DEC_BATCH, D), 1.0),
        "state_gdn": nrm(4, (DEPTH, DEC_BATCH, N_GDN_HEADS, GDN_HEAD_DIM, GDN_HEAD_DIM), 0.1),
        "state_gdn_conv": nrm(5, (DEPTH, DEC_BATCH, GDN_CONV_WIDTH - 1, QKV_WIDTH), 1.0),
        "state_conf_conv": nrm(6, (DEPTH, DEC_BATCH, CONF_KERNEL - 1, CONF_WIDTH), 0.5),
        "w_ada": nrm(7, (DEPTH, D, N_MOD * D), 0.5 * D ** -0.5),
        "b_ada": nrm(8, (DEPTH, N_MOD * D), 0.01),
        "g_norm1": 1.0 + nrm(9, (DEPTH, D), 0.01),
        "g_norm2": 1.0 + nrm(10, (DEPTH, D), 0.01),
        "w_in": nrm(11, (DEPTH, D, IN_WIDTH), D ** -0.5),
        "w_gdn_conv": nrm(12, (DEPTH, GDN_CONV_WIDTH, QKV_WIDTH), GDN_CONV_WIDTH ** -0.5),
        "a_log": jnp.log(jax.random.uniform(ks[13], (DEPTH, N_GDN_HEADS), f32, 1.0, 16.0)),
        "dt_bias": dt + jnp.log(-jnp.expm1(-dt)),
        "g_gdn_out": 1.0 + nrm(15, (DEPTH, GDN_HEAD_DIM), 0.01),
        "w_conf_dw": nrm(16, (DEPTH, CONF_KERNEL, CONF_WIDTH), CONF_KERNEL ** -0.5),
        "b_conf_dw": nrm(17, (DEPTH, CONF_WIDTH), 0.01),
        "g_conf_ln": 1.0 + nrm(18, (DEPTH, CONF_WIDTH), 0.01),
        "b_conf_ln": nrm(19, (DEPTH, CONF_WIDTH), 0.01),
        "w_out": nrm(20, (DEPTH, D, D), D ** -0.5),
        "w_ff_gate": nrm(21, (N_DENSE_LAYERS, D, D_FF_DENSE), D ** -0.5),
        "w_ff_up": nrm(22, (N_DENSE_LAYERS, D, D_FF_DENSE), D ** -0.5),
        "w_ff_down": nrm(23, (N_DENSE_LAYERS, D_FF_DENSE, D), D_FF_DENSE ** -0.5),
        "w_router": nrm(24, (N_MOE_LAYERS, D, N_EXPERTS), D ** -0.5),
        "b_router": nrm(25, (N_MOE_LAYERS, N_EXPERTS), 0.01),
        "w_exp_gate": nrm(26, (N_MOE_LAYERS, N_EXPERTS, D, D_FF_EXPERT), D ** -0.5),
        "w_exp_up": nrm(27, (N_MOE_LAYERS, N_EXPERTS, D, D_FF_EXPERT), D ** -0.5),
        "w_exp_down": nrm(28, (N_MOE_LAYERS, N_EXPERTS, D_FF_EXPERT, D), D_FF_EXPERT ** -0.5),
        "g_final": 1.0 + nrm(29, (D,), 0.01),
    }

def reference(x_prompt, x_sample, c_prompt, c_sample, state_gdn, state_gdn_conv, state_conf_conv,
              w_ada, b_ada, g_norm1, g_norm2, w_in, w_gdn_conv, a_log, dt_bias, g_gdn_out,
              w_conf_dw, b_conf_dw, g_conf_ln, b_conf_ln, w_out,
              w_ff_gate, w_ff_up, w_ff_down, w_router, b_router, w_exp_gate, w_exp_up, w_exp_down, g_final):
    params = (w_ada, b_ada, g_norm1, g_norm2, w_in, w_gdn_conv, a_log, dt_bias, g_gdn_out,
              w_conf_dw, b_conf_dw, g_conf_ln, b_conf_ln, w_out,
              w_ff_gate, w_ff_up, w_ff_down, w_router, b_router, w_exp_gate, w_exp_up, w_exp_down, g_final)
    bsz = x_prompt.shape[0]
    dt = x_prompt.dtype
    zero_s = jnp.zeros((DEPTH, bsz, N_GDN_HEADS, GDN_HEAD_DIM, GDN_HEAD_DIM), dt)
    zero_conv = jnp.zeros((DEPTH, bsz, GDN_CONV_WIDTH - 1, QKV_WIDTH), dt)
    zero_conf = jnp.zeros((DEPTH, bsz, CONF_KERNEL - 1, CONF_WIDTH), dt)
    y_prompt, s_p, conv_p, conf_p = decoder_trunk(x_prompt, c_prompt, zero_conv, zero_s, zero_conf, params)
    y_sample, s_s, conv_s, conf_s = decoder_trunk(x_sample, c_sample, state_gdn_conv, state_gdn,
                                                  state_conf_conv, params)
    return (y_prompt, y_sample, s_p, conv_p, conf_p, s_s, conv_s, conf_s)


_drawn_inputs = setup_inputs


def setup_inputs(seed=0):
    import zlib

    import numpy as np

    out = dict(_drawn_inputs(seed))
    spreads = {}
    factors = {'g_norm1': 3.609,
     'g_norm2': 5.345,
     'g_gdn_out': 3.754,
     'b_conf_dw': 6.306,
     'g_conf_ln': 8.0,
     'b_conf_ln': 7.801,
     'g_final': 5.842}
    for name, (base, spread) in spreads.items():
        noise = np.random.default_rng([zlib.crc32(name.encode()), seed]).standard_normal(out[name].shape)
        drawn = base * np.exp(spread * noise) if base else spread * noise
        out[name] = __import__('jax').numpy.asarray(drawn.astype(out[name].dtype))
    for name, factor in factors.items():
        out[name] = (out[name] * factor).astype(out[name].dtype)
    return out
```

```python
from contextlib import ExitStack

import numpy as np

import concourse.bass as bass
from concourse import mybir

F32 = mybir.dt.float32
F32R = mybir.dt.float32r
I32 = mybir.dt.int32
ACT = mybir.ActivationFunctionType
ALU = mybir.AluOpType
AX = mybir.AxisListType

P = 128
D = 1024
KD = D // P
DEPTH = 2
TP, NB, TD = 256, 8, 4
TS = NB * TD
T = TP + TS
NC_ = 1 + NB
H = 4
QKV_T = 3 * H
CW = 4
CK = 31
CT = 4
MODS = 6
FT = 2816 // P
NE = 8
FE = 3584
FC = FE // 512
IN_W = 3080
QPAD = TP + CW - 1 + NB * (TD + CW - 1)
CPAD = TP + CK - 1 + NB * (TD + CK - 1)
QSAMP, QSEG = TP + CW - 1, TD + CW - 1
CSAMP, CSEG = TP + CK - 1, TD + CK - 1
QOUT = QPAD - (CW - 1)

UNIT = 2048
NRAW, NSPLIT, LEAD = 6, 3, 2
N_ADA, N_IN, N_OUT, N_UP, N_DOWN = 24, 12, 4, FT, FT * KD // 16
PER_EXPERT = FC * 6
U_ADA, U_IN, U_OUT = [0, 0], [0, 0], [0, 0]
U_ADA[0] = 0
U_IN[0] = U_ADA[0] + N_ADA
U_ADA[1] = U_IN[0] + N_IN
U_OUT[0] = U_ADA[1] + N_ADA
U_UP = U_OUT[0] + N_OUT
U_DOWN = U_UP + N_UP
U_IN[1] = U_DOWN + N_DOWN
U_OUT[1] = U_IN[1] + N_IN
U_MOE = U_OUT[1] + N_OUT
N_UNITS = U_MOE + NE * PER_EXPERT

COL_Z, COL_B, COL_U, COL_G = 1536, 2048, 2056, 2568
IN_COLS = []
for _c in range(CT):
    IN_COLS += [COL_U + _c * P, COL_G + _c * P]
IN_COLS += [m * P for m in range(QKV_T)]
IN_COLS += [COL_Z + h * P for h in range(H)]


SCATTER_AT = range(1, 17, 2)
GATHER_AT = (18, 21, 24, 27, 30)


def expert_units():
    order = []
    for c in range(FC):
        order += [("g", c, 0), ("g", c, 1), ("u", c, 0), ("u", c, 1)]
        if c >= 1:
            order += [("d", c - 1, 0), ("d", c - 1, 1)]
    return order + [("d", FC - 1, 0), ("d", FC - 1, 1)]


def columns(sizes):
    at, out = 0, {}
    for name, n in sizes:
        out[name] = (at, at + n)
        at += n
    return out, at


_sizes = []
for _l in range(DEPTH):
    _sizes += [(f"b_ada{_l}", MODS * KD), (f"g1{_l}", KD), (f"g2{_l}", KD), (f"wq{_l}", QKV_T * CW),
               (f"wc{_l}", CT * CK), (f"bc{_l}", CT), (f"gln{_l}", CT), (f"bln{_l}", CT), (f"gout{_l}", 1),
               (f"wab{_l}", KD * 8), (f"alog{_l}", 12), (f"dt{_l}", 12)]
_sizes += [("wr", KD * NE), ("br", 3 * NE), ("gf", KD)]
PCOL, NPAR = columns(_sizes)

LEVELS = [2, 4, 8, 16, 32, 64]
CCOL, NCONST = columns(
    [("ones", P), ("ident", P), ("tri", P), ("after", P), ("m1l", P), ("m1t", P)]
    + [(f"mt{s}", P) for s in LEVELS]
    + [("before", P), ("iota", P), ("triS", P), ("afterS", P), ("seqf", NB * TS), ("seqp", NB),
       ("comb", NC_), ("eps6", 1), ("eps5", 1), ("epsq", 1), ("one", 1), ("ipart", 1), ("valid", 1),
       ("rank", 3 * NE), ("eye8", NE + 1)])


def constants():
    c = np.zeros((P, NCONST), np.float32)

    def put(name, a):
        lo, _ = CCOL[name]
        c[:a.shape[0], lo:lo + a.shape[1]] = a

    i, j = np.arange(P)[:, None], np.arange(P)[None, :]
    put("ones", np.ones((P, P)))
    put("ident", i == j)
    put("tri", i <= j)
    put("after", i > j)
    low = lambda s: (i // (2 * s) == j // (2 * s)) & (i % (2 * s) >= s) & (j % (2 * s) < s)
    put("m1l", low(1))
    put("m1t", low(1).T)
    for s in LEVELS:
        put(f"mt{s}", low(s).T)
    put("before", i < j)
    put("iota", np.broadcast_to(j, (P, P)))
    same = (i // TD == j // TD) & (i < TS) & (j < TS)
    put("triS", same & (i <= j))
    put("afterS", same & (i > j))
    seq = np.arange(TS)[None, :] // TD == np.arange(NB)[:, None]
    put("seqf", np.broadcast_to(seq.reshape(1, -1), (P, NB * TS)))
    put("seqp", np.arange(TS)[:, None] // TD == np.arange(NB)[None, :])
    put("comb", np.concatenate([np.eye(NC_), np.eye(NC_)]))
    put("eps6", np.full((P, 1), 1e-6))
    put("eps5", np.full((P, 1), 1e-5))
    put("epsq", np.full((P, 1), P * 1e-6))
    put("one", np.ones((P, 1)))
    put("ipart", i)
    put("valid", i < TS)
    put("rank", np.broadcast_to(NE - np.tile(np.arange(NE), 3)[None, :], (P, 3 * NE)))
    put("eye8", np.eye(NE))
    return c


class Steps:

    def __init__(self, eng, sem, at=0, extra=None):
        self.eng, self.sem, self.n, self.extra = eng, sem, at, extra

    def __call__(self, instruction):
        self.n += 1
        instruction.then_inc(self.sem, 1)
        self.eng.wait_ge(self.sem, self.n if self.extra is None else self.extra + self.n)


def later(value, it=None, per=0):
    return value if it is None else it * per + value


def program(nc, units, x_in, c_in, par_in, const_in, gdn_in, qst_in, cst_in,
            y_out, gdnp_out, gdns_out, qst_out, cst_out):
    ctx = ExitStack()
    with ctx:
        base = (nc.sbuf_base + 63) // 64 * 64
        room = nc.sbuf_usable_end - base - 64
        ctx.enter_context(nc.sbuf_tensor("arena", [P, room // 4], F32))
        cursor = [base]

        def at(name, offset, cols, dt=F32):
            return nc.alloc_sbuf_tensor_at(name, [P, cols], dt, offset=offset)

        def keep(name, cols, dt=F32):
            offset = cursor[0]
            cursor[0] = (offset + cols * 4 + 31) // 32 * 32
            assert cursor[0] <= base + room, (name, cursor[0] - base - room)
            return at(name, offset, cols, dt)

        raw = [keep(f"raw{i}", UNIT) for i in range(NRAW)]
        whi = [keep(f"whi{i}", UNIT, F32R) for i in range(NSPLIT)]
        wlo = [keep(f"wlo{i}", UNIT, F32R) for i in range(NSPLIT)]
        x = keep("x", KD * T)
        par = keep("par", NPAR)
        con = keep("con", NCONST)
        mod = [keep(f"mod{l}", MODS * KD * NC_) for l in range(DEPTH)]
        gain = [keep(f"gain{i}", KD * NC_) for i in range(2 * DEPTH)]
        rstd = keep("rstd", T)
        cstat = keep("cstat", KD * 2 * NC_, F32R)
        sg = keep("sg", 2 * T)
        ctmp = keep("ctmp", 2 * 316)
        small = keep("small", 576)
        posT = keep("posT", T)
        npass_i = keep("npass_i", 1, I32)
        r0 = cursor[0]
        h_hi = at("h_hi", r0, KD * T, F32R)
        h_lo = at("h_lo", r0 + 9216, KD * T, F32R)
        hf = at("hf", r0 + 18432, KD * T)
        sq = at("sq", r0 + 27648, KD * T)
        cs = at("cs", r0, KD * NC_)
        modrow = [at(f"modrow{i}", r0 + 27648 + 2048 * i, 512) for i in range(3)]
        qkv = at("qkv", r0 + 36864, QKV_T * T)
        zs = at("zs", r0 + 50688, H * T)
        yc = at("yc", r0 + 55296, CT * T)
        qpad = at("qpad", r0 + 59904, QKV_T * QPAD)
        cpad = at("cpad", r0 + 75040, CT * CPAD)
        oall = at("oall", r0 + 84480, H * T)
        qrs = [at(f"qrs{i}", r0 + 4608 * i, H * T) for i in range(2)]
        csq = at("csq", r0 + 9216, CT * T)
        crs = at("crs", r0 + 13824, CT * T)
        names = ["da", "dq", "AT", "L", "LT", "PM", "MT", "er"]
        blk = [{n: at(f"{n}{b}", r0 + 2048 * (8 * b + i), H * P) for i, n in enumerate(names)} for b in range(2)]
        S = at("S", r0 + 32768, H * P)
        sst = [at(f"sst{h}", r0 + 59904 + 4096 * h, NB * P) for h in range(H)]
        nwx = at("nwx", r0 + 76288, H * NB * TS)
        vx = at("vx", r0 + 80384, NB * P)
        osq = at("osq", r0 + 18432, H * T)
        ors = at("ors", r0 + 23040, H * T)
        act_hi = at("act_hi", r0 + 18432, FT * T, F32R)
        act_lo = at("act_lo", r0 + 43776, FT * T, F32R)
        tok_hi = at("tok_hi", r0 + 36864, 3 * D, F32R)
        tok_lo = at("tok_lo", r0 + 49152, 3 * D, F32R)
        facc = at("facc", r0 + 61440, KD * T)
        ht_hi = [at(f"ht_hi{i}", r0 + 70656 * i, D, F32R) for i in range(2)]
        ht_lo = [at(f"ht_lo{i}", r0 + 70656 * i + 4096, D, F32R) for i in range(2)]
        xe = at("xe", r0 + 78848, D)
        sge = [at(f"sge{i}", r0 + 8192 + 2048 * i, 512) for i in range(2)]
        ae = [at(f"ae{i}", r0 + 12288 + 2048 * i, 512) for i in range(2)]
        at_hi = at("at_hi", r0 + 16384, 512, F32R)
        at_lo = at("at_lo", r0 + 18432, 512, F32R)
        ye_hi = at("ye_hi", r0 + 20480, D, F32R)
        ye_lo = at("ye_lo", r0 + 24576, D, F32R)
        pe_sel = at("pe_sel", r0 + 28672, 3 * P, F32R)
        pt_sel = [at(f"pt_sel{i}", r0 + 30208 + i * 52736, T, F32R) for i in range(2)]
        pos_e = at("pos_e", r0 + 31360, T)
        assert r0 + 89088 <= base + room, (base + room - r0)
        ps = ctx.enter_context(nc.psum_tensor("ps", [P, 8, 512], F32))

        def cut(t, lo, n):
            return t[:, lo:lo + n]

        ab, beta, gg, gcs, bEG, eg, t0, t1, t2, glb = (
            cut(small, o, n) for o, n in [(0, 24), (24, 12), (36, 12), (48, 12), (60, 12), (72, 24), (96, 12),
                                          (108, 12), (120, 12), (448, 32)])
        lg, ex, o1, o2, scr, sel = (cut(small, 160 + 24 * i, 24) for i in range(6))
        wgt, posm = (cut(small, 512 + 32 * i, 3 * NE + 1) for i in range(2))
        m1, m2, rs3, cnt, npf, npf2 = (cut(small, 352 + 8 * i, 8) for i in range(6))
        pslot = [cut(small, 400 + i, 1) for i in range(2)]
        stmp = [cut(small, 416, 32), cut(small, 480, 32)]

        def pc(name, lo=0, n=None):
            a, b = PCOL[name]
            return par[:, a + lo:(b if n is None else a + lo + n)]

        def cc(name, rows=P, cols=None):
            a, b = CCOL[name]
            return con[0:rows, a:(b if cols is None else a + cols)]

        def kt(t, n=KD):
            return t[:, :].rearrange("p (k t) -> p k t", k=n)

        x3, hi3, lo3, hf3, sq3 = kt(x), kt(h_hi), kt(h_lo), kt(hf), kt(sq)
        qp3, cp3 = kt(qpad, QKV_T), kt(cpad, CT)

        def seqs(a):
            return a[:, TP:T].rearrange("p (b t) -> p b t", t=TD)

        def per_token(m9):
            return m9[:, :, 1:NC_].unsqueeze(3).to_broadcast([P, m9.shape[1], NB, TD])

        mod3 = [m[:, :].rearrange("p (s k c) -> p s k c", s=MODS, k=KD) for m in mod]
        gain3 = [g[:, :].rearrange("p (k c) -> p k c", k=KD) for g in gain]

        sem = lambda name: ctx.enter_context(nc.semaphore(name))
        raw_in = [sem(f"raw_in{i}") for i in range(NRAW)]
        hi_split = sem("hi_split")
        lo_split = sem("lo_split")
        unit_used = sem("unit_used")
        tile_done = sem("tile_done")
        bank_free = [sem(f"bank_free{i}") for i in range(4)]
        small_in, x_loaded, c_loaded = sem("small_in"), sem("x_loaded"), sem("c_loaded")
        dve_step, act_step = sem("dve_step"), sem("act_step")
        cs_ready, cstat_ready, expa_ready = sem("cs_ready"), sem("cstat_ready"), sem("expa_ready")
        row_ready, modT_ready, mod_ready = sem("row_ready"), sem("modT_ready"), sem("mod_ready")
        x_ready, sq_ready, ss_ready, rstd_ready = sem("x_ready"), sem("sq_ready"), sem("ss_ready"), sem("rstd_ready")
        hf_ready, hhi_ready, hlo_ready = sem("hf_ready"), sem("hhi_ready"), sem("hlo_ready")
        pad_ready, sig_ready, glu_ready, qkv_ready = sem("pad_ready"), sem("sig_ready"), sem("glu_ready"), sem("qkv_ready")
        z_ready, ab_done, ab_copied, conv_done = sem("z_ready"), sem("ab_done"), sem("ab_copied"), sem("conv_done")
        conf_done, silu_done = sem("conf_done"), sem("silu_done")
        qsq_ready, qss_ready, qrs_ready, qn_ready = sem("qsq_ready"), sem("qss_ready"), sem("qrs_ready"), sem("qn_ready")
        cmean_done, cent_ready, csq_ready, css_ready = sem("cmean_done"), sem("cent_ready"), sem("csq_ready"), sem("css_ready")
        crs_ready, cn_ready, cy_ready = sem("crs_ready"), sem("cn_ready"), sem("cy_ready")
        beta_ready, abs_ready, sp_ready, g_ready = sem("beta_ready"), sem("abs_ready"), sem("sp_ready"), sem("g_ready")
        cum_ready, eg_ready, beg_ready = sem("cum_ready"), sem("eg_ready"), sem("beg_ready")
        gb_ready, mm1_done, er_ready, diff_ready, dexp_ready, dmask_ready = (
            sem(n) for n in ("gb_ready", "mm1_done", "er_ready", "diff_ready", "dexp_ready", "dmask_ready"))
        A_ready, qk_ready, at_done, at_copied, linit_ready = (
            sem(n) for n in ("A_ready", "qk_ready", "at_done", "at_copied", "linit_ready"))
        mt_ready, pm_done, pm_copied, q_done, l_ready = (
            sem(n) for n in ("mt_ready", "pm_done", "pm_copied", "q_done", "l_ready"))
        kv_done, kv_ready, w_done, nw_ready, qd_ready = (
            sem(n) for n in ("kv_done", "kv_ready", "w_done", "nw_ready", "qd_ready"))
        vn_done, vn_ready, o_done, o_copied, s_done, s_ready = (
            sem(n) for n in ("vn_done", "vn_ready", "o_done", "o_copied", "s_done", "s_ready"))
        nwx_ready, vx_ready, sst_in, sst_done, sst_ready = (
            sem(n) for n in ("nwx_ready", "vx_ready", "sst_in", "sst_done", "sst_ready"))
        osq_ready, oss_ready, ors_ready, o_ready, mhi_ready, mlo_ready = (
            sem(n) for n in ("osq_ready", "oss_ready", "ors_ready", "o_ready", "mhi_ready", "mlo_ready"))
        gate_ready, prod_ready, ahi_ready, alo_ready = (
            sem(n) for n in ("gate_ready", "prod_ready", "ahi_ready", "alo_ready"))
        pads_in, pads_out, st_out, p_out, y_ready, y_sent = (
            sem(n) for n in ("pads_in", "pads_out", "st_out", "p_out", "y_ready", "y_sent"))
        tokT_done, tok_hi_ready, tok_lo_ready, lg_done, lg_ready, lsub_ready, lexp_ready = (
            sem(n) for n in ("tokT_done", "tok_hi_ready", "tok_lo_ready", "lg_done", "lg_ready", "lsub_ready", "lexp_ready"))
        sel_ready, pos_done, npass_ready, posT_done, posT_ready = (
            sem(n) for n in ("sel_ready", "pos_done", "npass_ready", "posT_done", "posT_ready"))
        psel_ready, gx_done, gx_copied, gt_done, gw_done, hthi_ready, htlo_ready, ptsel_ready = (
            sem(n) for n in ("psel_ready", "gx_done", "gx_copied", "gt_done", "gw_done", "hthi_ready", "htlo_ready", "ptsel_ready"))
        eg_gate, eg_prod, eT_done, eahi_ready, ealo_ready = (
            sem(n) for n in ("eg_gate", "eg_prod", "eT_done", "eahi_ready", "ealo_ready"))
        yhi_ready, ylo_ready, scat_done, facc_added, moe_step, fin_step = (
            sem(n) for n in ("yhi_ready", "ylo_ready", "scat_done", "facc_added", "moe_step", "fin_step"))
        moe_done, pass_step = sem("moe_done"), sem("pass_step")

        tiles = {}
        uses, done = [0] * 4, [0]

        def place(key, bank, unit=None):
            if unit is None:
                done[0] += 1
            tiles[key] = (bank, uses[bank], (tile_done, done[0]) if unit is None else (unit_used, unit + 1))
            uses[bank] += 1

        def place_pairs(phase, first_unit, n):
            for i in range(n):
                place((phase, i, 0), 2 * (i % 2))
                place((phase, i, 1), 2 * (i % 2) + 1, first_unit + i)

        def place_down():
            for d in range(KD):
                end = FT * (d + 1)
                place(("down", d), d % 4, U_DOWN + end // 16 - 1 if end % 16 == 0 else None)

        place_pairs(("in", 0), U_IN[0], N_IN)
        place_pairs(("out", 0), U_OUT[0], N_OUT)
        place_pairs("up", U_UP, N_UP)
        place_down()
        place_pairs(("in", 1), U_IN[1], N_IN)
        place_pairs(("out", 1), U_OUT[1], N_OUT)
        uses_at = {l: [tiles[(("in", l), N_IN - 2 + b // 2, b % 2)][1] + 1 for b in range(4)] for l in range(DEPTH)}

        block = ctx.enter_context(nc.Block())

        @block.sync
        def _(sp):
            sp.dma_start(con[:, :], const_in).then_inc(small_in, 16)
            sp.dma_start(par[:, :], par_in).then_inc(small_in, 16)
            sp.dma_start(cs[:, :], c_in).then_inc(c_loaded, 16)

            def load(u, index, it=None, per=0, first=False):
                at_ = sp.snap(index * (P * UNIT)) if it is not None else index * (P * UNIT)
                if not first:
                    sp.wait_ge(lo_split, later(u - NRAW + 1, it, per))
                src = flat[bass.ds(at_, P * UNIT)].rearrange("(p n) -> p n", p=P)
                sp.dma_start(raw[u % NRAW][:, :], src).then_inc(raw_in[u % NRAW], 16)

            flat = units.rearrange("u p n -> (u p n)")
            for u in range(NRAW):
                load(u, u, first=True)
                if u == 1:
                    sp.dma_start(x[:, :], x_in).then_inc(x_loaded, 16)
            turns = U_MOE // NRAW - 1
            with sp.Fori(0, turns) as i:
                for u in range(NRAW, 2 * NRAW):
                    load(u, i * NRAW + u, i, NRAW)
            for u in range((turns + 1) * NRAW, U_MOE + NRAW):
                load(u, u)
            sp.wait_ge(npass_ready, 1)
            n_pass = sp.value_load(npass_i[0:1, 0:1], min_val=1, max_val=3)
            with sp.Fori(0, n_pass) as p_:
                with sp.Fori(0, NE) as e_:
                    for k in range(PER_EXPERT):
                        load(U_MOE + NRAW + k, e_ * PER_EXPERT + (U_MOE + NRAW + k), p_ * NE + e_, PER_EXPERT)
            def landed(u):
                return sp.snap(n_pass * (NE * PER_EXPERT // NRAW * 16) + 16 * (u // NRAW + 1))

            sp.wait_ge(raw_in[U_MOE % NRAW], landed(U_MOE))
            sp.wait_ge(y_ready, 1)
            sp.dma_start(y_out[:, 0:KD * T // 2], hf[:, 0:KD * T // 2]).then_inc(y_sent, 16)
            last = landed(U_MOE + 1)
            assert U_MOE % NRAW == NRAW - 1
            for u in range(U_MOE + 1, U_MOE + NRAW):
                sp.wait_ge(raw_in[u % NRAW], last)
            sp.dma_start(y_out[:, KD * T // 2:], hf[:, KD * T // 2:]).then_inc(y_sent, 16)
            sp.wait_ge(y_sent, 32)

        @block.gpsimd
        def _(pool):
            def mask_heads(out, in_, mask, n):
                return pool.tensor_tensor(out, in_, mask.unsqueeze(1).to_broadcast([n, H, n]), ALU.mult)

            def heads(t, rows, n):
                return t[0:rows, 0:H * n].rearrange("p (h n) -> p h n", h=H)

            def gate_rows(l, b, blk_i, n):
                src = gg[0:n, blk_i * H:(blk_i + 1) * H].unsqueeze(2).to_broadcast([n, H, P])
                pool.tensor_copy(heads(blk[b]["MT"], n, P), src).then_inc(gb_ready, 1)

            def masks(l, b, blk_i, n):
                pool.wait_ge(dexp_ready, 3 * l + blk_i + 1)
                strict, incl = ("afterS", "triS") if blk_i == 2 else ("after", "tri")
                da, dq = heads(blk[b]["da"], n, n), heads(blk[b]["dq"], n, n)
                mask_heads(da, da, cc(strict, n, n), n)
                mask_heads(dq, dq, cc(incl, n, n), n).then_inc(dmask_ready, 1)

            def level_mask(l, b, blk_i, n, q, s):
                pool.wait_ge(at_copied, 3 * l + blk_i + 1)
                if q >= 2 and q < 12:
                    pool.wait_ge(pm_done, 13 * l + q - 1)
                mask_heads(heads(blk[b]["MT"], n, n), heads(blk[b]["AT"], n, n), cc(f"mt{s}", n, n), n)\
                    .then_inc(mt_ready, 1)

            pool.wait_ge(small_in, 32)
            for l in range(DEPTH):
                if l:
                    pool.wait_ge(st_out, 64 * l)
                    pool.wait_ge(x_ready, 2 * l)
                pool.memset(qp3[:, :, 0:CW - 1], 0.0)
                pool.memset(cp3[:, :, 0:CK - 1], 0.0).then_inc(pad_ready, 1)
                pool.dma_start(qp3[:, :, QSAMP:QPAD], qst_in[l].rearrange("p (m s) -> p m s", m=QKV_T)).then_inc(pads_in, 16)
                pool.dma_start(cp3[:, :, CSAMP:CPAD], cst_in[l].rearrange("p (m s) -> p m s", m=CT)).then_inc(pads_in, 16)
                pool.wait_ge(conv_done, QKV_T * (l + 1))
                pool.wait_ge(conf_done, l + 1)
                pool.dma_start(qst_out[l], qpad[:, :]).then_inc(pads_out, 16)
                pool.dma_start(cst_out[l], cpad[:, :]).then_inc(pads_out, 16)
                pool.wait_ge(g_ready, l + 1)
                pool.wait_ge(cn_ready, l + 1)
                for b in range(2):
                    gate_rows(l, b, b, P)
                pool.wait_ge(pads_out, 32 * (l + 1))
                for h in range(H):
                    pool.dma_start(sst[h][:, :], gdn_in[l, h]).then_inc(sst_in, 16)
                for b in range(2):
                    masks(l, b, b, P)
                for i, s in enumerate(LEVELS):
                    for b in range(2):
                        level_mask(l, b, b, P, 2 * i + b, s)
                pool.wait_ge(s_ready, 2 * l + 2)
                pool.dma_start(gdnp_out[l], S[:, :]).then_inc(p_out, 16)
                pool.wait_ge(s_done, 2 * l + 2)
                gate_rows(l, 0, 2, TS)
                masks(l, 0, 2, TS)
                level_mask(l, 0, 2, TS, 12, 2)
                for h in range(H):
                    pool.wait_ge(sst_ready, H * l + h + 1)
                    pool.dma_start(gdns_out[l, h], sst[h][:, :]).then_inc(st_out, 16)
            pool.wait_ge(hlo_ready, 8)
            pool.wait_ge(st_out, 64 * DEPTH)
            pool.memset(tok_hi[:, 2 * D:3 * D].bitcast(F32), 0.0)
            pool.memset(tok_lo[:, 2 * D:3 * D].bitcast(F32), 0.0).then_inc(pad_ready, 1)
            pool.memset(facc[:, :], 0.0).then_inc(pad_ready, 1)
            pool.wait_ge(p_out, 16 * DEPTH)

        @block.scalar
        def _(act):
            step = Steps(act, act_step)

            def split_hi(u, it=None, per=0):
                act.wait_ge(raw_in[u % NRAW], later(16 * (u // NRAW + 1), it, per // NRAW * 16))
                if u >= NSPLIT:
                    act.wait_ge(unit_used, later(u - NSPLIT + 1, it, per))
                act.activation(whi[u % NSPLIT][:, :], raw[u % NRAW][:, :], ACT.Copy).then_inc(hi_split, 1)

            def heads(t, rows, n):
                return t[0:rows, 0:H * n].rearrange("p (h n) -> p h n", h=H)

            def bank_heads(bank, rows, n):
                return ps[0:rows, bank, 0:H * n].rearrange("p (h n) -> p h n", h=H)

            def wait_tile(key, it=None, per=0):
                bank, use, (s, v) = tiles[key]
                act.wait_ge(s, later(v, it, per))
                return bank

            def row_copy(j, used, it=None):
                act.wait_ge(unit_used, later(used, it, 6))
                act.activation(modrow[j % 3][0:2 * NC_, :], ps[0:2 * NC_, 4 + j % 3, :], ACT.Copy).then_inc(row_ready, 1)

            def rsqrt(out, in_, scale, eps, done):
                step(act.activation(out, in_, ACT.Ln, bias=cc(eps), scale=scale))
                act.activation(out, out, ACT.Exp, scale=-0.5).then_inc(done, 1)

            def norm(n):
                act.wait_ge(x_ready, n) if n else act.wait_ge(x_loaded, 16)
                if n == 0:
                    act.wait_ge(modT_ready, 12)
                if n % 2:
                    act.wait_ge(p_out, 8 * (n + 1))
                act.activation(sq[:, :], x[:, :], ACT.Square).then_inc(sq_ready, 1)
                act.wait_ge(ss_ready, n + 1)
                rsqrt(rstd[:, :], ps[:, 7, 0:T], 1.0 / D, "eps6", rstd_ready)

            def round_h(n):
                for half in range(2):
                    ks = slice(4 * half, 4 * half + 4)
                    act.wait_ge(hf_ready, 2 * n + half + 1)
                    act.activation(hi3[:, ks], hf3[:, ks], ACT.Copy).then_inc(hhi_ready, 1)

            def silu_tile(l, m):
                act.wait_ge(conv_done, QKV_T * l + m + 1)
                src = ctmp[:, (m % 2) * 316:(m % 2) * 316 + 316]
                act.activation(kt(qkv, QKV_T)[:, m, 0:TP], src[:, 0:TP], ACT.Silu)
                act.activation(seqs(kt(qkv, QKV_T)[:, m]),
                               src[:, QSAMP:QSAMP + NB * QSEG].rearrange("p (b s) -> p b s", s=QSEG)[:, :, 0:TD],
                               ACT.Silu).then_inc(silu_done, 1)

            def project_in(l):
                for i in range(N_IN):
                    split_hi(U_IN[l] + i + LEAD)
                    if i < CT:
                        bank = wait_tile((("in", l), i, 1))
                        if i:
                            ub, uu, _ = tiles[(("in", l), i - 1, 0)]
                            act.wait_ge(bank_free[ub], uu + 1)
                        act.activation(sg[:, 0:T], ps[:, bank, 0:T], ACT.Sigmoid).then_inc(bank_free[bank], 1)
                    elif i < CT + QKV_T // 2:
                        if i == CT:
                            act.wait_ge(pads_in, 32 * (l + 1))
                        for s in range(2):
                            m = 2 * (i - CT) + s
                            bank = wait_tile((("in", l), i, s))
                            act.activation(qp3[:, m, CW - 1:QSAMP], ps[:, bank, 0:TP], ACT.Copy)
                            act.activation(qp3[:, m, QSAMP:QPAD].rearrange("p (b s) -> p b s", s=QSEG)[:, :, CW - 1:QSEG],
                                           seqs(ps[:, bank]), ACT.Copy).then_inc(bank_free[bank], 1)
                    else:
                        for s in range(2):
                            h = 2 * (i - CT - QKV_T // 2) + s
                            bank = wait_tile((("in", l), i, s))
                            act.activation(kt(zs, H)[:, h], ps[:, bank, 0:T], ACT.Silu).then_inc(bank_free[bank], 1)

            def block_start(l, b, blk_i, n):
                act.wait_ge(mm1_done, 3 * l + blk_i + 1)
                act.activation(heads(blk[b]["er"], P, n), bank_heads(b, P, n), ACT.Exp).then_inc(er_ready, 1)

            def decay(l, b, blk_i, n):
                act.wait_ge(diff_ready, 3 * l + blk_i + 1)
                da, dq = heads(blk[b]["da"], n, n), heads(blk[b]["dq"], n, n)
                act.activation(da, da, ACT.Exp, scale=-1.0)
                act.activation(dq, dq, ACT.Exp).then_inc(dexp_ready, 1)

            def copy_at(l, b, blk_i, n):
                act.wait_ge(at_done, 3 * l + blk_i + 1)
                act.activation(heads(blk[b]["AT"], n, n), bank_heads(b, n, n), ACT.Copy).then_inc(at_copied, 1)

            def copy_pm(l, b, n, q):
                act.wait_ge(pm_done, 13 * l + q + 1)
                act.activation(heads(blk[b]["PM"], n, n), bank_heads(2 + b, n, n), ACT.Copy).then_inc(pm_copied, 1)

            def scale_kv(l, b, blk_i, n, kd):
                act.wait_ge(kv_done, 3 * l + blk_i + 1)
                for bank, dst, scale in ((b, blk[b]["da"], bEG), (b, kd, cut(small, 84, 12)), (2 + b, blk[b]["AT"], beta)):
                    for h in range(H):
                        c = blk_i * H + h
                        last = act.activation(heads(dst, n, P)[:, h], bank_heads(bank, n, P)[:, h], ACT.Copy,
                                              scale=scale[0:n, c:c + 1])
                last.then_inc(kv_ready, 1)

            def negate_w(l, b, blk_i, n):
                act.wait_ge(w_done, 3 * l + blk_i + 1)
                act.activation(heads(blk[b]["PM"], P, n), bank_heads(4 + b, P, n), ACT.Copy, scale=-1.0)\
                    .then_inc(nw_ready, 1)

            def copy_vn(l, b, blk_i, n, dst):
                act.wait_ge(vn_done, 3 * l + blk_i + 1)
                act.activation(heads(dst, n, P), bank_heads(6 + b, n, P), ACT.Copy).then_inc(vn_ready, 1)

            def copy_o(l, b, blk_i, n):
                act.wait_ge(o_done, 3 * l + blk_i + 1)
                act.activation(kt(oall, H)[:, :, blk_i * P:blk_i * P + n], bank_heads(b, P, n), ACT.Copy)\
                    .then_inc(o_copied, 1)

            def mixer(l):
                act.wait_ge(ab_done, l + 1)
                act.wait_ge(silu_done, QKV_T * (l + 1))
                act.activation(hf[:, :], qkv[:, 0:2 * H * T], ACT.Square).then_inc(qsq_ready, 1)
                act.wait_ge(ab_copied, l + 1)
                ab3 = ab.rearrange("p (b c) -> p b c", b=3)
                act.activation(beta.rearrange("p (b c) -> p b c", b=3), ab3[:, :, 0:H], ACT.Sigmoid).then_inc(beta_ready, 1)
                act.wait_ge(abs_ready, l + 1)
                step(act.activation(t0, t0, ACT.Exp, scale=-1.0))
                act.activation(t0, t0, ACT.Ln, bias=cc("one")).then_inc(sp_ready, 1)
                for i, (scale, eps) in enumerate(((float(P), "epsq"), (1.0, "eps6"))):
                    act.wait_ge(qss_ready, 2 * l + i + 1)
                    rsqrt(kt(qrs[i], H), ps[:, 4 * i:4 * i + 4, 0:T], scale, eps, qrs_ready)
                act.wait_ge(cent_ready, l + 1)
                act.activation(csq[:, :], yc[:, :], ACT.Square).then_inc(csq_ready, 1)
                act.wait_ge(css_ready, l + 1)
                rsqrt(kt(crs, CT), ps[:, 4:8, 0:T], 1.0 / P, "eps5", crs_ready)
                act.wait_ge(cum_ready, l + 1)
                act.activation(eg, ps[:, 0, 0:24], ACT.Exp).then_inc(eg_ready, 1)
                for b in range(2):
                    block_start(l, b, b, P)
                for b in range(2):
                    decay(l, b, b, P)
                for b in range(2):
                    copy_at(l, b, b, P)
                for i in range(len(LEVELS)):
                    for b in range(2):
                        copy_pm(l, b, P, 2 * i + b)
                for b in range(2):
                    scale_kv(l, b, b, P, blk[b]["L"])
                for b in range(2):
                    negate_w(l, b, b, P)
                for b in range(2):
                    copy_vn(l, b, b, P, blk[b]["MT"])
                    copy_o(l, b, b, P)
                block_start(l, 0, 2, TS)
                decay(l, 0, 2, TS)
                copy_at(l, 0, 2, TS)
                copy_pm(l, 0, TS, 12)
                scale_kv(l, 0, 2, TS, blk[1]["MT"])
                negate_w(l, 0, 2, TS)
                copy_vn(l, 0, 2, TS, blk[1]["er"])
                copy_o(l, 0, 2, TS)
                act.wait_ge(o_copied, 3 * l + 3)
                act.activation(osq[:, :], oall[:, :], ACT.Square).then_inc(osq_ready, 1)
                act.wait_ge(oss_ready, l + 1)
                rsqrt(kt(ors, H), ps[:, 0:8:2, 0:T], 1.0 / P, "eps6", ors_ready)
                act.wait_ge(cn_ready, l + 1)
                for c in range(CT):
                    last = act.activation(kt(yc, CT)[:, c], kt(yc, CT)[:, c], ACT.Silu, bias=pc(f"bln{l}", c, 1),
                                          scale=pc(f"gln{l}", c, 1))
                last.then_inc(cy_ready, 1)
                act.wait_ge(cy_ready, l + 1)
                act.activation(hi3[:, 4:8], kt(yc, CT), ACT.Copy).then_inc(mhi_ready, 1)
                act.wait_ge(o_ready, l + 1)
                act.activation(hi3[:, 0:4], kt(oall, H), ACT.Copy).then_inc(mhi_ready, 1)

            act.wait_ge(c_loaded, 16)
            act.activation(cs[:, :], cs[:, :], ACT.Silu).then_inc(cs_ready, 1)
            act.wait_ge(cs_ready, 1)
            cst3 = cstat[:, :].rearrange("p (k c) -> p k c", k=KD)
            act.activation(cst3[:, :, 0:NC_], cs[:, :].rearrange("p (k c) -> p k c", k=KD), ACT.Copy).then_inc(cstat_ready, 1)
            act.wait_ge(small_in, 32)
            for l in range(DEPTH):
                a, _ = PCOL[f"alog{l}"]
                act.activation(par[:, a:a + 12], par[:, a:a + 12], ACT.Exp).then_inc(expa_ready, 1)
            for u in range(LEAD):
                split_hi(u)

            def ada(c, it=None):
                split_hi(U_ADA[0] + c + LEAD, it, 6)
                if c % 2:
                    row_copy(c // 2, U_ADA[0] + c + 1, it)

            for c in range(6):
                ada(c)
            with act.Fori(0, N_ADA // 6 - 1) as i:
                for c in range(6, 12):
                    ada(c, i)
            norm(0)
            round_h(0)
            project_in(0)
            for v in range(N_ADA):
                split_hi(U_ADA[1] + v + LEAD)
                if v % 2:
                    row_copy(v // 2, U_ADA[1] + v + 1)
                    silu_tile(0, v // 2)
            mixer(0)
            for i in range(N_OUT):
                split_hi(U_OUT[0] + i + LEAD)
            norm(1)
            round_h(1)

            def up(i, it=None):
                split_hi(U_UP + i + LEAD, it, 6)
                bank, use, (s, v) = tiles[("up", i, 0)]
                act.wait_ge(s, later(v, it, 6))
                ub, uu, _ = tiles[("up", i, 1)]
                act.wait_ge(bank_free[ub], later(uu, it, 3))
                act.activation(sg[:, (i % 2) * T:(i % 2) * T + T], ps[:, bank, 0:T], ACT.Silu).then_inc(bank_free[bank], 1)
                act.wait_ge(bank_free[ub], later(uu + 1, it, 3))
                dst = act_hi[:, i * T:(i + 1) * T] if it is None else act_hi[:, bass.ds(it * (6 * T) + i * T, T)]
                act.activation(dst, ctmp[:, (i % 2) * 316:(i % 2) * 316 + T], ACT.Copy).then_inc(ahi_ready, 1)

            act.wait_ge(st_out, 64)
            with act.Fori(0, N_UP // 6) as i:
                for c in range(6):
                    up(c, i)
            for c in range(N_UP // 6 * 6, N_UP):
                up(c)
            for i in range(N_DOWN):
                split_hi(U_DOWN + i + LEAD)
            norm(2)
            round_h(2)
            project_in(1)
            for m in range(QKV_T):
                silu_tile(1, m)
            mixer(1)
            for i in range(N_OUT):
                split_hi(U_OUT[1] + i + LEAD)
            norm(3)
            round_h(3)
            for b in range(3):
                n = TS if b == 2 else P
                if b == 2:
                    act.wait_ge(pad_ready, DEPTH + 1)
                act.wait_ge(tokT_done, b + 1)
                act.activation(tok_hi[0:n, b * D:(b + 1) * D].rearrange("p (a n) -> p a n", a=2),
                               ps[0:n, 2 * b:2 * b + 2, :], ACT.Copy).then_inc(tok_hi_ready, 1)
            act.wait_ge(lsub_ready, 1)
            act.activation(ex, lg, ACT.Exp).then_inc(lexp_ready, 1)
            act.wait_ge(npass_ready, 1)
            n_pass = act.value_load(npass_i[0:1, 0:1], min_val=1, max_val=3)

            def gather(g, q, part):
                if part < 2:
                    act.wait_ge(gx_done, g * 2 + part + 1)
                    act.activation(xe[:, part * 512:(part + 1) * 512], ps[:, 7, :], ACT.Copy).then_inc(gx_copied, 1)
                elif part < 4:
                    act.wait_ge(gt_done, g * 2 + part - 1)
                    act.activation(ht_hi[q][:, (part - 2) * 512:(part - 1) * 512], ps[:, 7, :], ACT.Copy).then_inc(hthi_ready, 1)

            with act.Fori(0, n_pass) as p_:
                for part in range(4):
                    gather(p_ * (NE + 1), 0, part)
                with act.Fori(0, NE // 2) as pair:
                    for q in range(2):
                        it = p_ * NE + pair * 2 + q

                        def round_hidden(c):
                            act.wait_ge(eT_done, it * FC + c + 1)
                            act.activation(at_hi[:, :], ps[:, 4, :], ACT.Copy).then_inc(eahi_ready, 1)

                        for k, (kind, c, half) in enumerate(expert_units()):
                            split_hi(U_MOE + k + LEAD, it, PER_EXPERT)
                            if kind == "g" and half:
                                act.wait_ge(unit_used, later(U_MOE + k + 1, it, PER_EXPERT))
                                if c >= 2:
                                    act.wait_ge(eg_prod, it * FC + c - 1)
                                act.activation(sge[c % 2][:, :], ps[:, c % 2, :], ACT.Silu).then_inc(eg_gate, 1)
                                if c:
                                    round_hidden(c - 1)
                            if (kind, c, half) == ("d", FC - 2, 1):
                                round_hidden(FC - 1)
                            if k - 1 in GATHER_AT:
                                gather(p_ * (NE + 1) + pair * 2 + (q + 1), 1 - q, GATHER_AT.index(k - 1))
                        act.wait_ge(scat_done, it * KD + KD)
                        act.wait_ge(unit_used, later(U_MOE + PER_EXPERT, it, PER_EXPERT))
                        act.activation(ye_hi[:, :].rearrange("p (a n) -> p a n", a=2), ps[:, 5:7, :], ACT.Copy,
                                       scale=pslot[q]).then_inc(yhi_ready, 1)
            norm(4)

        @block.vector
        def _(dve):
            step = Steps(dve, dve_step)

            def split_lo(u, it=None, per=0):
                dve.wait_ge(hi_split, later(u + 1, it, per))
                dve.tensor_tensor(wlo[u % NSPLIT][:, :], raw[u % NRAW][:, :], whi[u % NSPLIT][:, :].bitcast(F32),
                                  ALU.subtract).then_inc(lo_split, 1)

            def heads(t, rows, n):
                return t[0:rows, 0:H * n].rearrange("p (h n) -> p h n", h=H)

            def bank_heads(bank, rows, n):
                return ps[0:rows, bank, 0:H * n].rearrange("p (h n) -> p h n", h=H)

            def wait_tile(key, it=None, per=0):
                bank, use, (s, v) = tiles[key]
                dve.wait_ge(s, later(v, it, per))
                return bank

            def modulation(l):
                dve.wait_ge(modT_ready, 12 * (l + 1))
                bias = pc(f"b_ada{l}").unsqueeze(2).to_broadcast([P, MODS * KD, NC_])
                step(dve.tensor_tensor(mod[l][:, :].rearrange("p (k c) -> p k c", c=NC_),
                                       ps[:, 7, 0:MODS * KD * NC_].rearrange("p (k c) -> p k c", c=NC_), bias, ALU.add))
                for i, (s, g) in enumerate(((1, "g1"), (4, "g2"))):
                    g9 = pc(f"{g}{l}").unsqueeze(2).to_broadcast([P, KD, NC_])
                    last = dve.scalar_tensor_tensor(gain3[2 * l + i], mod3[l][:, s], 1.0, g9, ALU.add, ALU.mult)
                last.then_inc(mod_ready, 1)

            def norm(n):
                l, shift = n // 2, mod3[n // 2][:, 3 * (n % 2)]
                dve.wait_ge(rstd_ready, n + 1)
                dve.wait_ge(mod_ready, l + 1)
                step(dve.tensor_tensor(sq3, x3, rstd[:, :].unsqueeze(1).to_broadcast([P, KD, T]), ALU.mult))
                for half in range(2):
                    for k in range(4 * half, 4 * half + 4):
                        dve.tensor_scalar(hf3[:, k, 0:TP], sq3[:, k, 0:TP], gain3[n][:, k, 0:1], shift[:, k, 0:1],
                                          ALU.mult, ALU.add)
                    ks = slice(4 * half, 4 * half + 4)
                    sample = lambda t: t[:, ks, TP:T].rearrange("p k (b t) -> p k b t", t=TD)
                    step(dve.tensor_tensor(sample(hf3), sample(sq3), per_token(gain3[n][:, ks]), ALU.mult))
                    dve.tensor_tensor(sample(hf3), sample(hf3), per_token(shift[:, ks]), ALU.add).then_inc(hf_ready, 1)
                for half in range(2):
                    ks = slice(4 * half, 4 * half + 4)
                    dve.wait_ge(hhi_ready, 2 * n + half + 1)
                    dve.tensor_tensor(lo3[:, ks], hf3[:, ks], hi3[:, ks].bitcast(F32), ALU.subtract).then_inc(hlo_ready, 1)

            def conf_taps(l, first, end):
                for n in range(first, end):
                    c, j = divmod(n, CK)
                    y = kt(yc, CT)[:, c]
                    window = cp3[:, c, CSAMP:CPAD].rearrange("p (b s) -> p b s", s=CSEG)[:, :, j:j + TD]
                    w = pc(f"wc{l}", n, 1)
                    if j == 0:
                        ub, uu, _ = tiles[(("in", l), c, 0)]
                        dve.wait_ge(bank_free[ub], uu + 1)
                        bias = pc(f"bc{l}", c, 1)
                        dve.tensor_scalar(y[:, 0:TP], cp3[:, c, 0:TP], w, bias, ALU.mult, ALU.add)
                        step(dve.tensor_scalar(seqs(y), window, w, bias, ALU.mult, ALU.add))
                        continue
                    dve.scalar_tensor_tensor(y[:, 0:TP], cp3[:, c, j:j + TP], w, y[:, 0:TP], ALU.mult, ALU.add)
                    last = dve.scalar_tensor_tensor(seqs(y), window, w, seqs(y), ALU.mult, ALU.add)
                    if n == CT * CK - 1:
                        last.then_inc(conf_done, 1)
                    else:
                        step(last)

            def conv_tile(l, m):
                bank, use, _ = tiles[(("in", l), CT + m // 2, m % 2)]
                dve.wait_ge(bank_free[bank], use + 1)
                if m >= 2 or l:
                    dve.wait_ge(silu_done, QKV_T * l + m - 1)
                y = ctmp[:, (m % 2) * 316:(m % 2) * 316 + QOUT]
                step(dve.tensor_scalar(y, qp3[:, m, 0:QOUT], pc(f"wq{l}", m * CW, 1), None, ALU.mult))
                for j in range(1, CW):
                    last = dve.scalar_tensor_tensor(y, qp3[:, m, j:j + QOUT], pc(f"wq{l}", m * CW + j, 1), y,
                                                    ALU.mult, ALU.add)
                    if j < CW - 1:
                        step(last)
                last.then_inc(conv_done, 1)

            def project_in(l):
                for i in range(N_IN):
                    split_lo(U_IN[l] + i + LEAD)
                    if i == 0:
                        dve.wait_ge(pads_in, 32 * (l + 1))
                        dve.wait_ge(pad_ready, l + 1)
                    if i < CT:
                        bank = wait_tile((("in", l), i, 0))
                        gb, gu, _ = tiles[(("in", l), i, 1)]
                        dve.wait_ge(bank_free[gb], gu + 1)
                        dve.tensor_tensor(cp3[:, i, CK - 1:CSAMP], ps[:, bank, 0:TP], sg[:, 0:TP], ALU.mult)
                        dst = cp3[:, i, CSAMP:CPAD].rearrange("p (b s) -> p b s", s=CSEG)[:, :, CK - 1:CSEG]
                        dve.tensor_tensor(dst, seqs(ps[:, bank]), seqs(sg), ALU.mult).then_inc(bank_free[bank], 1)
                    if i:
                        conf_taps(l, 8 * (i - 1), 8 * i)

            def copy_rates(l):
                step(dve.memset(ab, 0.0))
                dve.wait_ge(ab_done, l + 1)
                dve.tensor_copy(ab[:, 0:16], ps[:, 7, 0:16])
                dve.tensor_copy(ab[0:TS, 16:24], ps[0:TS, 7, 16:24]).then_inc(ab_copied, 1)

            def decay_rates(l):
                dve.wait_ge(ab_copied, l + 1)
                a3 = ab.rearrange("p (b c) -> p b c", b=3)[:, :, H:2 * H]
                v3 = lambda t: t.rearrange("p (b c) -> p b c", b=3)
                step(dve.tensor_tensor(v3(t1), a3, v3(pc(f"dt{l}")), ALU.add))
                step(dve.tensor_scalar(t2, t1, -1.0, None, ALU.mult))
                dve.tensor_tensor(t0, t1, t2, ALU.max).then_inc(abs_ready, 1)
                dve.wait_ge(abs_ready, l + 1)
                step(dve.tensor_scalar(t1, t1, 0.0, None, ALU.max))
                dve.wait_ge(sp_ready, l + 1)
                step(dve.tensor_tensor(t1, t1, t0, ALU.add))
                dve.wait_ge(expa_ready, l + 1)
                dve.scalar_tensor_tensor(gg, t1, -1.0, pc(f"alog{l}"), ALU.mult, ALU.mult).then_inc(g_ready, 1)

            def differences(l, b, blk_i, n):
                dve.wait_ge(er_ready, 3 * l + blk_i + 1)
                for dst, clip in (("da", ALU.max), ("dq", ALU.min)):
                    for h in range(H):
                        last = dve.tensor_scalar(heads(blk[b][dst], n, n)[:, h], bank_heads(b, n, n)[:, h],
                                                 gcs[0:n, blk_i * H + h:blk_i * H + h + 1], 0.0, ALU.subtract, clip)
                last.then_inc(diff_ready, 1)

            def products(l, b, blk_i, n):
                dve.wait_ge(dmask_ready, 3 * l + blk_i + 1)
                for h in range(H):
                    da = heads(blk[b]["da"], n, n)[:, h]
                    last = dve.scalar_tensor_tensor(da, bank_heads(2 + b, n, n)[:, h],
                                                    beta[0:n, blk_i * H + h:blk_i * H + h + 1], da, ALU.mult, ALU.mult)
                last.then_inc(A_ready, 1)
                dq = heads(blk[b]["dq"], n, n)
                dve.tensor_tensor(dq, bank_heads(4 + b, n, n), dq, ALU.mult).then_inc(qk_ready, 1)

            def inverse_start(l, b, blk_i, n):
                wide = lambda name: cc(name, n, n).unsqueeze(1).to_broadcast([n, H, n])
                L, LT = heads(blk[b]["L"], n, n), heads(blk[b]["LT"], n, n)
                dve.wait_ge(A_ready, 3 * l + blk_i + 1)
                step(dve.tensor_tensor(L, heads(blk[b]["da"], n, n), wide("m1l"), ALU.mult))
                step(dve.tensor_tensor(L, wide("ident"), L, ALU.subtract))
                dve.wait_ge(at_copied, 3 * l + blk_i + 1)
                step(dve.tensor_tensor(LT, heads(blk[b]["AT"], n, n), wide("m1t"), ALU.mult))
                dve.tensor_tensor(LT, wide("ident"), LT, ALU.subtract).then_inc(linit_ready, 1)

            def inverse_level(l, b, n, q, final):
                dve.wait_ge(q_done, 13 * l + q + 1)
                if q in (0, 1, 12):
                    dve.wait_ge(linit_ready, 3 * l + (2 if q == 12 else q) + 1)
                else:
                    dve.wait_ge(l_ready, 13 * l + q - 1)
                L, LT = heads(blk[b]["L"], n, n), heads(blk[b]["LT"], n, n)
                if not final:
                    dve.tensor_tensor(L, L, bank_heads(4 + b, n, n), ALU.subtract)
                dve.tensor_tensor(LT, LT, bank_heads(6 + b, n, n), ALU.subtract).then_inc(l_ready, 1)

            def decayed_q(l, b, blk_i, n):
                er = heads(blk[b]["er"], P, n)
                if blk_i < 2:
                    step(dve.tensor_copy(glb[:, b * H:(b + 1) * H], er[:, :, n - 1]))
                else:
                    step(dve.tensor_copy(glb.rearrange("p (h b) -> p h b", h=H), er[:, :, TD - 1:n:TD]))
                dve.tensor_tensor(er, kt(qkv, QKV_T)[:, 0:H, blk_i * P:blk_i * P + n], er, ALU.mult).then_inc(qd_ready, 1)

            def mixer(l, rest_of_taps):
                decay_rates(l)
                rest_of_taps()
                for i in range(2):
                    dve.wait_ge(qrs_ready, 2 * l + i + 1)
                    q3 = kt(qkv, QKV_T)[:, H * i:H * i + H]
                    dve.tensor_tensor(q3, q3, kt(qrs[i], H), ALU.mult).then_inc(qn_ready, 1)
                dve.wait_ge(cmean_done, l + 1)
                dve.wait_ge(conf_done, l + 1)
                y = kt(yc, CT)
                dve.scalar_tensor_tensor(y, ps[:, 4:8, 0:T], -1.0 / P, y, ALU.mult, ALU.add).then_inc(cent_ready, 1)
                dve.wait_ge(crs_ready, l + 1)
                dve.tensor_tensor(y, y, kt(crs, CT), ALU.mult).then_inc(cn_ready, 1)
                dve.wait_ge(eg_ready, l + 1)
                dve.wait_ge(beta_ready, l + 1)
                dve.tensor_copy(gcs, ps[:, 0, 0:12])
                dve.tensor_tensor(bEG, beta, eg[:, 0:12], ALU.mult).then_inc(beg_ready, 1)
                dve.wait_ge(beg_ready, l + 1)
                for b in range(2):
                    differences(l, b, b, P)
                for b in range(2):
                    products(l, b, b, P)
                for b in range(2):
                    inverse_start(l, b, b, P)
                for i in range(len(LEVELS)):
                    for b in range(2):
                        inverse_level(l, b, P, 2 * i + b, i == len(LEVELS) - 1)
                for b in range(2):
                    decayed_q(l, b, b, P)
                dve.wait_ge(s_done, 2 * l + 1)
                if l:
                    dve.wait_ge(p_out, 16 * l)
                dve.tensor_copy(heads(S, P, P), bank_heads(2, P, P)).then_inc(s_ready, 1)
                dve.wait_ge(s_done, 2 * l + 2)
                dve.wait_ge(s_ready, 2 * l + 1)
                for h in range(H):
                    s = heads(S, P, P)[:, h]
                    last = dve.scalar_tensor_tensor(s, s, glb[:, H + h:H + h + 1], bank_heads(3, P, P)[:, h],
                                                    ALU.mult, ALU.add)
                last.then_inc(s_ready, 1)
                differences(l, 0, 2, TS)
                products(l, 0, 2, TS)
                inverse_start(l, 0, 2, TS)
                inverse_level(l, 0, TS, 12, True)
                decayed_q(l, 0, 2, TS)
                dve.wait_ge(nw_ready, 3 * l + 3)
                dve.tensor_tensor(nwx[:, :].rearrange("p (h b n) -> p h b n", h=H, b=NB),
                                  heads(blk[0]["PM"], P, TS).unsqueeze(2).to_broadcast([P, H, NB, TS]),
                                  cc("seqf").rearrange("p (b n) -> p b n", b=NB).unsqueeze(1).to_broadcast([P, H, NB, TS]),
                                  ALU.mult).then_inc(nwx_ready, 1)
                spread(l, 0)
                dve.wait_ge(ors_ready, l + 1)
                step(dve.tensor_tensor(oall[:, :], oall[:, :], ors[:, :], ALU.mult))
                dve.scalar_tensor_tensor(oall[:, :], oall[:, :], pc(f"gout{l}"), zs[:, :], ALU.mult, ALU.mult)\
                    .then_inc(o_ready, 1)
                dve.wait_ge(mhi_ready, 2 * l + 1)
                dve.tensor_tensor(lo3[:, 4:8], kt(yc, CT), hi3[:, 4:8].bitcast(F32), ALU.subtract).then_inc(mlo_ready, 1)
                dve.wait_ge(mhi_ready, 2 * l + 2)
                dve.tensor_tensor(lo3[:, 0:4], kt(oall, H), hi3[:, 0:4].bitcast(F32), ALU.subtract).then_inc(mlo_ready, 1)

            def spread(l, h):
                dve.wait_ge(vn_ready, 3 * l + 3)
                if h:
                    dve.wait_ge(sst_done, H * l + h)
                v = heads(blk[1]["er"], TS, P)[:, h].unsqueeze(1).to_broadcast([TS, NB, P])
                dve.tensor_tensor(vx[0:TS, :].rearrange("p (b n) -> p b n", b=NB), v,
                                  cc("seqp", TS).unsqueeze(2).to_broadcast([TS, NB, P]), ALU.mult).then_inc(vx_ready, 1)

            def new_states(l, h):
                dve.wait_ge(sst_done, H * l + h + 1)
                for b in range(NB):
                    s = sst[h][:, b * P:(b + 1) * P]
                    last = dve.scalar_tensor_tensor(s, s, glb[:, h * NB + b:h * NB + b + 1],
                                                    ps[:, 4 + 2 * (h % 2) + b // 4, (b % 4) * P:(b % 4 + 1) * P],
                                                    ALU.mult, ALU.add)
                last.then_inc(sst_ready, 1)

            def residual(key, l, which, d, done=None):
                bank, use, (s, v) = tiles[key]
                dve.wait_ge(s, v)
                add_gated(ps[:, bank], mod3[l][:, which], d, bank_free[bank], done)

            def add_gated(src, gate, d, read, done=None):
                tmp = stmp[d % 2].rearrange("p (b t) -> p b t", t=TD)
                step(dve.tensor_tensor(tmp, seqs(src), gate[:, d, 1:NC_].unsqueeze(2).to_broadcast([P, NB, TD]), ALU.mult))
                dve.tensor_tensor(seqs(x3[:, d]), seqs(x3[:, d]), tmp, ALU.add)
                last = dve.scalar_tensor_tensor(x3[:, d, 0:TP], src[:, 0:TP], gate[:, d, 0:1], x3[:, d, 0:TP],
                                                ALU.mult, ALU.add)
                if read is not None:
                    last.then_inc(read, 1)

            cst3 = cstat[:, :].rearrange("p (k c) -> p k c", k=KD)
            dve.wait_ge(cstat_ready, 1)
            dve.tensor_tensor(cst3[:, :, NC_:2 * NC_], cs[:, :].rearrange("p (k c) -> p k c", k=KD),
                              cst3[:, :, 0:NC_].bitcast(F32), ALU.subtract).then_inc(cstat_ready, 1)
            dve.wait_ge(small_in, 32)
            for u in range(LEAD):
                split_lo(u)
            with dve.Fori(0, N_ADA // 6) as i:
                for c in range(6):
                    split_lo(U_ADA[0] + c + LEAD, i, 6)
            modulation(0)
            norm(0)
            project_in(0)
            for v in range(N_ADA):
                split_lo(U_ADA[1] + v + LEAD)
                if v == 1:
                    copy_rates(0)
                if v % 2:
                    conf_taps(0, 88 + 3 * (v // 2), 88 + 3 * (v // 2) + 3)
                else:
                    conv_tile(0, v // 2)
            modulation(1)
            mixer(0, lambda: None)

            def project_out(l):
                for i in range(N_OUT):
                    split_lo(U_OUT[l] + i + LEAD)
                    for s in range(2):
                        residual((("out", l), i, s), l, 2, 2 * i + s)
                    new_states(l, i)
                    if i + 1 < H:
                        spread(l, i + 1)
                dve.memset(stmp[0], 0.0).then_inc(x_ready, 1)

            project_out(0)
            norm(1)

            def up(i, it=None):
                split_lo(U_UP + i + LEAD, it, 6)
                gb, gu, _ = tiles[("up", i, 0)]
                bank, use, (s, v) = tiles[("up", i, 1)]
                dve.wait_ge(bank_free[gb], later(gu + 1, it, 3))
                dve.wait_ge(s, later(v, it, 6))
                tmp = ctmp[:, (i % 2) * 316:(i % 2) * 316 + T]
                dve.tensor_tensor(tmp, ps[:, bank, 0:T], sg[:, (i % 2) * T:(i % 2) * T + T], ALU.mult)\
                    .then_inc(bank_free[bank], 1)
                dve.wait_ge(ahi_ready, later(i + 1, it, 6))
                cols = slice(i * T, (i + 1) * T) if it is None else bass.ds(it * (6 * T) + i * T, T)
                dve.tensor_tensor(act_lo[:, cols], tmp, act_hi[:, cols].bitcast(F32), ALU.subtract).then_inc(alo_ready, 1)

            dve.wait_ge(st_out, 64)
            with dve.Fori(0, N_UP // 6) as i:
                for c in range(6):
                    up(c, i)
            for c in range(N_UP // 6 * 6, N_UP):
                up(c)
            d = 0
            for i in range(N_DOWN):
                split_lo(U_DOWN + i + LEAD)
                while d < KD and (FT * (d + 1) - 1) // 16 == i:
                    residual(("down", d), 0, 5, d)
                    d += 1
            dve.memset(stmp[0], 0.0).then_inc(x_ready, 1)
            norm(2)
            project_in(1)
            copy_rates(1)
            for m in range(QKV_T):
                conv_tile(1, m)
            mixer(1, lambda: conf_taps(1, 88, CT * CK))
            project_out(1)
            norm(3)

            step(dve.memset(lg, 0.0))
            step(dve.memset(small[:, 512:576], 0.0))
            dve.wait_ge(lg_done, 1)
            step(dve.tensor_tensor(lg[:, 0:2 * NE], ps[:, 7, 0:2 * NE], pc("br", 0, 2 * NE), ALU.add))
            step(dve.tensor_tensor(lg[0:TS, 2 * NE:3 * NE], ps[0:TS, 7, 2 * NE:3 * NE], pc("br", 2 * NE, NE)[0:TS], ALU.add))
            g3 = lambda t: t.rearrange("p (b e) -> p b e", e=NE)
            one = lambda t: t[:, 0:3]
            wide = lambda t: one(t).unsqueeze(2).to_broadcast([P, 3, NE])
            step(dve.tensor_reduce(one(m1), g3(lg), AX.X, ALU.max))
            dve.tensor_tensor(g3(lg), g3(lg), wide(m1), ALU.subtract).then_inc(lsub_ready, 1)
            dve.wait_ge(lexp_ready, 1)
            step(dve.tensor_reduce(one(rs3), g3(ex), AX.X, ALU.add))
            step(dve.reciprocal(one(rs3), one(rs3)))
            step(dve.tensor_tensor(g3(ex), g3(ex), wide(rs3), ALU.mult))
            for top, hot in ((m1, o1), (m2, o2)):
                step(dve.tensor_reduce(one(top), g3(ex), AX.X, ALU.max))
                step(dve.tensor_tensor(g3(scr), g3(ex), wide(top), ALU.is_equal))
                step(dve.tensor_tensor(scr, scr, cc("rank"), ALU.mult))
                step(dve.tensor_reduce(one(cnt), g3(scr), AX.X, ALU.max))
                step(dve.tensor_tensor(g3(hot), g3(scr), wide(cnt), ALU.is_equal))
                if hot is o1:
                    step(dve.scalar_tensor_tensor(ex, o1, -2.0, ex, ALU.mult, ALU.add))
            step(dve.tensor_tensor(one(rs3), one(m1), one(m2), ALU.add))
            step(dve.reciprocal(one(rs3), one(rs3)))
            step(dve.tensor_tensor(sel, o1, o2, ALU.add))
            dve.tensor_scalar(sel[:, 2 * NE:3 * NE], sel[:, 2 * NE:3 * NE], cc("valid"), None, ALU.mult).then_inc(sel_ready, 1)
            step(dve.tensor_tensor(g3(o1), g3(o1), wide(m1), ALU.mult))
            step(dve.tensor_tensor(g3(o2), g3(o2), wide(m2), ALU.mult))
            step(dve.tensor_tensor(o1, o1, o2, ALU.add))
            step(dve.tensor_tensor(g3(wgt[:, 0:3 * NE]), g3(o1), wide(rs3), ALU.mult))
            dve.wait_ge(pos_done, 1)
            dve.wait_ge(sel_ready, 1)
            step(dve.scalar_tensor_tensor(posm[:, 0:3 * NE], ps[:, 6, 0:3 * NE], 1000.0, sel, ALU.add, ALU.mult))
            step(dve.tensor_scalar(posm, posm, -1000.0, None, ALU.add))
            step(dve.tensor_reduce(npf[:, 0:1], ps[:, 6, 3 * NE:4 * NE].unsqueeze(1), AX.X, ALU.max))
            step(dve.tensor_scalar(npf2[:, 0:1], npf[:, 0:1], 128.5, 1.0, ALU.is_gt, ALU.add))
            step(dve.scalar_tensor_tensor(npf[:, 0:1], npf[:, 0:1], 256.5, npf2[:, 0:1], ALU.is_gt, ALU.add))
            dve.tensor_copy(npass_i[:, :], npf[:, 0:1]).then_inc(npass_ready, 1)
            for b in range(3):
                n = TS if b == 2 else P
                dve.wait_ge(tok_hi_ready, b + 1)
                if b == 2:
                    dve.wait_ge(pad_ready, DEPTH + 1)
                dve.tensor_tensor(tok_lo[0:n, b * D:(b + 1) * D].rearrange("p (a n) -> p a n", a=2),
                                  ps[0:n, 2 * b:2 * b + 2, :],
                                  tok_hi[0:n, b * D:(b + 1) * D].bitcast(F32).rearrange("p (a n) -> p a n", a=2),
                                  ALU.subtract).then_inc(tok_lo_ready, 1)
            dve.wait_ge(posT_done, 1)
            dve.tensor_copy(posT[0:NE, :], ps[0:NE, 7, 0:T]).then_inc(posT_ready, 1)
            dve.wait_ge(posT_ready, 1)
            dve.wait_ge(pad_ready, DEPTH + 2)
            dve.wait_ge(npass_ready, 1)
            n_pass = dve.value_load(npass_i[0:1, 0:1], min_val=1, max_val=3)
            f3 = kt(facc)

            def select(g, q, e):
                for b in range(3):
                    dve.tensor_scalar(pe_sel[:, b * P:(b + 1) * P], cc("iota"), posm[:, bass.ds(e + b * NE, 1)],
                                      None, ALU.is_equal)
                dve.tensor_scalar(pos_e[0:NE, :], posT[0:NE, :], cc("eye8", NE)[:, bass.ds(e, 1)], None, ALU.mult)\
                    .then_inc(psel_ready, 1)

            def gather(g, q, part):
                if 2 <= part < 4:
                    cols = slice((part - 2) * 512, (part - 1) * 512)
                    dve.wait_ge(hthi_ready, g * 2 + part - 1)
                    dve.tensor_tensor(ht_lo[q][:, cols], ps[:, 7, :], ht_hi[q][:, cols].bitcast(F32), ALU.subtract)\
                        .then_inc(htlo_ready, 1)
                elif part == 4:
                    dve.wait_ge(gw_done, g + 1)
                    dve.tensor_copy(pslot[q], ps[:, 7, 0:1])
                    dve.tensor_scalar(pt_sel[q][:, :], ps[:, 7, 8:8 + T], cc("ipart"), None, ALU.is_equal)\
                        .then_inc(ptsel_ready, 1)

            def add_output(at_, d, bank):
                dve.wait_ge(scat_done, at_ + d + 1)
                dve.tensor_tensor(f3[:, d], ps[:, bank, 0:T], f3[:, d], ALU.add).then_inc(facc_added, 1)

            dve.memset(ye_hi[:, :].bitcast(F32), 0.0)
            dve.memset(ye_lo[:, :].bitcast(F32), 0.0)
            dve.memset(pt_sel[1][:, :].bitcast(F32), 0.0).then_inc(ylo_ready, 1)
            with dve.Fori(0, n_pass) as p_:
                select(p_ * (NE + 1), 0, 0)
                for part in range(5):
                    gather(p_ * (NE + 1), 0, part)
                with dve.Fori(0, NE // 2) as pair:
                    for q in range(2):
                        it = p_ * NE + pair * 2 + q
                        g = p_ * (NE + 1) + pair * 2 + (q + 1)

                        def rest_hidden(c):
                            dve.wait_ge(eahi_ready, it * FC + c + 1)
                            dve.tensor_tensor(at_lo[:, :], ps[:, 4, :], at_hi[:, :].bitcast(F32), ALU.subtract)\
                                .then_inc(ealo_ready, 1)

                        for k, (kind, c, half) in enumerate(expert_units()):
                            split_lo(U_MOE + k + LEAD, it, PER_EXPERT)
                            if kind == "g" and half and c:
                                rest_hidden(c - 1)
                            if kind == "u" and half:
                                dve.wait_ge(eg_gate, it * FC + c + 1)
                                dve.wait_ge(unit_used, later(U_MOE + k + 1, it, PER_EXPERT))
                                dve.tensor_tensor(ae[c % 2][:, :], ps[:, 2 + c % 2, :], sge[c % 2][:, :], ALU.mult)\
                                    .then_inc(eg_prod, 1)
                            if (kind, c, half) == ("d", FC - 2, 1):
                                rest_hidden(FC - 1)
                            if k - 1 in SCATTER_AT:
                                add_output(it * KD, SCATTER_AT.index(k - 1), 7)
                            if k == GATHER_AT[0] - 1:
                                select(g, 1 - q, pair * 2 + (q + 1))
                            if k - 1 in GATHER_AT:
                                gather(g, 1 - q, GATHER_AT.index(k - 1))
                        dve.wait_ge(facc_added, it * KD + KD)
                        dve.wait_ge(yhi_ready, it + 1)
                        dve.scalar_tensor_tensor(ye_lo[:, :].rearrange("p (a n) -> p a n", a=2), ps[:, 5:7, :], pslot[q],
                                                 ye_hi[:, :].bitcast(F32).rearrange("p (a n) -> p a n", a=2),
                                                 ALU.mult, ALU.subtract).then_inc(ylo_ready, 1)
                dve.tensor_scalar(posm, posm, -128.0, None, ALU.add)
                dve.tensor_scalar(posT[0:NE, :], posT[0:NE, :], -128.0, None, ALU.add).then_inc(pass_step, 1)
                dve.wait_ge(pass_step, p_ + 1)
            end = dve.snap(n_pass * (NE * KD))
            for d in range(KD):
                add_output(end, d, d % 4)
            dve.wait_ge(facc_added, end + KD)
            for d in range(KD):
                add_gated(f3[:, d], mod3[1][:, 5], d, None)
            dve.memset(stmp[0], 0.0).then_inc(x_ready, 1)
            dve.wait_ge(rstd_ready, 5)
            step(dve.tensor_tensor(sq3, x3, rstd[:, :].unsqueeze(1).to_broadcast([P, KD, T]), ALU.mult))
            dve.tensor_tensor(hf3, sq3, pc("gf").unsqueeze(2).to_broadcast([P, KD, T]), ALU.mult).then_inc(y_ready, 1)

        @block.tensor
        def _(pe):
            mm = pe.matmul

            def heads(t, rows, n):
                return t[0:rows, 0:H * n].rearrange("p (h n) -> p h n", h=H)

            def bank_heads(bank, rows, n):
                return ps[0:rows, bank, 0:H * n].rearrange("p (h n) -> p h n", h=H)

            def three(out, w_hi, w_lo, x_hi, x_lo, start, stop):
                mm(out, w_hi, x_hi, start=start, stop=False)
                mm(out, w_hi, x_lo, start=False, stop=False)
                return mm(out, w_lo, x_hi, start=False, stop=stop)

            def ada_unit(u, half, j, it=None):
                pe.wait_ge(lo_split, later(u + 1, it, 6))
                cst3 = cstat[:, :].rearrange("p (k c) -> p k c", k=KD)
                for k in range(4):
                    for i, w in enumerate((whi, wlo)):
                        last = mm(ps[0:2 * NC_, 4 + j % 3, :], cst3[:, 4 * half + k], w[u % NSPLIT][:, k * 512:(k + 1) * 512],
                                  start=(half == 0 and k == 0 and i == 0), stop=(half == 1 and k == 3 and i == 1))
                last.then_inc(unit_used, 1)

            def ada_columns(j, rows_at, it=None):
                pe.wait_ge(row_ready, later(rows_at, it, 3))
                for q in range(4):
                    c = (4 * j + q) * NC_
                    cols = slice(c, c + NC_) if it is None else bass.ds(it * (12 * NC_) + c, NC_)
                    last = mm(ps[:, 7, cols], modrow[j % 3][0:2 * NC_, q * P:(q + 1) * P], cc("comb", 2 * NC_),
                              start=True, stop=True)
                return last

            def sums(src3, n, banks, done):
                for i in range(n):
                    last = mm(ps[:, banks[i], 0:T], cc("ones"), src3[:, i], start=True, stop=True)
                last.then_inc(done, 1)

            def norm(n):
                pe.wait_ge(sq_ready, n + 1)
                if n < 2:
                    pe.wait_ge(mod_ready, n + 1)
                for k in range(KD):
                    last = mm(ps[:, 7, 0:T], cc("ones"), sq3[:, k], start=(k == 0), stop=(k == KD - 1))
                last.then_inc(ss_ready, 1)

            def pairs(phase, first_unit, n, ready=None, it=None):
                for i in range(n):
                    u = first_unit + i
                    pe.wait_ge(lo_split, later(u + 1, it, 6))
                    for s in range(2):
                        bank, use, _ = tiles[(phase, i, s)]
                        if use:
                            pe.wait_ge(bank_free[bank], later(use, it, 3))
                        for k in range(KD):
                            if ready is not None and i == 0 and s == 0 and k % 4 == 0:
                                pe.wait_ge(ready[0], ready[1] + k // 4)
                            w = slice((s * KD + k) * P, (s * KD + k + 1) * P)
                            last = three(ps[:, bank, 0:T], whi[u % NSPLIT][:, w], wlo[u % NSPLIT][:, w], hi3[:, k], lo3[:, k],
                                         k == 0, k == KD - 1)
                        last.then_inc(unit_used if s else tile_done, 1)

            def block_start(l, b, blk_i, n):
                pe.wait_ge(gb_ready, 3 * l + blk_i + 1)
                q3 = kt(qkv, QKV_T)
                cols = slice(blk_i * P, blk_i * P + n)
                for h in range(H):
                    mm(bank_heads(b, P, n)[:, h], heads(blk[b]["MT"], n, P)[:, h], cc("triS" if blk_i == 2 else "tri", n, n),
                       start=True, stop=True)
                for h in range(H):
                    mm(bank_heads(2 + b, n, n)[:, h], q3[:, H + h, cols], q3[:, H + h, cols], start=True, stop=True)
                for h in range(H):
                    last = mm(bank_heads(4 + b, n, n)[:, h], q3[:, H + h, cols], q3[:, h, cols], start=True, stop=True)
                last.then_inc(mm1_done, 1)

            def transpose_a(l, b, blk_i, n):
                pe.wait_ge(A_ready, 3 * l + blk_i + 1)
                for h in range(H):
                    last = pe.transpose(bank_heads(b, n, n)[:, h], heads(blk[b]["da"], n, n)[:, h], cc("ident", n, n))
                last.then_inc(at_done, 1)

            def level_pm(l, b, blk_i, n, q):
                pe.wait_ge(mt_ready, 13 * l + q + 1)
                if q in (0, 1, 12):
                    pe.wait_ge(linit_ready, 3 * l + blk_i + 1)
                else:
                    pe.wait_ge(l_ready, 13 * l + q - 1)
                for h in range(H):
                    last = mm(bank_heads(2 + b, n, n)[:, h], heads(blk[b]["MT"], n, n)[:, h], heads(blk[b]["L"], n, n)[:, h],
                              start=True, stop=True)
                last.then_inc(pm_done, 1)

            def level_q(l, b, blk_i, n, q, final):
                pe.wait_ge(pm_copied, 13 * l + q + 1)
                if q in (0, 1, 12):
                    pe.wait_ge(qk_ready, 3 * l + blk_i + 1)
                LT, PM = heads(blk[b]["LT"], n, n), heads(blk[b]["PM"], n, n)
                if not final:
                    for h in range(H):
                        mm(bank_heads(4 + b, n, n)[:, h], LT[:, h], PM[:, h], start=True, stop=True)
                for h in range(H):
                    last = mm(bank_heads(6 + b, n, n)[:, h], PM[:, h], LT[:, h], start=True, stop=True)
                last.then_inc(q_done, 1)

            def tokens_kv(l, b, blk_i, n):
                for bank, first in ((b, H), (2 + b, 2 * H)):
                    for h in range(H):
                        last = pe.transpose(bank_heads(bank, n, P)[:, h],
                                            kt(qkv, QKV_T)[:, first + h, blk_i * P:blk_i * P + n], cc("ident"))
                last.then_inc(kv_done, 1)

            def w_rows(l, b, blk_i, n, q):
                pe.wait_ge(kv_ready, 3 * l + blk_i + 1)
                pe.wait_ge(l_ready, 13 * l + q + 1)
                for h in range(H):
                    last = mm(bank_heads(4 + b, P, n)[:, h], heads(blk[b]["da"], n, P)[:, h], heads(blk[b]["LT"], n, n)[:, h],
                              start=True, stop=True)
                last.then_inc(w_done, 1)

            def mixer(l):
                pe.wait_ge(qsq_ready, l + 1)
                pe.wait_ge(ab_copied, l + 1)
                pe.wait_ge(mod_ready, DEPTH)
                for b in range(4):
                    pe.wait_ge(bank_free[b], uses_at[l][b])
                sums(kt(hf)[:, 0:4], 4, range(4), qss_ready)
                sums(kt(hf)[:, 4:8], 4, range(4, 8), qss_ready)
                pe.wait_ge(conf_done, l + 1)
                pe.wait_ge(qrs_ready, 2 * l + 2)
                sums(kt(yc, CT), CT, range(4, 8), cmean_done)
                pe.wait_ge(g_ready, l + 1)
                for mask, maskS, c in (("tri", "triS", 0), ("after", "afterS", 12)):
                    mm(ps[:, 0, c:c + 8], cc(mask), gg[:, 0:8], start=True, stop=True)
                    last = mm(ps[:, 0, c + 8:c + 12], cc(maskS), gg[:, 8:12], start=True, stop=True)
                last.then_inc(cum_ready, 1)
                pe.wait_ge(csq_ready, l + 1)
                sums(kt(csq, CT), CT, range(4, 8), css_ready)
                pe.wait_ge(qn_ready, 2 * l + 2)
                pe.wait_ge(beg_ready, l + 1)
                for b in range(2):
                    block_start(l, b, b, P)
                for b in range(2):
                    transpose_a(l, b, b, P)
                for i in range(len(LEVELS)):
                    for b in range(2):
                        level_pm(l, b, b, P, 2 * i + b)
                    for b in range(2):
                        level_q(l, b, b, P, 2 * i + b, i == len(LEVELS) - 1)
                for b in range(2):
                    tokens_kv(l, b, b, P)
                for b in range(2):
                    w_rows(l, b, b, P, 10 + b)
                for b in range(2):
                    pe.wait_ge(nw_ready, 3 * l + b + 1)
                    pe.wait_ge(qd_ready, 3 * l + b + 1)
                    if b:
                        pe.wait_ge(s_ready, 2 * l + 1)
                    S3 = heads(S, P, P)
                    for h in range(H):
                        out = bank_heads(6 + b, P, P)[:, h]
                        last = mm(out, heads(blk[b]["LT"], P, P)[:, h], heads(blk[b]["AT"], P, P)[:, h], start=True, stop=(b == 0))
                        if b:
                            last = mm(out, heads(blk[b]["PM"], P, P)[:, h], S3[:, h], start=False, stop=True)
                    last.then_inc(vn_done, 1)
                    pe.wait_ge(vn_ready, 3 * l + b + 1)
                    for h in range(H):
                        out = bank_heads(b, P, P)[:, h]
                        if b:
                            mm(out, S3[:, h], heads(blk[b]["er"], P, P)[:, h], start=True, stop=False)
                        last = mm(out, heads(blk[b]["MT"], P, P)[:, h], heads(blk[b]["dq"], P, P)[:, h], start=(b == 0), stop=True)
                    last.then_inc(o_done, 1)
                    for h in range(H):
                        last = mm(bank_heads(2 + b, P, P)[:, h], heads(blk[b]["L"], P, P)[:, h], heads(blk[b]["MT"], P, P)[:, h],
                                  start=True, stop=True)
                    last.then_inc(s_done, 1)
                pe.wait_ge(o_copied, 3 * l + 2)
                pe.wait_ge(s_ready, 2 * l + 2)
                n = TS
                block_start(l, 0, 2, n)
                transpose_a(l, 0, 2, n)
                level_pm(l, 0, 2, n, 12)
                level_q(l, 0, 2, n, 12, True)
                tokens_kv(l, 0, 2, n)
                w_rows(l, 0, 2, n, 12)
                pe.wait_ge(nwx_ready, l + 1)
                pe.wait_ge(sst_in, 64 * (l + 1))
                nwx4 = nwx[:, :].rearrange("p (h b n) -> p h b n", h=H, b=NB)
                for h in range(H):
                    out = bank_heads(6, n, P)[:, h]
                    mm(out, heads(blk[0]["LT"], n, n)[:, h], heads(blk[0]["AT"], n, P)[:, h], start=True, stop=False)
                    for b in range(NB):
                        last = mm(out, nwx4[:, h, b], sst[h][:, b * P:(b + 1) * P], start=False, stop=(b == NB - 1))
                last.then_inc(vn_done, 1)
                pe.wait_ge(qd_ready, 3 * l + 3)
                pe.wait_ge(vn_ready, 3 * l + 3)
                for h in range(H):
                    out = bank_heads(0, P, n)[:, h]
                    for b in range(NB):
                        cols = slice(TD * b, TD * (b + 1))
                        mm(out[:, cols], sst[h][:, b * P:(b + 1) * P], heads(blk[0]["er"], P, n)[:, h, cols],
                           start=(b == 0), stop=False, skip_group_check=True)
                    last = mm(out, heads(blk[1]["er"], n, P)[:, h], heads(blk[0]["dq"], n, n)[:, h], start=False, stop=True,
                              skip_group_check=True)
                last.then_inc(o_done, 1)
                pe.wait_ge(osq_ready, l + 1)
                sums(kt(osq, H), H, range(0, 8, 2), oss_ready)
                pe.wait_ge(ors_ready, l + 1)

            def project_out(l):
                pe.wait_ge(mlo_ready, 2 * l + 2)
                for i in range(N_OUT):
                    u = U_OUT[l] + i
                    pe.wait_ge(lo_split, u + 1)
                    for s in range(2):
                        bank, use, _ = tiles[(("out", l), i, s)]
                        pe.wait_ge(bank_free[bank], use)
                        for k in range(KD):
                            w = slice((s * KD + k) * P, (s * KD + k + 1) * P)
                            last = three(ps[:, bank, 0:T], whi[u % NSPLIT][:, w], wlo[u % NSPLIT][:, w], hi3[:, k], lo3[:, k],
                                         k == 0, k == KD - 1)
                        last.then_inc(unit_used if s else tile_done, 1)
                    pe.wait_ge(vx_ready, H * l + i + 1)
                    if i >= 2:
                        pe.wait_ge(sst_ready, H * l + i - 1)
                    for half in range(2):
                        last = mm(ps[:, 4 + 2 * (i % 2) + half, :], heads(blk[1]["MT"], TS, P)[:, i],
                                  vx[0:TS, half * 512:(half + 1) * 512], start=True, stop=True)
                    last.then_inc(sst_done, 1)

            pe.wait_ge(cstat_ready, 2)
            pe.wait_ge(small_in, 32)
            with pe.Fori(0, N_ADA // 6) as i:
                for c in range(6):
                    ada_unit(U_ADA[0] + c, c % 2, c // 2, i)
                    if c % 2:
                        last = ada_columns(c // 2, c // 2 + 1, i)
                        last.then_inc(modT_ready, 1)
            norm(0)
            pairs(("in", 0), U_IN[0], N_IN, (hlo_ready, 1))

            def token_rates(l):
                a, _ = PCOL[f"wab{l}"]
                for b in range(3):
                    n = TS if b == 2 else P
                    for k in range(KD):
                        last = mm(ps[0:n, 7, 8 * b:8 * b + 8], hf3[:, k, b * P:b * P + n], par[:, a + 8 * k:a + 8 * k + 8],
                                  start=(k == 0), stop=(k == KD - 1))
                last.then_inc(ab_done, 1)

            pe.wait_ge(rstd_ready, 1)
            token_rates(0)
            for v in range(N_ADA):
                ada_unit(U_ADA[1] + v, v % 2, v // 2)
                if v % 2:
                    if v == 1:
                        pe.wait_ge(ab_copied, 1)
                    last = ada_columns(v // 2, 12 + v // 2 + 1)
                    last.then_inc(modT_ready, 1)
            mixer(0)
            project_out(0)
            norm(1)
            with pe.Fori(0, N_UP // 6) as i:
                pe.wait_ge(hlo_ready, 4)
                pairs("up", U_UP, 6, None, i)
            for c in range(N_UP // 6 * 6, N_UP):
                u = U_UP + c
                pe.wait_ge(lo_split, u + 1)
                for s in range(2):
                    bank, use, _ = tiles[("up", c, s)]
                    pe.wait_ge(bank_free[bank], use)
                    for k in range(KD):
                        w = slice((s * KD + k) * P, (s * KD + k + 1) * P)
                        last = three(ps[:, bank, 0:T], whi[u % NSPLIT][:, w], wlo[u % NSPLIT][:, w], hi3[:, k], lo3[:, k],
                                     k == 0, k == KD - 1)
                    last.then_inc(unit_used if s else tile_done, 1)
            pe.wait_ge(alo_ready, N_UP)
            for n in range(FT * KD):
                d, f = divmod(n, FT)
                u = U_DOWN + n // 16
                bank, use, _ = tiles[("down", d)]
                if n % 16 == 0:
                    pe.wait_ge(lo_split, u + 1)
                if f == 0:
                    pe.wait_ge(bank_free[bank], use)
                w = slice((n % 16) * P, (n % 16 + 1) * P)
                cols = slice(f * T, (f + 1) * T)
                last = three(ps[:, bank, 0:T], whi[u % NSPLIT][:, w], wlo[u % NSPLIT][:, w], act_hi[:, cols], act_lo[:, cols],
                             f == 0, f == FT - 1)
                if n % 16 == 15:
                    last.then_inc(unit_used, 1)
                elif f == FT - 1:
                    last.then_inc(tile_done, 1)
            norm(2)
            pairs(("in", 1), U_IN[1], N_IN, (hlo_ready, 5))
            token_rates(1)
            mixer(1)
            project_out(1)
            norm(3)
            pe.wait_ge(hf_ready, 8)
            pe.wait_ge(rstd_ready, 4)
            a, _ = PCOL["wr"]
            for b in range(3):
                n = TS if b == 2 else P
                for k in range(KD):
                    last = mm(ps[0:n, 7, NE * b:NE * b + NE], hf3[:, k, b * P:b * P + n], par[:, a + NE * k:a + NE * k + NE],
                              start=(k == 0), stop=(k == KD - 1))
            last.then_inc(lg_done, 1)
            for b in range(3):
                n = TS if b == 2 else P
                for k in range(KD):
                    last = pe.transpose(ps[0:n, 2 * b + k // 4, (k % 4) * P:(k % 4 + 1) * P], hf3[:, k, b * P:b * P + n],
                                        cc("ident"))
                last.then_inc(tokT_done, 1)
            pe.wait_ge(sel_ready, 1)
            s8 = lambda b: sel[:, NE * b:NE * b + NE]
            for b in range(3):
                for a in range(b):
                    mm(ps[:, 6, NE * b:NE * b + NE], cc("ones"), s8(a), start=(a == 0), stop=False)
                mm(ps[:, 6, NE * b:NE * b + NE], cc("before"), s8(b), start=(b == 0), stop=True)
            for b in range(3):
                last = mm(ps[:, 6, 3 * NE:4 * NE], cc("ones"), s8(b), start=(b == 0), stop=(b == 2))
            last.then_inc(pos_done, 1)
            pe.wait_ge(npass_ready, 1)
            for b in range(3):
                n = TS if b == 2 else P
                last = mm(ps[0:NE, 7, b * P:b * P + n], posm[0:n, NE * b:NE * b + NE], cc("ident", n, n), start=True, stop=True)
            last.then_inc(posT_done, 1)
            pe.wait_ge(tok_lo_ready, 3)
            n_pass = pe.value_load(npass_i[0:1, 0:1], min_val=1, max_val=3)

            def gather(g, q, part):
                if part == 0:
                    pe.wait_ge(psel_ready, g + 1)
                elif part <= 2:
                    pe.wait_ge(gx_copied, g * 2 + part)
                else:
                    pe.wait_ge(htlo_ready, g * 2 + part - 2)
                if part < 2:
                    for i, tok in enumerate((tok_hi, tok_lo)):
                        for b in range(3):
                            last = mm(ps[:, 7, :], pe_sel[:, b * P:(b + 1) * P],
                                      tok[:, b * D + part * 512:b * D + (part + 1) * 512],
                                      start=(i == 0 and b == 0), stop=(i == 1 and b == 2))
                    last.then_inc(gx_done, 1)
                elif part < 4:
                    for d in range(4):
                        c = (4 * (part - 2) + d) * P
                        last = pe.transpose(ps[:, 7, d * P:(d + 1) * P], xe[:, c:c + P], cc("ident"))
                    last.then_inc(gt_done, 1)
                else:
                    for b in range(3):
                        mm(ps[:, 7, 0:1], pe_sel[:, b * P:(b + 1) * P].bitcast(F32), wgt[:, bass.ds(q + b * NE, 1)],
                           start=(b == 0), stop=(b == 2))
                    mm(ps[:, 7, 8:8 + T], cc("ones", NE), pos_e[0:NE, :], start=True, stop=True).then_inc(gw_done, 1)

            def scatter(d, q, bank):
                w = slice(d * P, (d + 1) * P)
                mm(ps[:, bank, 0:T], ye_hi[:, w], pt_sel[q][:, :], start=True, stop=False)
                mm(ps[:, bank, 0:T], ye_lo[:, w], pt_sel[q][:, :], start=False, stop=True).then_inc(scat_done, 1)

            with pe.Fori(0, n_pass) as p_:
                for part in range(5):
                    gather(p_ * (NE + 1), 0, part)
                with pe.Fori(0, NE // 2) as pair:
                    for q in range(2):
                        it = p_ * NE + pair * 2 + q
                        g = p_ * (NE + 1) + pair * 2 + (q + 1)
                        pe.wait_ge(htlo_ready, g * 2)

                        def hidden_rows(c):
                            pe.wait_ge(eg_prod, it * FC + c + 1)
                            for i in range(4):
                                last = pe.transpose(ps[:, 4, i * P:(i + 1) * P], ae[c % 2][:, i * P:(i + 1) * P], cc("ident"))
                            last.then_inc(eT_done, 1)

                        for k, (kind, c, half) in enumerate(expert_units()):
                            if (kind, half) == ("u", 0) and c:
                                hidden_rows(c - 1)
                            if (kind, c, half) == ("d", FC - 1, 0):
                                hidden_rows(FC - 1)
                            u = U_MOE + k
                            pe.wait_ge(lo_split, later(u + 1, it, PER_EXPERT))
                            if kind == "d":
                                if half == 0:
                                    pe.wait_ge(ealo_ready, it * FC + c + 1)
                                bank, a_hi, a_lo, first, end = 5 + half, at_hi, at_lo, c == 0, c == FC - 1
                                off = 0
                            else:
                                if c >= 2 and half == 0:
                                    pe.wait_ge(eg_gate if kind == "g" else eg_prod, it * FC + c - 1)
                                bank, first, end = (0 if kind == "g" else 2) + c % 2, half == 0, half == 1
                                a_hi, a_lo, off = ht_hi[q], ht_lo[q], 4 * half
                            for i in range(4):
                                a = slice((off + i) * P, (off + i + 1) * P)
                                w = slice(i * 512, (i + 1) * 512)
                                mm(ps[:, bank, :], a_hi[:, a], whi[u % NSPLIT][:, w], start=(first and i == 0), stop=False)
                                mm(ps[:, bank, :], a_hi[:, a], wlo[u % NSPLIT][:, w], start=False, stop=False)
                                last = mm(ps[:, bank, :], a_lo[:, a], whi[u % NSPLIT][:, w], start=False, stop=(end and i == 3))
                            last.then_inc(unit_used, 1)
                            if k in SCATTER_AT:
                                d = SCATTER_AT.index(k)
                                if d:
                                    pe.wait_ge(facc_added, it * KD + d)
                                else:
                                    pe.wait_ge(ylo_ready, it + 1)
                                    pe.wait_ge(ptsel_ready, g)
                                scatter(d, 1 - q, 7)
                            if k in GATHER_AT:
                                if k == GATHER_AT[0]:
                                    pe.wait_ge(facc_added, it * KD + KD)
                                part = GATHER_AT.index(k)
                                gather(g, pair * 2 + (q + 1) if part == 4 else None, part)
            end = pe.snap(n_pass * NE + 1)
            pe.wait_ge(ylo_ready, end)
            end = pe.snap(n_pass * (NE * KD))
            for d in range(KD):
                if d >= 4:
                    pe.wait_ge(facc_added, end + (d - 3))
                scatter(d, 1, d % 4)
            norm(4)


def pack_units(w_ada, w_in, w_out, w_gate, w_up, w_down, e_gate, e_up, e_down):
    out = np.empty((N_UNITS + NRAW, P, UNIT), np.float32)

    def column_units(w, first):
        m = w.shape[1] // 512
        out[first:first + 2 * m] = w.reshape(2, 4, P, m, 512).transpose(3, 0, 2, 1, 4).reshape(2 * m, P, UNIT)

    def tile_units(w, cols, first):
        t = np.stack([w[:, c:c + P] for c in cols])
        t = t.reshape(len(cols) // 2, 2, KD, P, P).transpose(0, 3, 1, 2, 4)
        out[first:first + len(cols) // 2] = t.reshape(len(cols) // 2, P, UNIT)

    for l in range(DEPTH):
        column_units(w_ada[l], U_ADA[l])
        tile_units(w_in[l], IN_COLS, U_IN[l])
        tile_units(w_out[l], [P * d for d in range(KD)], U_OUT[l])
    pair = np.stack([w_gate[0].reshape(D, FT, P), w_up[0].reshape(D, FT, P)], 2).reshape(D, 2 * FT * P)
    tile_units(pair, [P * i for i in range(2 * FT)], U_UP)
    t = w_down[0].reshape(FT, P, KD, P).transpose(2, 0, 1, 3).reshape(N_DOWN, 16, P, P)
    out[U_DOWN:U_DOWN + N_DOWN] = t.transpose(0, 2, 1, 3).reshape(N_DOWN, P, UNIT)
    for k, (kind, c, half) in enumerate(expert_units()):
        if kind == "d":
            w = e_down[0][:, c * 512:(c + 1) * 512, half * 512:(half + 1) * 512]
        else:
            w = (e_gate if kind == "g" else e_up)[0][:, half * 512:(half + 1) * 512, c * 512:(c + 1) * 512]
        w = w.reshape(NE, 4, P, 512).transpose(0, 2, 1, 3).reshape(NE, P, UNIT)
        out[U_MOE + k:U_MOE + NE * PER_EXPERT:PER_EXPERT] = w
    out[N_UNITS:] = out[U_MOE:U_MOE + NRAW]
    return out


def channel_major(a, tiles_n):
    return a.reshape(a.shape[0], tiles_n, P).transpose(2, 1, 0)


def kernel(**inputs):
    import concourse.bacc as bacc
    from concourse.bass_utils import run_bass_kernel_spmd

    g = {k: np.asarray(v) for k, v in inputs.items()}
    arrays = {}
    arrays["units"] = pack_units(g["w_ada"], g["w_in"], g["w_out"], g["w_ff_gate"], g["w_ff_up"], g["w_ff_down"],
                                 g["w_exp_gate"], g["w_exp_up"], g["w_exp_down"])
    tokens = np.concatenate([g["x_prompt"].reshape(TP, D), g["x_sample"].reshape(TS, D)])
    arrays["x_in"] = channel_major(tokens, KD).reshape(P, KD * T)
    arrays["c_in"] = channel_major(np.concatenate([g["c_prompt"], g["c_sample"]]), KD).reshape(P, KD * NC_)
    par = np.empty((P, NPAR), np.float32)

    def put(name, a):
        lo, hi = PCOL[name]
        par[:, lo:hi] = a.reshape(P, hi - lo)

    for l in range(DEPTH):
        put(f"b_ada{l}", channel_major(g["b_ada"][l][None], MODS * KD))
        put(f"g1{l}", channel_major(g["g_norm1"][l][None], KD))
        put(f"g2{l}", channel_major(g["g_norm2"][l][None], KD))
        put(f"wq{l}", channel_major(g["w_gdn_conv"][l], QKV_T))
        put(f"wc{l}", channel_major(g["w_conf_dw"][l], CT))
        put(f"bc{l}", channel_major(g["b_conf_dw"][l][None], CT))
        put(f"gln{l}", channel_major(g["g_conf_ln"][l][None], CT))
        put(f"bln{l}", channel_major(g["b_conf_ln"][l][None], CT))
        put(f"gout{l}", g["g_gdn_out"][l][:, None])
        put(f"wab{l}", np.ascontiguousarray(g["w_in"][l][:, COL_B:COL_B + 8].reshape(KD, P, 8).transpose(1, 0, 2)))
        put(f"alog{l}", np.broadcast_to(np.tile(g["a_log"][l], 3), (P, 12)))
        put(f"dt{l}", np.broadcast_to(np.tile(g["dt_bias"][l], 3), (P, 12)))
    put("wr", np.ascontiguousarray(g["w_router"][0].reshape(KD, P, NE).transpose(1, 0, 2)))
    put("br", np.broadcast_to(np.tile(g["b_router"][0], 3), (P, 3 * NE)))
    put("gf", channel_major(g["g_final"][None], KD))
    arrays["par_in"] = par
    arrays["const_in"] = constants()
    arrays["gdn_in"] = g["state_gdn"].transpose(0, 2, 3, 1, 4).reshape(DEPTH, H, P, NB * P)

    def pads(state, tiles_n, seg):
        rows = state.shape[2]
        a = np.zeros((DEPTH, P, tiles_n, NB, seg), np.float32)
        a[..., :rows] = state.reshape(DEPTH, NB, rows, tiles_n, P).transpose(0, 4, 3, 1, 2)
        return a.reshape(DEPTH, P, tiles_n * NB * seg)

    arrays["qst_in"] = pads(g["state_gdn_conv"], QKV_T, QSEG)
    arrays["cst_in"] = pads(g["state_conf_conv"], CT, CSEG)
    arrays = {k: np.ascontiguousarray(v, np.float32) for k, v in arrays.items()}

    nc = bacc.Bacc("TRN2", target_bir_lowering=False, num_devices=1, dynamic_dma_scratch_size=4096)
    args = [nc.dram_tensor(k, v.shape, F32, kind="ExternalInput").ap() for k, v in arrays.items()]
    outs = {"y_out": (P, KD * T), "gdnp_out": (DEPTH, P, H * P), "gdns_out": (DEPTH, H, P, NB * P),
            "qst_out": (DEPTH, P, QKV_T * QPAD), "cst_out": (DEPTH, P, CT * CPAD)}
    args += [nc.dram_tensor(k, s, F32, kind="ExternalOutput").ap() for k, s in outs.items()]
    program(nc, *args)
    r = run_bass_kernel_spmd(nc, [arrays], core_ids=[0]).results[0]

    y = r["y_out"].reshape(P, KD, T).transpose(2, 1, 0).reshape(T, D)
    q = r["qst_out"].reshape(DEPTH, P, QKV_T, QPAD)
    c = r["cst_out"].reshape(DEPTH, P, CT, CPAD)

    def rows(a, first, n):
        a = a[..., first:first + n]
        axes = (0, *range(3, a.ndim), 2, 1)
        a = a.transpose(axes)
        return np.ascontiguousarray(a.reshape(*a.shape[:-2], -1))

    return (
        np.ascontiguousarray(y[:TP].reshape(1, TP, D)),
        np.ascontiguousarray(y[TP:].reshape(NB, TD, D)),
        np.ascontiguousarray(r["gdnp_out"].reshape(DEPTH, P, H, P).transpose(0, 2, 1, 3)[:, None]),
        rows(q, QSAMP - (CW - 1), CW - 1)[:, None],
        rows(c, CSAMP - (CK - 1), CK - 1)[:, None],
        np.ascontiguousarray(r["gdns_out"].reshape(DEPTH, H, P, NB, P).transpose(0, 3, 1, 2, 4)),
        rows(q[..., QSAMP:].reshape(DEPTH, P, QKV_T, NB, QSEG), QSEG - (CW - 1), CW - 1),
        rows(c[..., CSAMP:].reshape(DEPTH, P, CT, NB, CSEG), CSEG - (CK - 1), CK - 1),
    )
```

```python
from contextlib import ExitStack

import numpy as np

import concourse.bass as bass
from concourse import mybir

F32 = mybir.dt.float32
F32R = mybir.dt.float32r
I32 = mybir.dt.int32
ACT = mybir.ActivationFunctionType
ALU = mybir.AluOpType
AX = mybir.AxisListType

P = 128
D = 1024
KD = D // P
DEPTH = 2
TP, NB, TD = 256, 8, 4
TS = NB * TD
T = TP + TS
NC_ = 1 + NB
H = 4
QKV_T = 3 * H
CW = 4
CK = 31
CT = 4
MODS = 6
FT = 2816 // P
NE = 8
FE = 3584
FC = FE // 512
IN_W = 3080
QPAD = TP + CW - 1 + NB * (TD + CW - 1)
CPAD = TP + CK - 1 + NB * (TD + CK - 1)
QSAMP, QSEG = TP + CW - 1, TD + CW - 1
CSAMP, CSEG = TP + CK - 1, TD + CK - 1
QOUT = QPAD - (CW - 1)

UNIT = 2048
NRAW, NSPLIT, LEAD = 6, 3, 2
N_ADA, N_IN, N_OUT, N_UP, N_DOWN = 24, 12, 4, FT, FT * KD // 16
PER_EXPERT = FC * 6
U_IN, U_OUT = [0, 0], [0, 0]
U_IN[0] = N_ADA
U_OUT[0] = U_IN[0] + N_IN + N_ADA
U_UP = U_OUT[0] + N_OUT
U_DOWN = U_UP + N_UP
U_IN[1] = U_DOWN + N_DOWN
U_OUT[1] = U_IN[1] + N_IN
U_MOE = U_OUT[1] + N_OUT
N_UNITS = U_MOE + NE * PER_EXPERT


def in_unit(l, i):
    return U_IN[l] + (3 * i if l == 0 else i)


def ada_unit_of(l, v):
    return v if l == 0 else U_IN[0] + 3 * (v // 2) + 1 + v % 2


COL_Z, COL_B, COL_U, COL_G = 1536, 2048, 2056, 2568
I_QKV, I_Z = 2, 2 + QKV_T // 2
CONF_UNITS = (0, 1, 10, 11)
_conf = [[COL_U + c * P, COL_G + c * P] for c in range(CT)]
IN_COLS = _conf[0] + _conf[1] + [m * P for m in range(QKV_T)] + [COL_Z + h * P for h in range(H)] + _conf[2] + _conf[3]
CONV_POOL = 2 * H
COLUMNS_IN = 316


def taps_in(l, i):
    done = sum(taps_in(l, j) for j in range(i)) if i else 0
    want = ((8, 3) if l == 0 else (10, 5))[I_QKV + H + 1 <= i < I_QKV + H + 1 + H] if i else 0
    return min(want, 2 * CK - done)


FILL = (14, 7, 14, 4, 4, 3)

SCATTER_AT = range(1, 17, 2)
GATHER_AT = (18, 21, 24, 27, 30)


def expert_units():
    order = []
    for c in range(FC):
        order += [("g", c, 0), ("g", c, 1), ("u", c, 0), ("u", c, 1)]
        if c >= 1:
            order += [("d", c - 1, 0), ("d", c - 1, 1)]
    return order + [("d", FC - 1, 0), ("d", FC - 1, 1)]


def columns(sizes):
    at, out = 0, {}
    for name, n in sizes:
        out[name] = (at, at + n)
        at += n
    return out, at


_sizes = []
for _l in range(DEPTH):
    _sizes += [(f"b_ada{_l}", MODS * KD), (f"g1{_l}", KD), (f"g2{_l}", KD), (f"wq{_l}", QKV_T * CW),
               (f"wc{_l}", CT * CK), (f"bc{_l}", CT), (f"gln{_l}", CT), (f"bln{_l}", CT), (f"gout{_l}", 1),
               (f"wab{_l}", KD * 8), (f"alog{_l}", 12), (f"dt{_l}", 12)]
_sizes += [("wr", KD * NE), ("br", 3 * NE), ("gf", KD)]
PCOL, NPAR = columns(_sizes)

LEVELS = [2, 4, 8, 16, 32, 64]
CCOL, NCONST = columns(
    [("ones", P), ("ident", P), ("tri", P), ("after", P), ("m1l", P), ("m1t", P)]
    + [(f"mt{s}", P) for s in LEVELS]
    + [("before", P), ("iota", P), ("triS", P), ("afterS", P), ("seqp", NB),
       ("comb", NC_), ("eps6", 1), ("eps5", 1), ("epsq", 1), ("one", 1), ("ipart", 1), ("valid", 1),
       ("rank", 3 * NE), ("eye8", NE + 1)])


def constants():
    c = np.zeros((P, NCONST), np.float32)

    def put(name, a):
        lo, _ = CCOL[name]
        c[:a.shape[0], lo:lo + a.shape[1]] = a

    i, j = np.arange(P)[:, None], np.arange(P)[None, :]
    put("ones", np.ones((P, P)))
    put("ident", i == j)
    put("tri", i <= j)
    put("after", i > j)
    low = lambda s: (i // (2 * s) == j // (2 * s)) & (i % (2 * s) >= s) & (j % (2 * s) < s)
    put("m1l", low(1))
    put("m1t", low(1).T)
    for s in LEVELS:
        put(f"mt{s}", low(s).T)
    put("before", i < j)
    put("iota", np.broadcast_to(j, (P, P)))
    same = (i // TD == j // TD) & (i < TS) & (j < TS)
    put("triS", same & (i <= j))
    put("afterS", same & (i > j))
    put("seqp", np.arange(TS)[:, None] // TD == np.arange(NB)[None, :])
    put("comb", np.concatenate([np.eye(NC_), np.eye(NC_)]))
    put("eps6", np.full((P, 1), 1e-6))
    put("eps5", np.full((P, 1), 1e-5))
    put("epsq", np.full((P, 1), P * 1e-6))
    put("one", np.ones((P, 1)))
    put("ipart", i)
    put("valid", i < TS)
    put("rank", np.broadcast_to(NE - np.tile(np.arange(NE), 3)[None, :], (P, 3 * NE)))
    put("eye8", np.eye(NE))
    return c


class Steps:

    def __init__(self, eng, sem, at=0, extra=None):
        self.eng, self.sem, self.n, self.extra = eng, sem, at, extra

    def __call__(self, instruction):
        self.n += 1
        instruction.then_inc(self.sem, 1)
        self.eng.wait_ge(self.sem, self.n if self.extra is None else self.extra + self.n)


def later(value, it=None, per=0):
    return value if it is None else it * per + value


def program(nc, units, x_in, c_in, par_in, const_in, gdn_in, qst_in, cst_in,
            y_out, gdnp_out, gdns_out, qst_out, cst_out):
    ctx = ExitStack()
    with ctx:
        base = (nc.sbuf_base + 63) // 64 * 64
        room = nc.sbuf_usable_end - base - 64
        ctx.enter_context(nc.sbuf_tensor("arena", [P, room // 4], F32))
        cursor = [base]

        def at(name, offset, cols, dt=F32):
            return nc.alloc_sbuf_tensor_at(name, [P, cols], dt, offset=offset)

        def keep(name, cols, dt=F32):
            offset = cursor[0]
            cursor[0] = (offset + cols * 4 + 31) // 32 * 32
            assert cursor[0] <= base + room, (name, cursor[0] - base - room)
            return at(name, offset, cols, dt)

        raw = [keep(f"raw{i}", UNIT) for i in range(NRAW)]
        whi = [keep(f"whi{i}", UNIT, F32R) for i in range(NSPLIT)]
        wlo = [keep(f"wlo{i}", UNIT, F32R) for i in range(NSPLIT)]
        x = keep("x", KD * T)
        par = keep("par", NPAR)
        con = keep("con", NCONST)
        mod = [keep(f"mod{l}", MODS * KD * NC_) for l in range(DEPTH)]
        gain = [keep(f"gain{i}", KD * NC_) for i in range(2 * DEPTH)]
        rstd = keep("rstd", T)
        cstat = keep("cstat", KD * 2 * NC_, F32R)
        sg = keep("sg", 2 * T)
        ctmp = keep("ctmp", 2 * 316)
        small = keep("small", 576)
        posT = keep("posT", T)
        npass_i = keep("npass_i", 1, I32)
        r0 = cursor[0]
        h_hi = at("h_hi", r0, KD * T, F32R)
        h_lo = at("h_lo", r0 + 9216, KD * T, F32R)
        hf = at("hf", r0 + 18432, KD * T)
        sq = at("sq", r0 + 27648, KD * T)
        cs = at("cs", r0, KD * NC_)
        modrow = [[at(f"modrow{l}_{i}", r0 + o + 2048 * i, 512) for i in range(3)] for l, o in enumerate((18432, 27648))]
        sqx = [at(f"sqx{n}", r0 + o, KD * T) for n, o in enumerate((9216, 18432, 0, 18432, 18432))]
        qkv = at("qkv", r0 + 36864, QKV_T * T)
        zs = at("zs", r0 + 50688, H * T)
        yc = at("yc", r0 + 55296, CT * T)
        qpad = at("qpad", r0 + 59904, QKV_T * QPAD)
        cpad = at("cpad", r0 + 75040, CT * CPAD)
        oall = at("oall", r0 + 84480, H * T)
        taps_s = at("taps_s", r0 + 84480, TD * NB * CK)
        qrs = [at(f"qrs{i}", r0 + 4608 * i, H * T) for i in range(2)]
        csq = at("csq", r0 + 59904, CT * T)
        crs = at("crs", r0 + 64512, CT * T)
        names = ["da", "dq", "AT", "L", "LT", "PM", "MT", "er"]
        pconv = [at(f"pconv{i}", r0 + 18432 + 1280 * i, 316) for i in range(3)]
        blk = [{n: at(f"{n}{b}", r0 + 2048 * (8 * b + i), H * P) for i, n in enumerate(names)} for b in range(2)]
        S = at("S", r0 + 32768, H * P)
        sst = [at(f"sst{h}", r0 + 59904 + 4096 * h, NB * P) for h in range(H)]
        wq = at("wq", r0 + 76288, H * NB * 2 * TD)
        swq = at("swq", r0 + 77312, H * NB * 2 * TD)
        vx = at("vx", r0 + 80384, NB * P)
        osq = at("osq", r0 + 18432, H * T)
        ors = at("ors", r0 + 23040, H * T)
        act_hi = at("act_hi", r0 + 18432, FT * T, F32R)
        act_lo = at("act_lo", r0 + 43776, FT * T, F32R)
        tok_hi = at("tok_hi", r0 + 36864, 3 * D, F32R)
        tok_lo = at("tok_lo", r0 + 49152, 3 * D, F32R)
        facc = at("facc", r0 + 61440, KD * T)
        ht_hi = [at(f"ht_hi{i}", r0 + 70656 * i, D, F32R) for i in range(2)]
        ht_lo = [at(f"ht_lo{i}", r0 + 70656 * i + 4096, D, F32R) for i in range(2)]
        xe = at("xe", r0 + 78848, D)
        sge = [at(f"sge{i}", r0 + 8192 + 2048 * i, 512) for i in range(2)]
        ae = [at(f"ae{i}", r0 + 12288 + 2048 * i, 512) for i in range(2)]
        at_hi = at("at_hi", r0 + 16384, 512, F32R)
        at_lo = at("at_lo", r0 + 18432, 512, F32R)
        ye_hi = at("ye_hi", r0 + 20480, D, F32R)
        ye_lo = at("ye_lo", r0 + 24576, D, F32R)
        pe_sel = at("pe_sel", r0 + 28672, 3 * P, F32R)
        pt_sel = [at(f"pt_sel{i}", r0 + 30208 + i * 52736, T, F32R) for i in range(2)]
        pos_e = at("pos_e", r0 + 31360, T)
        assert r0 + 89088 <= base + room, (base + room - r0)
        ps = ctx.enter_context(nc.psum_tensor("ps", [P, 8, 512], F32))

        wq5 = wq[:, :].rearrange("p (h b s t) -> p h b s t", h=H, b=NB, s=2)

        def cut(t, lo, n):
            return t[:, lo:lo + n]

        ab, beta, gg, gcs, bEG, eg, t0, t1, t2, glb = (
            cut(small, o, n) for o, n in [(0, 24), (24, 12), (36, 12), (48, 12), (60, 12), (72, 24), (96, 12),
                                          (108, 12), (120, 12), (448, 32)])
        lg, ex, o1, o2, scr, sel = (cut(small, 160 + 24 * i, 24) for i in range(6))
        wgt, posm = (cut(small, 512 + 32 * i, 3 * NE + 1) for i in range(2))
        m1, m2, rs3, cnt, npf, npf2 = (cut(small, 352 + 8 * i, 8) for i in range(6))
        pslot = [cut(small, 400 + i, 1) for i in range(2)]
        stmp = [cut(small, 416, 32), cut(small, 480, 32)]

        def pc(name, lo=0, n=None):
            a, b = PCOL[name]
            return par[:, a + lo:(b if n is None else a + lo + n)]

        def cc(name, rows=P, cols=None):
            a, b = CCOL[name]
            return con[0:rows, a:(b if cols is None else a + cols)]

        def kt(t, n=KD):
            return t[:, :].rearrange("p (k t) -> p k t", k=n)

        x3, hi3, lo3, hf3, sq3 = kt(x), kt(h_hi), kt(h_lo), kt(hf), kt(sq)
        qp3, cp3 = kt(qpad, QKV_T), kt(cpad, CT)

        def seqs(a):
            return a[:, TP:T].rearrange("p (b t) -> p b t", t=TD)

        def per_token(m9):
            return m9[:, :, 1:NC_].unsqueeze(3).to_broadcast([P, m9.shape[1], NB, TD])

        mod3 = [m[:, :].rearrange("p (s k c) -> p s k c", s=MODS, k=KD) for m in mod]
        gain3 = [g[:, :].rearrange("p (k c) -> p k c", k=KD) for g in gain]

        sem = lambda name: ctx.enter_context(nc.semaphore(name))
        raw_in = [sem(f"raw_in{i}") for i in range(NRAW)]
        hi_split = sem("hi_split")
        lo_split = sem("lo_split")
        unit_used = sem("unit_used")
        tile_done = sem("tile_done")
        bank_free = [sem(f"bank_free{i}") for i in range(4)]
        con_in, par_in_, x_loaded, c_loaded = sem("con_in"), sem("par_in"), sem("x_loaded"), sem("c_loaded")
        tap_prompt, taps_ready, taps_summed = sem("tap_prompt"), sem("taps_ready"), sem("taps_summed")
        dve_step, act_step = sem("dve_step"), sem("act_step")
        cs_ready, cstat_ready, expa_ready = sem("cs_ready"), sem("cstat_ready"), sem("expa_ready")
        row_ready, modT_ready, mod_ready = sem("row_ready"), sem("modT_ready"), sem("mod_ready")
        x_ready, sq_ready, ss_ready, rstd_ready = sem("x_ready"), sem("sq_ready"), sem("ss_ready"), sem("rstd_ready")
        hf_ready, hhi_ready, hlo_ready = sem("hf_ready"), sem("hhi_ready"), sem("hlo_ready")
        pad_ready, sig_ready, glu_ready, qkv_ready = sem("pad_ready"), sem("sig_ready"), sem("glu_ready"), sem("qkv_ready")
        z_ready, ab_done, ab_copied, conv_done = sem("z_ready"), sem("ab_done"), sem("ab_copied"), sem("conv_done")
        silu_done = sem("silu_done")
        pool_step, pconv_done, psilu_done = sem("pool_step"), sem("pconv_done"), sem("psilu_done")
        qsq_ready, qss_ready, qrs_ready, qn_ready = sem("qsq_ready"), sem("qss_ready"), sem("qrs_ready"), sem("qn_ready")
        cmean_done, cent_ready, csq_ready, css_ready = sem("cmean_done"), sem("cent_ready"), sem("csq_ready"), sem("css_ready")
        crs_ready, cn_ready, cy_ready = sem("crs_ready"), sem("cn_ready"), sem("cy_ready")
        beta_ready, abs_ready, sp_ready, g_ready = sem("beta_ready"), sem("abs_ready"), sem("sp_ready"), sem("g_ready")
        cum_ready, eg_ready, beg_ready = sem("cum_ready"), sem("eg_ready"), sem("beg_ready")
        gb_ready, mm1_done, er_ready, diff_ready, dexp_ready, dmask_ready = (
            sem(n) for n in ("gb_ready", "mm1_done", "er_ready", "diff_ready", "dexp_ready", "dmask_ready"))
        A_ready, qk_ready, at_done, at_copied, linit_ready = (
            sem(n) for n in ("A_ready", "qk_ready", "at_done", "at_copied", "linit_ready"))
        mt_ready, pm_done, pm_copied, q_done, l_ready = (
            sem(n) for n in ("mt_ready", "pm_done", "pm_copied", "q_done", "l_ready"))
        kv_done, kv_ready, w_done, nw_ready, qd_ready = (
            sem(n) for n in ("kv_done", "kv_ready", "w_done", "nw_ready", "qd_ready"))
        vn_done, vn_ready, o_done, o_copied, s_done, s_ready = (
            sem(n) for n in ("vn_done", "vn_ready", "o_done", "o_copied", "s_done", "s_ready"))
        swq_done, swq_copied, vx_ready, sst_in, sst_done, sst_ready = (
            sem(n) for n in ("swq_done", "swq_copied", "vx_ready", "sst_in", "sst_done", "sst_ready"))
        osq_ready, oss_ready, ors_ready, o_ready, mhi_ready, mlo_ready = (
            sem(n) for n in ("osq_ready", "oss_ready", "ors_ready", "o_ready", "mhi_ready", "mlo_ready"))
        gate_ready, prod_ready, ahi_ready, alo_ready = (
            sem(n) for n in ("gate_ready", "prod_ready", "ahi_ready", "alo_ready"))
        pads_in, pads_out, st_out, p_out, y_ready, y_sent = (
            sem(n) for n in ("pads_in", "pads_out", "st_out", "p_out", "y_ready", "y_sent"))
        tokT_done, tok_hi_ready, tok_lo_ready, lg_done, lg_ready, lsub_ready, lexp_ready = (
            sem(n) for n in ("tokT_done", "tok_hi_ready", "tok_lo_ready", "lg_done", "lg_ready", "lsub_ready", "lexp_ready"))
        sel_ready, pos_done, npass_ready, posT_done, posT_ready = (
            sem(n) for n in ("sel_ready", "pos_done", "npass_ready", "posT_done", "posT_ready"))
        psel_ready, gx_done, gx_copied, gt_done, gw_done, hthi_ready, htlo_ready, ptsel_ready = (
            sem(n) for n in ("psel_ready", "gx_done", "gx_copied", "gt_done", "gw_done", "hthi_ready", "htlo_ready", "ptsel_ready"))
        eg_gate, eg_prod, eT_done, eahi_ready, ealo_ready = (
            sem(n) for n in ("eg_gate", "eg_prod", "eT_done", "eahi_ready", "ealo_ready"))
        yhi_ready, ylo_ready, scat_done, facc_added, moe_step, fin_step = (
            sem(n) for n in ("yhi_ready", "ylo_ready", "scat_done", "facc_added", "moe_step", "fin_step"))
        moe_done, pass_step = sem("moe_done"), sem("pass_step")

        tiles = {}
        uses, done = [0] * 4, [0]

        def place(key, bank, unit=None):
            if unit is None:
                done[0] += 1
            tiles[key] = (bank, uses[bank], (tile_done, done[0]) if unit is None else (unit_used, unit + 1))
            uses[bank] += 1

        def place_pairs(phase, unit_of, n):
            for i in range(n):
                place((phase, i, 0), 2 * (i % 2))
                place((phase, i, 1), 2 * (i % 2) + 1, unit_of(i))

        def place_down():
            for d in range(KD):
                end = FT * (d + 1)
                place(("down", d), d % 4, U_DOWN + end // 16 - 1 if end % 16 == 0 else None)

        place_pairs(("in", 0), lambda i: in_unit(0, i), N_IN)
        place_pairs(("out", 0), lambda i: U_OUT[0] + i, N_OUT)
        place_pairs("up", lambda i: U_UP + i, N_UP)
        place_down()
        place_pairs(("in", 1), lambda i: in_unit(1, i), N_IN)
        place_pairs(("out", 1), lambda i: U_OUT[1] + i, N_OUT)
        uses_at = {l: [tiles[(("in", l), N_IN - 2 + b // 2, b % 2)][1] + 1 for b in range(4)] for l in range(DEPTH)}

        block = ctx.enter_context(nc.Block())

        @block.sync
        def _(sp):
            sp.dma_start(cs[:, :], c_in).then_inc(c_loaded, 16)

            def load(u, index, it=None, per=0, first=False):
                at_ = sp.snap(index * (P * UNIT)) if it is not None else index * (P * UNIT)
                if not first:
                    sp.wait_ge(lo_split, later(u - NRAW + 1, it, per))
                src = flat[bass.ds(at_, P * UNIT)].rearrange("(p n) -> p n", p=P)
                sp.dma_start(raw[u % NRAW][:, :], src).then_inc(raw_in[u % NRAW], 16)

            flat = units.rearrange("u p n -> (u p n)")
            for u in range(NRAW):
                load(u, u, first=True)
                if u == 1:
                    sp.dma_start(con[:, :], const_in).then_inc(con_in, 16)
                    sp.dma_start(x[:, :], x_in).then_inc(x_loaded, 16)
                if u == 3:
                    sp.dma_start(par[:, :], par_in).then_inc(par_in_, 16)
            turns = U_MOE // NRAW - 1
            with sp.Fori(0, turns) as i:
                for u in range(NRAW, 2 * NRAW):
                    load(u, i * NRAW + u, i, NRAW)
            for u in range((turns + 1) * NRAW, U_MOE + NRAW):
                load(u, u)
            sp.wait_ge(npass_ready, 1)
            n_pass = sp.value_load(npass_i[0:1, 0:1], min_val=1, max_val=3)
            with sp.Fori(0, n_pass) as p_:
                with sp.Fori(0, NE) as e_:
                    for k in range(PER_EXPERT):
                        load(U_MOE + NRAW + k, e_ * PER_EXPERT + (U_MOE + NRAW + k), p_ * NE + e_, PER_EXPERT)
            def landed(u):
                return sp.snap(n_pass * (NE * PER_EXPERT // NRAW * 16) + 16 * (u // NRAW + 1))

            sp.wait_ge(raw_in[U_MOE % NRAW], landed(U_MOE))
            sp.wait_ge(y_ready, 1)
            sp.dma_start(y_out[:, 0:KD * T // 2], hf[:, 0:KD * T // 2]).then_inc(y_sent, 16)
            last = landed(U_MOE + 1)
            assert U_MOE % NRAW == NRAW - 1
            for u in range(U_MOE + 1, U_MOE + NRAW):
                sp.wait_ge(raw_in[u % NRAW], last)
            sp.dma_start(y_out[:, KD * T // 2:], hf[:, KD * T // 2:]).then_inc(y_sent, 16)
            sp.wait_ge(y_sent, 32)

        @block.gpsimd
        def _(pool):
            def mask_heads(out, in_, mask, n):
                return pool.tensor_tensor(out, in_, mask.unsqueeze(1).to_broadcast([n, H, n]), ALU.mult)

            def heads(t, rows, n):
                return t[0:rows, 0:H * n].rearrange("p (h n) -> p h n", h=H)

            def masks(l, b, blk_i, n):
                pool.wait_ge(dexp_ready, 3 * l + blk_i + 1)
                strict, incl = ("afterS", "triS") if blk_i == 2 else ("after", "tri")
                da, dq = heads(blk[b]["da"], n, n), heads(blk[b]["dq"], n, n)
                mask_heads(da, da, cc(strict, n, n), n)
                mask_heads(dq, dq, cc(incl, n, n), n).then_inc(dmask_ready, 1)

            def level_mask(l, b, blk_i, n, q, s):
                pool.wait_ge(at_copied, 3 * l + blk_i + 1)
                if q >= 2 and q < 12:
                    pool.wait_ge(pm_done, 13 * l + q - 1)
                mask_heads(heads(blk[b]["MT"], n, n), heads(blk[b]["AT"], n, n), cc(f"mt{s}", n, n), n)\
                    .then_inc(mt_ready, 1)

            step = Steps(pool, pool_step)

            def conv_tile(l, m):
                bank, use, _ = tiles[(("in", l), I_QKV + m // 2, m % 2)]
                pool.wait_ge(bank_free[bank], use + 1)
                if m >= 2:
                    pool.wait_ge(psilu_done, CONV_POOL * l + m - 1)
                y, tmp = pconv[m % 2][:, 0:QOUT], pconv[2][:, 0:QOUT]
                step(pool.tensor_scalar(y, qp3[:, m, 0:QOUT], pc(f"wq{l}", m * CW, 1), None, ALU.mult))
                for j in range(1, CW):
                    step(pool.tensor_scalar(tmp, qp3[:, m, j:j + QOUT], pc(f"wq{l}", m * CW + j, 1), None, ALU.mult))
                    last = pool.tensor_tensor(y, y, tmp, ALU.add)
                    if j < CW - 1:
                        step(last)
                last.then_inc(pconv_done, 1)

            pool.wait_ge(con_in, 16)
            pool.wait_ge(par_in_, 16)
            for l in range(DEPTH):
                if l:
                    pool.wait_ge(st_out, 64 * l)
                    pool.wait_ge(x_ready, 2 * KD * l)
                pool.memset(qp3[:, :, 0:CW - 1], 0.0)
                pool.memset(cp3[:, :, 0:CK - 1], 0.0).then_inc(pad_ready, 1)
                pool.dma_start(qp3[:, :, QSAMP:QPAD], qst_in[l].rearrange("p (m s) -> p m s", m=QKV_T)).then_inc(pads_in, 16)
                pool.dma_start(cp3[:, :, CSAMP:CPAD], cst_in[l].rearrange("p (m s) -> p m s", m=CT)).then_inc(pads_in, 16)
                pool.wait_ge(ab_done, l + 1)
                for m in range(CONV_POOL):
                    conv_tile(l, m)
                if l:
                    pool.wait_ge(o_ready, l)
                for c in range(CT):
                    bank, use, _ = tiles[(("in", l), CONF_UNITS[c], 0)]
                    pool.wait_ge(bank_free[bank], use + 1)
                    if c or l:
                        pool.wait_ge(taps_summed, CT * l + c)
                    seg = cp3[:, c, CSAMP:CPAD].rearrange("p (b s) -> p b s", s=CSEG)
                    w = pc(f"wc{l}", CK * c, CK).unsqueeze(1).to_broadcast([P, NB, CK])
                    dst = taps_s[:, :].rearrange("p (b t j) -> p b t j", b=NB, t=TD)
                    for t in range(TD):
                        last = pool.tensor_tensor(dst[:, :, t], seg[:, :, t:t + CK], w, ALU.mult)
                    last.then_inc(taps_ready, 1)
                for m in range(QKV_T - 4, QKV_T):
                    bank, use, _ = tiles[(("in", l), I_QKV + m // 2, m % 2)]
                    pool.wait_ge(bank_free[bank], use + 1)
                for i in CONF_UNITS[2:]:
                    bank, use, _ = tiles[(("in", l), i, 0)]
                    pool.wait_ge(bank_free[bank], use + 1)
                pool.dma_start(qst_out[l], qpad[:, :]).then_inc(pads_out, 16)
                pool.dma_start(cst_out[l], cpad[:, :]).then_inc(pads_out, 16)
                for b in range(2):
                    masks(l, b, b, P)
                for i, s in enumerate(LEVELS):
                    for b in range(2):
                        level_mask(l, b, b, P, 2 * i + b, s)
                pool.wait_ge(pads_out, 32 * (l + 1))
                pool.wait_ge(cn_ready, 2 * l + 2)
                for h in range(H):
                    pool.dma_start(sst[h][:, :], gdn_in[l, h]).then_inc(sst_in, 16)
                pool.wait_ge(s_ready, 2 * l + 2)
                pool.dma_start(gdnp_out[l], S[:, :]).then_inc(p_out, 16)
                masks(l, 0, 2, TS)
                level_mask(l, 0, 2, TS, 12, 2)
                for h in range(H):
                    pool.wait_ge(sst_ready, H * l + h + 1)
                    pool.dma_start(gdns_out[l, h], sst[h][:, :]).then_inc(st_out, 16)
            pool.wait_ge(hlo_ready, 8)
            pool.wait_ge(st_out, 64 * DEPTH)
            pool.memset(tok_hi[:, 2 * D:3 * D].bitcast(F32), 0.0)
            pool.memset(tok_lo[:, 2 * D:3 * D].bitcast(F32), 0.0).then_inc(pad_ready, 1)
            pool.memset(facc[:, :], 0.0).then_inc(pad_ready, 1)
            pool.wait_ge(lg_done, 1)
            pool.wait_ge(tokT_done, 3)
            pool.memset(ye_hi[:, :].bitcast(F32), 0.0)
            pool.memset(ye_lo[:, :].bitcast(F32), 0.0)
            pool.memset(pt_sel[1][:, :].bitcast(F32), 0.0).then_inc(ylo_ready, 1)
            pool.wait_ge(p_out, 16 * DEPTH)

        @block.scalar
        def _(act):
            step = Steps(act, act_step)

            def split_hi(u, it=None, per=0):
                act.wait_ge(raw_in[u % NRAW], later(16 * (u // NRAW + 1), it, per // NRAW * 16))
                if u >= NSPLIT:
                    act.wait_ge(unit_used, later(u - NSPLIT + 1, it, per))
                act.activation(whi[u % NSPLIT][:, :], raw[u % NRAW][:, :], ACT.Copy).then_inc(hi_split, 1)

            def heads(t, rows, n):
                return t[0:rows, 0:H * n].rearrange("p (h n) -> p h n", h=H)

            def bank_heads(bank, rows, n):
                return ps[0:rows, bank, 0:H * n].rearrange("p (h n) -> p h n", h=H)

            def wait_tile(key, it=None, per=0):
                bank, use, (s, v) = tiles[key]
                act.wait_ge(s, later(v, it, per))
                return bank

            def row_copy(l, j, bank, used, it=None):
                act.wait_ge(unit_used, later(used, it, 6))
                act.activation(modrow[l][j % 3][0:2 * NC_, :], ps[0:2 * NC_, bank, :], ACT.Copy).then_inc(row_ready, 1)

            def rsqrt(out, in_, scale, eps, done):
                step(act.activation(out, in_, ACT.Ln, bias=cc(eps), scale=scale))
                act.activation(out, out, ACT.Exp, scale=-0.5).then_inc(done, 1)

            def norm(n):
                for d in range(KD):
                    act.wait_ge(x_ready, KD * (n - 1) + d + 1) if n else act.wait_ge(x_loaded, 16)
                    act.activation(kt(sqx[n])[:, d], x3[:, d], ACT.Square).then_inc(sq_ready, 1)
                act.wait_ge(ss_ready, n + 1)
                rsqrt(rstd[:, :], ps[:, 0 if n < 4 and n != 2 else 7, 0:T], 1.0 / D, "eps6", rstd_ready)

            def round_h(n):
                for half in range(2):
                    ks = slice(4 * half, 4 * half + 4)
                    act.wait_ge(hf_ready, 2 * n + half + 1)
                    act.activation(hi3[:, ks], hf3[:, ks], ACT.Copy).then_inc(hhi_ready, 1)

            def silu_tile(l, m):
                if m < CONV_POOL:
                    act.wait_ge(pconv_done, CONV_POOL * l + m + 1)
                    src, done = pconv[m % 2], psilu_done
                else:
                    act.wait_ge(conv_done, H * l + m - CONV_POOL + 1)
                    src, done = ctmp[:, (m % 2) * COLUMNS_IN:(m % 2 + 1) * COLUMNS_IN], silu_done
                act.activation(kt(qkv, QKV_T)[:, m, 0:TP], src[:, 0:TP], ACT.Silu)
                act.activation(seqs(kt(qkv, QKV_T)[:, m]),
                               src[:, QSAMP:QSAMP + NB * QSEG].rearrange("p (b s) -> p b s", s=QSEG)[:, :, 0:TD],
                               ACT.Silu).then_inc(done, 1)

            def project_in(l):
                for i in range(N_IN):
                    split_hi(in_unit(l, i) + LEAD)
                    if l == 0 and i:
                        row_copy(1, i - 1, 5 + (i - 1) % 2, ada_unit_of(1, 2 * i - 1) + 1)
                    if i in CONF_UNITS:
                        c = CONF_UNITS.index(i)
                        bank = wait_tile((("in", l), i, 1))
                        if c:
                            ub, uu, _ = tiles[(("in", l), CONF_UNITS[c - 1], 0)]
                            act.wait_ge(bank_free[ub], uu + 1)
                        act.activation(sg[:, 0:T], ps[:, bank, 0:T], ACT.Sigmoid).then_inc(bank_free[bank], 1)
                    elif i < I_Z:
                        if i == I_QKV:
                            act.wait_ge(pads_in, 32 * (l + 1))
                        for s in range(2):
                            m = 2 * (i - I_QKV) + s
                            bank = wait_tile((("in", l), i, s))
                            act.activation(qp3[:, m, CW - 1:QSAMP], ps[:, bank, 0:TP], ACT.Copy)
                            act.activation(qp3[:, m, QSAMP:QPAD].rearrange("p (b s) -> p b s", s=QSEG)[:, :, CW - 1:QSEG],
                                           seqs(ps[:, bank]), ACT.Copy).then_inc(bank_free[bank], 1)
                    else:
                        for s in range(2):
                            bank = wait_tile((("in", l), i, s))
                            act.activation(kt(zs, H)[:, 2 * (i - I_Z) + s], ps[:, bank, 0:T], ACT.Silu)\
                                .then_inc(bank_free[bank], 1)
                    if i >= 4:
                        silu_tile(l, i - 4)
                    if i >= 8:
                        silu_tile(l, CONV_POOL + i - 8)
                    if l == 0:
                        split_hi(in_unit(l, i) + 1 + LEAD)
                        split_hi(in_unit(l, i) + 2 + LEAD)
                if l == 0:
                    row_copy(1, N_IN - 1, 5 + (N_IN - 1) % 2, ada_unit_of(1, 2 * N_IN - 1) + 1)

            def gate_rows(l, b, blk_i, n):
                src = gg[0:n, blk_i * H:(blk_i + 1) * H].unsqueeze(2).to_broadcast([n, H, P])
                act.activation(heads(blk[b]["MT"], n, P), src, ACT.Copy).then_inc(gb_ready, 1)

            def block_start(l, b, blk_i, n):
                act.wait_ge(mm1_done, 3 * l + blk_i + 1)
                act.activation(heads(blk[b]["er"], P, n), bank_heads(b, P, n), ACT.Exp).then_inc(er_ready, 1)

            def decay(l, b, blk_i, n):
                act.wait_ge(diff_ready, 3 * l + blk_i + 1)
                da, dq = heads(blk[b]["da"], n, n), heads(blk[b]["dq"], n, n)
                act.activation(da, da, ACT.Exp, scale=-1.0)
                act.activation(dq, dq, ACT.Exp).then_inc(dexp_ready, 1)

            def copy_at(l, b, blk_i, n):
                act.wait_ge(at_done, 3 * l + blk_i + 1)
                act.activation(heads(blk[b]["AT"], n, n), bank_heads(b, n, n), ACT.Copy).then_inc(at_copied, 1)

            def copy_pm(l, b, n, q):
                act.wait_ge(pm_done, 13 * l + q + 1)
                act.activation(heads(blk[b]["PM"], n, n), bank_heads(2 + b, n, n), ACT.Copy).then_inc(pm_copied, 1)

            def scale_kv(l, b, blk_i, n, kd):
                act.wait_ge(kv_done, 3 * l + blk_i + 1)
                for bank, dst, scale in ((b, blk[b]["da"], bEG), (b, kd, cut(small, 84, 12)), (2 + b, blk[b]["AT"], beta)):
                    for h in range(H):
                        c = blk_i * H + h
                        last = act.activation(heads(dst, n, P)[:, h], bank_heads(bank, n, P)[:, h], ACT.Copy,
                                              scale=scale[0:n, c:c + 1])
                last.then_inc(kv_ready, 1)

            def negate_w(l, b, blk_i, n):
                act.wait_ge(w_done, 3 * l + blk_i + 1)
                act.activation(heads(blk[b]["PM"], P, n), bank_heads(4 + b, P, n), ACT.Copy, scale=-1.0)\
                    .then_inc(nw_ready, 1)

            def copy_vn(l, b, blk_i, n, dst, bank):
                act.wait_ge(vn_done, 3 * l + blk_i + 1)
                act.activation(heads(dst, n, P), bank_heads(bank, n, P), ACT.Copy).then_inc(vn_ready, 1)

            def copy_o(l, b, blk_i, n):
                act.wait_ge(o_done, 3 * l + blk_i + 1)
                act.activation(kt(oall, H)[:, :, blk_i * P:blk_i * P + n], bank_heads(b, P, n), ACT.Copy)\
                    .then_inc(o_copied, 1)

            def square_conf(l, t):
                act.wait_ge(cent_ready, 2 * l + t + 1)
                if t == 0:
                    act.wait_ge(pads_out, 32 * (l + 1))
                act.activation(kt(csq, CT)[:, 2 * t:2 * t + 2], kt(yc, CT)[:, 2 * t:2 * t + 2], ACT.Square)\
                    .then_inc(csq_ready, 1)

            def rates_conf(l, t):
                act.wait_ge(css_ready, 2 * l + t + 1)
                rsqrt(kt(crs, CT)[:, 2 * t:2 * t + 2], ps[:, 0:2, 0:T], 1.0 / P, "eps5", crs_ready)

            def mixer(l):
                act.wait_ge(ab_done, l + 1)
                act.wait_ge(psilu_done, CONV_POOL * (l + 1))
                act.activation(hf[:, :], qkv[:, 0:2 * H * T], ACT.Square).then_inc(qsq_ready, 1)
                act.wait_ge(ab_copied, l + 1)
                ab3 = ab.rearrange("p (b c) -> p b c", b=3)
                act.activation(beta.rearrange("p (b c) -> p b c", b=3), ab3[:, :, 0:H], ACT.Sigmoid).then_inc(beta_ready, 1)
                act.wait_ge(abs_ready, l + 1)
                step(act.activation(t0, t0, ACT.Exp, scale=-1.0))
                act.activation(t0, t0, ACT.Ln, bias=cc("one")).then_inc(sp_ready, 1)
                for i, (scale, eps) in enumerate(((float(P), "epsq"), (1.0, "eps6"))):
                    act.wait_ge(qss_ready, 2 * l + i + 1)
                    rsqrt(kt(qrs[i], H), ps[:, 4 * i:4 * i + 4, 0:T], scale, eps, qrs_ready)
                act.wait_ge(g_ready, l + 1)
                for b in range(2):
                    gate_rows(l, b, b, P)
                act.wait_ge(cum_ready, l + 1)
                act.activation(eg, ps[:, 0, 0:24], ACT.Exp).then_inc(eg_ready, 1)
                for b in range(2):
                    block_start(l, b, b, P)
                for b in range(2):
                    decay(l, b, b, P)
                for b in range(2):
                    copy_at(l, b, b, P)
                for i in range(len(LEVELS)):
                    for b in range(2):
                        copy_pm(l, b, P, 2 * i + b)
                    if i in (3, 5):
                        square_conf(l, (i - 3) // 2)
                    if i == 4:
                        rates_conf(l, 0)
                rates_conf(l, 1)
                for b in range(2):
                    scale_kv(l, b, b, P, blk[b]["L"])
                for b in range(2):
                    negate_w(l, b, b, P)
                for b in range(2):
                    copy_vn(l, b, b, P, blk[b]["MT"], 6 + b)
                    copy_o(l, b, b, P)
                act.wait_ge(s_done, 2 * l + 2)
                gate_rows(l, 0, 2, TS)
                block_start(l, 0, 2, TS)
                decay(l, 0, 2, TS)
                copy_at(l, 0, 2, TS)
                copy_pm(l, 0, TS, 12)
                scale_kv(l, 0, 2, TS, blk[1]["MT"])
                act.wait_ge(w_done, 3 * l + 3)
                act.activation(wq5[:, :, :, 0], ps[:, 4, 0:H * TS].rearrange("p (h b t) -> p h b t", h=H, b=NB), ACT.Copy,
                               scale=-1.0).then_inc(nw_ready, 1)
                act.wait_ge(cn_ready, 2 * l + 2)
                for c in range(CT):
                    last = act.activation(kt(yc, CT)[:, c], kt(yc, CT)[:, c], ACT.Silu, bias=pc(f"bln{l}", c, 1),
                                          scale=pc(f"gln{l}", c, 1))
                last.then_inc(cy_ready, 1)
                act.wait_ge(cy_ready, l + 1)
                act.wait_ge(swq_done, l + 1)
                for s in range(2):
                    act.activation(swq[:, s * H * TS:(s + 1) * H * TS].rearrange("p (n t) -> p n t", t=TD),
                                   ps[:, 6, 0:2 * H * TS].rearrange("p (n s t) -> p n s t", s=2, t=TD)[:, :, s],
                                   ACT.Copy).then_inc(swq_copied, 1)
                copy_vn(l, 0, 2, TS, blk[1]["er"], 2)
                act.activation(hi3[:, 4:8], kt(yc, CT), ACT.Copy).then_inc(mhi_ready, 1)
                act.wait_ge(o_copied, 3 * l + 3)
                act.activation(osq[:, :], oall[:, :], ACT.Square).then_inc(osq_ready, 1)
                act.wait_ge(oss_ready, l + 1)
                rsqrt(kt(ors, H), ps[:, 0:8:2, 0:T], 1.0 / P, "eps6", ors_ready)
                act.wait_ge(o_ready, l + 1)
                act.activation(hi3[:, 0:4], kt(oall, H), ACT.Copy).then_inc(mhi_ready, 1)

            act.wait_ge(c_loaded, 16)
            act.activation(cs[:, :], cs[:, :], ACT.Silu).then_inc(cs_ready, 1)
            act.wait_ge(cs_ready, 1)
            cst3 = cstat[:, :].rearrange("p (k c) -> p k c", k=KD)
            act.activation(cst3[:, :, 0:NC_], cs[:, :].rearrange("p (k c) -> p k c", k=KD), ACT.Copy).then_inc(cstat_ready, 1)
            for u in range(LEAD):
                split_hi(u)
            act.wait_ge(con_in, 16)
            norm(0)
            act.wait_ge(par_in_, 16)
            for l in range(DEPTH):
                a, _ = PCOL[f"alog{l}"]
                act.activation(par[:, a:a + 12], par[:, a:a + 12], ACT.Exp).then_inc(expa_ready, 1)

            def ada(c, it=None):
                split_hi(c + LEAD, it, 6)
                if c % 2:
                    row_copy(0, c // 2, 4 + c // 2 % 3, c + 1, it)

            for c in range(6):
                ada(c)
            with act.Fori(0, N_ADA // 6 - 1) as i:
                for c in range(6, 12):
                    ada(c, i)
            round_h(0)
            project_in(0)
            mixer(0)
            for i in range(N_OUT):
                split_hi(U_OUT[0] + i + LEAD)
            norm(1)
            round_h(1)

            def up(i, it=None):
                split_hi(U_UP + i + LEAD, it, 6)
                bank, use, (s, v) = tiles[("up", i, 0)]
                act.wait_ge(s, later(v, it, 6))
                ub, uu, _ = tiles[("up", i, 1)]
                act.wait_ge(bank_free[ub], later(uu, it, 3))
                act.activation(sg[:, (i % 2) * T:(i % 2) * T + T], ps[:, bank, 0:T], ACT.Silu).then_inc(bank_free[bank], 1)
                act.wait_ge(bank_free[ub], later(uu + 1, it, 3))
                dst = act_hi[:, i * T:(i + 1) * T] if it is None else act_hi[:, bass.ds(it * (6 * T) + i * T, T)]
                act.activation(dst, ctmp[:, (i % 2) * 316:(i % 2) * 316 + T], ACT.Copy).then_inc(ahi_ready, 1)

            act.wait_ge(st_out, 64)
            with act.Fori(0, N_UP // 6) as i:
                for c in range(6):
                    up(c, i)
            for c in range(N_UP // 6 * 6, N_UP):
                up(c)
            for i in range(N_DOWN):
                split_hi(U_DOWN + i + LEAD)
            norm(2)
            round_h(2)
            project_in(1)
            mixer(1)
            for i in range(N_OUT):
                split_hi(U_OUT[1] + i + LEAD)
            norm(3)
            round_h(3)
            act.wait_ge(lsub_ready, 1)
            act.activation(ex, lg, ACT.Exp).then_inc(lexp_ready, 1)
            for b in range(3):
                n = TS if b == 2 else P
                if b == 2:
                    act.wait_ge(pad_ready, DEPTH + 1)
                act.wait_ge(tokT_done, b + 1)
                act.activation(tok_hi[0:n, b * D:(b + 1) * D].rearrange("p (a n) -> p a n", a=2),
                               ps[0:n, 2 * b:2 * b + 2, :], ACT.Copy).then_inc(tok_hi_ready, 1)
            act.wait_ge(npass_ready, 1)
            n_pass = act.value_load(npass_i[0:1, 0:1], min_val=1, max_val=3)

            def gather(g, q, part, bank=7):
                if part < 2:
                    act.wait_ge(gx_done, g * 2 + part + 1)
                    act.activation(xe[:, part * 512:(part + 1) * 512], ps[:, bank, :], ACT.Copy).then_inc(gx_copied, 1)
                elif part < 4:
                    act.wait_ge(gt_done, g * 2 + part - 1)
                    act.activation(ht_hi[q][:, (part - 2) * 512:(part - 1) * 512], ps[:, bank, :], ACT.Copy).then_inc(hthi_ready, 1)

            with act.Fori(0, n_pass) as p_:
                for part in range(4):
                    gather(p_ * (NE + 1), 0, part, part)
                with act.Fori(0, NE // 2) as pair:
                    for q in range(2):
                        it = p_ * NE + pair * 2 + q

                        def round_hidden(c):
                            act.wait_ge(eT_done, it * FC + c + 1)
                            act.activation(at_hi[:, :], ps[:, 4, :], ACT.Copy).then_inc(eahi_ready, 1)

                        for k, (kind, c, half) in enumerate(expert_units()):
                            split_hi(U_MOE + k + LEAD, it, PER_EXPERT)
                            if kind == "g" and half:
                                act.wait_ge(unit_used, later(U_MOE + k + 1, it, PER_EXPERT))
                                if c >= 2:
                                    act.wait_ge(eg_prod, it * FC + c - 1)
                                act.activation(sge[c % 2][:, :], ps[:, c % 2, :], ACT.Silu).then_inc(eg_gate, 1)
                                if c:
                                    round_hidden(c - 1)
                            if (kind, c, half) == ("d", FC - 2, 1):
                                round_hidden(FC - 1)
                            if k - 1 in GATHER_AT:
                                gather(p_ * (NE + 1) + pair * 2 + (q + 1), 1 - q, GATHER_AT.index(k - 1))
                        act.wait_ge(scat_done, it * KD + KD)
                        act.wait_ge(unit_used, later(U_MOE + PER_EXPERT, it, PER_EXPERT))
                        act.activation(ye_hi[:, :].rearrange("p (a n) -> p a n", a=2), ps[:, 5:7, :], ACT.Copy,
                                       scale=pslot[q]).then_inc(yhi_ready, 1)
            norm(4)

        @block.vector
        def _(dve):
            step = Steps(dve, dve_step)

            def split_lo(u, it=None, per=0):
                dve.wait_ge(hi_split, later(u + 1, it, per))
                dve.tensor_tensor(wlo[u % NSPLIT][:, :], raw[u % NRAW][:, :], whi[u % NSPLIT][:, :].bitcast(F32),
                                  ALU.subtract).then_inc(lo_split, 1)

            def heads(t, rows, n):
                return t[0:rows, 0:H * n].rearrange("p (h n) -> p h n", h=H)

            def bank_heads(bank, rows, n):
                return ps[0:rows, bank, 0:H * n].rearrange("p (h n) -> p h n", h=H)

            def wait_tile(key, it=None, per=0):
                bank, use, (s, v) = tiles[key]
                dve.wait_ge(s, later(v, it, per))
                return bank

            def modulation(l):
                dve.wait_ge(modT_ready, 12 * (l + 1))
                bias = pc(f"b_ada{l}").unsqueeze(2).to_broadcast([P, MODS * KD, NC_])
                step(dve.tensor_tensor(mod[l][:, :].rearrange("p (k c) -> p k c", c=NC_),
                                       ps[:, 7, 0:MODS * KD * NC_].rearrange("p (k c) -> p k c", c=NC_), bias, ALU.add))
                for i, (s, g) in enumerate(((1, "g1"), (4, "g2"))):
                    g9 = pc(f"{g}{l}").unsqueeze(2).to_broadcast([P, KD, NC_])
                    last = dve.scalar_tensor_tensor(gain3[2 * l + i], mod3[l][:, s], 1.0, g9, ALU.add, ALU.mult)
                last.then_inc(mod_ready, 1)

            def rate(n, half):
                ks = slice(4 * half, 4 * half + 4)
                step(dve.tensor_tensor(sq3[:, ks], x3[:, ks], rstd[:, :].unsqueeze(1).to_broadcast([P, 4, T]), ALU.mult))

            def norm(n):
                l, shift = n // 2, mod3[n // 2][:, 3 * (n % 2)]
                if n:
                    dve.wait_ge(x_ready, KD * n)
                    dve.wait_ge(rstd_ready, n + 1)
                if n % 2:
                    dve.wait_ge(p_out, 8 * (n + 1))
                    dve.wait_ge(sst_done, H * (n + 1) // 2)
                dve.wait_ge(mod_ready, l + 1)
                for half in range(2):
                    if n:
                        rate(n, half)
                    for k in range(4 * half, 4 * half + 4):
                        dve.tensor_scalar(hf3[:, k, 0:TP], sq3[:, k, 0:TP], gain3[n][:, k, 0:1], shift[:, k, 0:1],
                                          ALU.mult, ALU.add)
                    ks = slice(4 * half, 4 * half + 4)
                    sample = lambda t: t[:, ks, TP:T].rearrange("p k (b t) -> p k b t", t=TD)
                    step(dve.tensor_tensor(sample(hf3), sample(sq3), per_token(gain3[n][:, ks]), ALU.mult))
                    dve.tensor_tensor(sample(hf3), sample(hf3), per_token(shift[:, ks]), ALU.add).then_inc(hf_ready, 1)
                for half in range(2):
                    ks = slice(4 * half, 4 * half + 4)
                    dve.wait_ge(hhi_ready, 2 * n + half + 1)
                    dve.tensor_tensor(lo3[:, ks], hf3[:, ks], hi3[:, ks].bitcast(F32), ALU.subtract).then_inc(hlo_ready, 1)

            def conf_taps(l, first, end):
                for n in range(first, end):
                    c, j = divmod(n, CK)
                    y = kt(yc, CT)[:, c, 0:TP]
                    w = pc(f"wc{l}", n, 1)
                    if j == 0:
                        ub, uu, _ = tiles[(("in", l), CONF_UNITS[c], 0)]
                        dve.wait_ge(bank_free[ub], uu + 1)
                        dve.tensor_scalar(y, cp3[:, c, 0:TP], w, pc(f"bc{l}", c, 1), ALU.mult, ALU.add)\
                            .then_inc(tap_prompt, 1)
                        continue
                    dve.wait_ge(tap_prompt, l * CT * CK + n)
                    dve.scalar_tensor_tensor(y, cp3[:, c, j:j + TP], w, y, ALU.mult, ALU.add).then_inc(tap_prompt, 1)

            def sample_taps(l, c):
                dve.wait_ge(taps_ready, CT * l + c + 1)
                y = kt(yc, CT)[:, c, TP:T]
                step(dve.tensor_reduce(y, taps_s[:, :].rearrange("p (n j) -> p n j", j=CK), AX.X, ALU.add))
                dve.tensor_scalar(y, y, pc(f"bc{l}", c, 1), None, ALU.add).then_inc(taps_summed, 1)

            def conv_tile(l, m):
                bank, use, _ = tiles[(("in", l), I_QKV + m // 2, m % 2)]
                dve.wait_ge(bank_free[bank], use + 1)
                if m >= CONV_POOL + 2:
                    dve.wait_ge(silu_done, H * l + m - CONV_POOL - 1)
                y = ctmp[:, (m % 2) * COLUMNS_IN:(m % 2) * COLUMNS_IN + QOUT]
                step(dve.tensor_scalar(y, qp3[:, m, 0:QOUT], pc(f"wq{l}", m * CW, 1), None, ALU.mult))
                for j in range(1, CW):
                    last = dve.scalar_tensor_tensor(y, qp3[:, m, j:j + QOUT], pc(f"wq{l}", m * CW + j, 1), y,
                                                    ALU.mult, ALU.add)
                    if j < CW - 1:
                        step(last)
                last.then_inc(conv_done, 1)

            taps = [0]

            def fill(l, n):
                n = min(n, CT * CK - taps[0])
                conf_taps(l, taps[0], taps[0] + n)
                taps[0] += n

            def project_in(l):
                taps[0] = 0
                for i in range(N_IN):
                    split_lo(in_unit(l, i) + LEAD)
                    if i == 0:
                        dve.wait_ge(pads_in, 32 * (l + 1))
                        dve.wait_ge(pad_ready, l + 1)
                    v = i - (I_QKV + H + 1)
                    if 0 <= v < H:
                        conv_tile(l, CONV_POOL + v)
                    if i == 1:
                        copy_rates(l)
                    fill(l, taps_in(l, i))
                    if i in CONF_UNITS:
                        c = CONF_UNITS.index(i)
                        bank = wait_tile((("in", l), i, 0))
                        gb, gu, _ = tiles[(("in", l), i, 1)]
                        dve.wait_ge(bank_free[gb], gu + 1)
                        dve.tensor_tensor(cp3[:, c, CK - 1:CSAMP], ps[:, bank, 0:TP], sg[:, 0:TP], ALU.mult)
                        dst = cp3[:, c, CSAMP:CPAD].rearrange("p (b s) -> p b s", s=CSEG)[:, :, CK - 1:CSEG]
                        dve.tensor_tensor(dst, seqs(ps[:, bank]), seqs(sg), ALU.mult).then_inc(bank_free[bank], 1)
                    if l == 0:
                        split_lo(in_unit(l, i) + 1 + LEAD)
                        split_lo(in_unit(l, i) + 2 + LEAD)

            def copy_rates(l):
                step(dve.memset(ab, 0.0))
                dve.wait_ge(ab_done, l + 1)
                dve.tensor_copy(ab[:, 0:16], ps[:, 4, 0:16])
                dve.tensor_copy(ab[0:TS, 16:24], ps[0:TS, 4, 16:24]).then_inc(ab_copied, 1)

            def decay_rates(l):
                dve.wait_ge(ab_copied, l + 1)
                a3 = ab.rearrange("p (b c) -> p b c", b=3)[:, :, H:2 * H]
                v3 = lambda t: t.rearrange("p (b c) -> p b c", b=3)
                step(dve.tensor_tensor(v3(t1), a3, v3(pc(f"dt{l}")), ALU.add))
                step(dve.tensor_scalar(t2, t1, -1.0, None, ALU.mult))
                dve.tensor_tensor(t0, t1, t2, ALU.max).then_inc(abs_ready, 1)
                dve.wait_ge(abs_ready, l + 1)
                step(dve.tensor_scalar(t1, t1, 0.0, None, ALU.max))
                dve.wait_ge(sp_ready, l + 1)
                step(dve.tensor_tensor(t1, t1, t0, ALU.add))
                dve.wait_ge(expa_ready, l + 1)
                dve.scalar_tensor_tensor(gg, t1, -1.0, pc(f"alog{l}"), ALU.mult, ALU.mult).then_inc(g_ready, 1)

            def differences(l, b, blk_i, n):
                dve.wait_ge(er_ready, 3 * l + blk_i + 1)
                for dst, clip in (("da", ALU.max), ("dq", ALU.min)):
                    for h in range(H):
                        last = dve.tensor_scalar(heads(blk[b][dst], n, n)[:, h], bank_heads(b, n, n)[:, h],
                                                 gcs[0:n, blk_i * H + h:blk_i * H + h + 1], 0.0, ALU.subtract, clip)
                last.then_inc(diff_ready, 1)

            def products(l, b, blk_i, n):
                dve.wait_ge(dmask_ready, 3 * l + blk_i + 1)
                for h in range(H):
                    da = heads(blk[b]["da"], n, n)[:, h]
                    last = dve.scalar_tensor_tensor(da, bank_heads(2 + b, n, n)[:, h],
                                                    beta[0:n, blk_i * H + h:blk_i * H + h + 1], da, ALU.mult, ALU.mult)
                last.then_inc(A_ready, 1)
                dq = heads(blk[b]["dq"], n, n)
                dve.tensor_tensor(dq, bank_heads(4 + b, n, n), dq, ALU.mult).then_inc(qk_ready, 1)

            def inverse_start(l, b, blk_i, n):
                wide = lambda name: cc(name, n, n).unsqueeze(1).to_broadcast([n, H, n])
                L, LT = heads(blk[b]["L"], n, n), heads(blk[b]["LT"], n, n)
                dve.wait_ge(A_ready, 3 * l + blk_i + 1)
                step(dve.tensor_tensor(L, heads(blk[b]["da"], n, n), wide("m1l"), ALU.mult))
                step(dve.tensor_tensor(L, wide("ident"), L, ALU.subtract))
                dve.wait_ge(at_copied, 3 * l + blk_i + 1)
                step(dve.tensor_tensor(LT, heads(blk[b]["AT"], n, n), wide("m1t"), ALU.mult))
                dve.tensor_tensor(LT, wide("ident"), LT, ALU.subtract).then_inc(linit_ready, 1)

            def inverse_level(l, b, n, q, s, final):
                dve.wait_ge(q_done, 13 * l + q + 1)
                if q in (0, 1, 12):
                    dve.wait_ge(linit_ready, 3 * l + (2 if q == 12 else q) + 1)
                else:
                    dve.wait_ge(l_ready, 13 * l + q - 1)
                half = lambda t, i: t.rearrange("p (g c) -> p g c", c=2 * s)[:, :, i * s:(i + 1) * s]
                L, LT = blk[b]["L"][0:n, 0:H * n], blk[b]["LT"][0:n, 0:H * n]
                if not final:
                    dve.tensor_tensor(half(L, 0), half(L, 0), half(ps[0:n, 4 + b, 0:H * n], 0), ALU.subtract)
                dve.tensor_tensor(half(LT, 1), half(LT, 1), half(ps[0:n, 6 + b, 0:H * n], 1), ALU.subtract).then_inc(l_ready, 1)

            def decayed_q(l, b, blk_i, n):
                er = heads(blk[b]["er"], P, n)
                if blk_i < 2:
                    step(dve.tensor_copy(glb[:, b * H:(b + 1) * H], er[:, :, n - 1]))
                else:
                    step(dve.tensor_copy(glb.rearrange("p (h b) -> p h b", h=H), er[:, :, TD - 1:n:TD]))
                q = kt(qkv, QKV_T)[:, 0:H, blk_i * P:blk_i * P + n]
                if blk_i < 2:
                    dve.tensor_tensor(er, q, er, ALU.mult).then_inc(qd_ready, 1)
                else:
                    by_seq = lambda t: t.rearrange("p h (b t) -> p h b t", t=TD)
                    dve.tensor_tensor(wq5[:, :, :, 1], by_seq(q), by_seq(er), ALU.mult).then_inc(qd_ready, 1)

            def center_conf(l, t):
                y = kt(yc, CT)[:, 2 * t:2 * t + 2]
                dve.wait_ge(cmean_done, 2 * l + t + 1)
                dve.wait_ge(taps_summed, CT * (l + 1))
                dve.wait_ge(tap_prompt, CT * CK * (l + 1))
                dve.scalar_tensor_tensor(y, ps[:, 0:2, 0:T], -1.0 / P, y, ALU.mult, ALU.add).then_inc(cent_ready, 1)

            def scale_conf(l, t):
                y = kt(yc, CT)[:, 2 * t:2 * t + 2]
                dve.wait_ge(crs_ready, 2 * l + t + 1)
                dve.tensor_tensor(y, y, kt(crs, CT)[:, 2 * t:2 * t + 2], ALU.mult).then_inc(cn_ready, 1)

            def mixer(l):
                decay_rates(l)
                fill(l, FILL[0])
                sample_taps(l, 0)
                for i in range(2):
                    dve.wait_ge(qrs_ready, 2 * l + i + 1)
                    q3 = kt(qkv, QKV_T)[:, H * i:H * i + H]
                    dve.tensor_tensor(q3, q3, kt(qrs[i], H), ALU.mult).then_inc(qn_ready, 1)
                    fill(l, FILL[1])
                    sample_taps(l, 1 + i)
                dve.wait_ge(eg_ready, l + 1)
                dve.wait_ge(beta_ready, l + 1)
                dve.tensor_copy(gcs, ps[:, 0, 0:12])
                dve.tensor_tensor(bEG, beta, eg[:, 0:12], ALU.mult).then_inc(beg_ready, 1)
                dve.wait_ge(beg_ready, l + 1)
                fill(l, FILL[2])
                sample_taps(l, 3)
                for b in range(2):
                    differences(l, b, b, P)
                    fill(l, FILL[3])
                for b in range(2):
                    products(l, b, b, P)
                    fill(l, FILL[4])
                for b in range(2):
                    inverse_start(l, b, b, P)
                for i in range(len(LEVELS)):
                    for b in range(2):
                        inverse_level(l, b, P, 2 * i + b, LEVELS[i], i == len(LEVELS) - 1)
                        fill(l, FILL[5] if i == 0 else CT * CK)
                    if i in (2, 4):
                        center_conf(l, (i - 2) // 2)
                    if i == 4:
                        scale_conf(l, 0)
                for b in range(2):
                    decayed_q(l, b, b, P)
                scale_conf(l, 1)
                dve.wait_ge(s_done, 2 * l + 1)
                if l:
                    dve.wait_ge(p_out, 16 * l)
                dve.tensor_copy(heads(S, P, P), bank_heads(2, P, P)).then_inc(s_ready, 1)
                dve.wait_ge(s_done, 2 * l + 2)
                dve.wait_ge(s_ready, 2 * l + 1)
                for h in range(H):
                    s = heads(S, P, P)[:, h]
                    last = dve.scalar_tensor_tensor(s, s, glb[:, H + h:H + h + 1], bank_heads(3, P, P)[:, h],
                                                    ALU.mult, ALU.add)
                last.then_inc(s_ready, 1)
                differences(l, 0, 2, TS)
                products(l, 0, 2, TS)
                inverse_start(l, 0, 2, TS)
                inverse_level(l, 0, TS, 12, 2, True)
                dve.wait_ge(pads_out, 32 * (l + 1))
                decayed_q(l, 0, 2, TS)
                spread(l, 0)
                dve.wait_ge(o_done, 3 * l + 3)
                dve.wait_ge(swq_copied, 2 * l + 2)
                dve.tensor_tensor(kt(oall, H)[:, :, TP:T], bank_heads(0, P, TS),
                                  swq[:, H * TS:2 * H * TS].rearrange("p (h n) -> p h n", h=H), ALU.add)\
                    .then_inc(o_copied, 1)
                dve.wait_ge(mhi_ready, 2 * l + 1)
                dve.tensor_tensor(lo3[:, 4:8], kt(yc, CT), hi3[:, 4:8].bitcast(F32), ALU.subtract).then_inc(mlo_ready, 1)
                dve.wait_ge(ors_ready, l + 1)
                step(dve.tensor_tensor(oall[:, :], oall[:, :], ors[:, :], ALU.mult))
                dve.scalar_tensor_tensor(oall[:, :], oall[:, :], pc(f"gout{l}"), zs[:, :], ALU.mult, ALU.mult)\
                    .then_inc(o_ready, 1)
                dve.wait_ge(mhi_ready, 2 * l + 2)
                dve.tensor_tensor(lo3[:, 0:4], kt(oall, H), hi3[:, 0:4].bitcast(F32), ALU.subtract).then_inc(mlo_ready, 1)

            def spread(l, h):
                dve.wait_ge(vn_ready, 3 * l + 3)
                if h:
                    dve.wait_ge(sst_done, H * l + h)
                v = heads(blk[1]["er"], TS, P)[:, h].unsqueeze(1).to_broadcast([TS, NB, P])
                dve.tensor_tensor(vx[0:TS, :].rearrange("p (b n) -> p b n", b=NB), v,
                                  cc("seqp", TS).unsqueeze(2).to_broadcast([TS, NB, P]), ALU.mult).then_inc(vx_ready, 1)

            def new_states(l, h):
                dve.wait_ge(sst_done, H * l + h + 1)
                for b in range(NB):
                    s = sst[h][:, b * P:(b + 1) * P]
                    last = dve.scalar_tensor_tensor(s, s, glb[:, h * NB + b:h * NB + b + 1],
                                                    ps[:, 4 + 2 * (h % 2) + b // 4, (b % 4) * P:(b % 4 + 1) * P],
                                                    ALU.mult, ALU.add)
                last.then_inc(sst_ready, 1)

            def residual(key, l, which, d):
                bank, use, (s, v) = tiles[key]
                dve.wait_ge(s, v)
                add_gated(ps[:, bank], mod3[l][:, which], d, bank_free[bank])

            def add_gated(src, gate, d, read):
                tmp = stmp[d % 2].rearrange("p (b t) -> p b t", t=TD)
                step(dve.tensor_tensor(tmp, seqs(src), gate[:, d, 1:NC_].unsqueeze(2).to_broadcast([P, NB, TD]), ALU.mult))
                last = dve.scalar_tensor_tensor(x3[:, d, 0:TP], src[:, 0:TP], gate[:, d, 0:1], x3[:, d, 0:TP],
                                                ALU.mult, ALU.add)
                if read is not None:
                    last.then_inc(read, 1)
                dve.tensor_tensor(seqs(x3[:, d]), seqs(x3[:, d]), tmp, ALU.add).then_inc(x_ready, 1)

            cst3 = cstat[:, :].rearrange("p (k c) -> p k c", k=KD)
            dve.wait_ge(cstat_ready, 1)
            dve.tensor_tensor(cst3[:, :, NC_:2 * NC_], cs[:, :].rearrange("p (k c) -> p k c", k=KD),
                              cst3[:, :, 0:NC_].bitcast(F32), ALU.subtract).then_inc(cstat_ready, 1)
            for u in range(LEAD):
                split_lo(u)
            dve.wait_ge(rstd_ready, 1)
            for half in range(2):
                rate(0, half)
            with dve.Fori(0, N_ADA // 6) as i:
                for c in range(6):
                    split_lo(c + LEAD, i, 6)
            dve.wait_ge(par_in_, 16)
            modulation(0)
            norm(0)
            project_in(0)
            modulation(1)
            mixer(0)

            def project_out(l):
                for i in range(N_OUT):
                    split_lo(U_OUT[l] + i + LEAD)
                    for s in range(2):
                        residual((("out", l), i, s), l, 2, 2 * i + s)
                    new_states(l, i)
                    if i + 1 < H:
                        spread(l, i + 1)

            project_out(0)
            norm(1)

            def up(i, it=None):
                split_lo(U_UP + i + LEAD, it, 6)
                gb, gu, _ = tiles[("up", i, 0)]
                bank, use, (s, v) = tiles[("up", i, 1)]
                dve.wait_ge(bank_free[gb], later(gu + 1, it, 3))
                dve.wait_ge(s, later(v, it, 6))
                tmp = ctmp[:, (i % 2) * 316:(i % 2) * 316 + T]
                dve.tensor_tensor(tmp, ps[:, bank, 0:T], sg[:, (i % 2) * T:(i % 2) * T + T], ALU.mult)\
                    .then_inc(bank_free[bank], 1)
                dve.wait_ge(ahi_ready, later(i + 1, it, 6))
                cols = slice(i * T, (i + 1) * T) if it is None else bass.ds(it * (6 * T) + i * T, T)
                dve.tensor_tensor(act_lo[:, cols], tmp, act_hi[:, cols].bitcast(F32), ALU.subtract).then_inc(alo_ready, 1)

            dve.wait_ge(st_out, 64)
            with dve.Fori(0, N_UP // 6) as i:
                for c in range(6):
                    up(c, i)
            for c in range(N_UP // 6 * 6, N_UP):
                up(c)
            d = 0
            for i in range(N_DOWN):
                split_lo(U_DOWN + i + LEAD)
                while d < KD and (FT * (d + 1) - 1) // 16 == i:
                    residual(("down", d), 0, 5, d)
                    d += 1
            norm(2)
            project_in(1)
            mixer(1)
            project_out(1)
            norm(3)

            step(dve.memset(lg, 0.0))
            step(dve.memset(small[:, 512:576], 0.0))
            dve.wait_ge(lg_done, 1)
            step(dve.tensor_tensor(lg[:, 0:2 * NE], ps[:, 7, 0:2 * NE], pc("br", 0, 2 * NE), ALU.add))
            step(dve.tensor_tensor(lg[0:TS, 2 * NE:3 * NE], ps[0:TS, 7, 2 * NE:3 * NE], pc("br", 2 * NE, NE)[0:TS], ALU.add))
            g3 = lambda t: t.rearrange("p (b e) -> p b e", e=NE)
            one = lambda t: t[:, 0:3]
            wide = lambda t: one(t).unsqueeze(2).to_broadcast([P, 3, NE])
            step(dve.tensor_reduce(one(m1), g3(lg), AX.X, ALU.max))
            dve.tensor_tensor(g3(lg), g3(lg), wide(m1), ALU.subtract).then_inc(lsub_ready, 1)
            dve.wait_ge(lexp_ready, 1)
            step(dve.tensor_reduce(one(rs3), g3(ex), AX.X, ALU.add))
            step(dve.reciprocal(one(rs3), one(rs3)))
            step(dve.tensor_tensor(g3(ex), g3(ex), wide(rs3), ALU.mult))
            for top, hot in ((m1, o1), (m2, o2)):
                step(dve.tensor_reduce(one(top), g3(ex), AX.X, ALU.max))
                step(dve.tensor_tensor(g3(scr), g3(ex), wide(top), ALU.is_equal))
                step(dve.tensor_tensor(scr, scr, cc("rank"), ALU.mult))
                step(dve.tensor_reduce(one(cnt), g3(scr), AX.X, ALU.max))
                step(dve.tensor_tensor(g3(hot), g3(scr), wide(cnt), ALU.is_equal))
                if hot is o1:
                    step(dve.scalar_tensor_tensor(ex, o1, -2.0, ex, ALU.mult, ALU.add))
            step(dve.tensor_tensor(one(rs3), one(m1), one(m2), ALU.add))
            step(dve.reciprocal(one(rs3), one(rs3)))
            step(dve.tensor_tensor(sel, o1, o2, ALU.add))
            dve.tensor_scalar(sel[:, 2 * NE:3 * NE], sel[:, 2 * NE:3 * NE], cc("valid"), None, ALU.mult).then_inc(sel_ready, 1)
            step(dve.tensor_tensor(g3(o1), g3(o1), wide(m1), ALU.mult))
            step(dve.tensor_tensor(g3(o2), g3(o2), wide(m2), ALU.mult))
            step(dve.tensor_tensor(o1, o1, o2, ALU.add))
            step(dve.tensor_tensor(g3(wgt[:, 0:3 * NE]), g3(o1), wide(rs3), ALU.mult))
            for b in range(3):
                n = TS if b == 2 else P
                dve.wait_ge(tok_hi_ready, b + 1)
                if b == 2:
                    dve.wait_ge(pad_ready, DEPTH + 1)
                dve.tensor_tensor(tok_lo[0:n, b * D:(b + 1) * D].rearrange("p (a n) -> p a n", a=2),
                                  ps[0:n, 2 * b:2 * b + 2, :],
                                  tok_hi[0:n, b * D:(b + 1) * D].bitcast(F32).rearrange("p (a n) -> p a n", a=2),
                                  ALU.subtract).then_inc(tok_lo_ready, 1)
            dve.wait_ge(pos_done, 1)
            dve.wait_ge(sel_ready, 1)
            step(dve.scalar_tensor_tensor(posm[:, 0:3 * NE], ps[:, 6, 0:3 * NE], 1000.0, sel, ALU.add, ALU.mult))
            step(dve.tensor_scalar(posm, posm, -1000.0, None, ALU.add))
            step(dve.tensor_reduce(npf[:, 0:1], ps[:, 6, 3 * NE:4 * NE].unsqueeze(1), AX.X, ALU.max))
            step(dve.tensor_scalar(npf2[:, 0:1], npf[:, 0:1], 128.5, 1.0, ALU.is_gt, ALU.add))
            step(dve.scalar_tensor_tensor(npf[:, 0:1], npf[:, 0:1], 256.5, npf2[:, 0:1], ALU.is_gt, ALU.add))
            dve.tensor_copy(npass_i[:, :], npf[:, 0:1]).then_inc(npass_ready, 1)
            dve.wait_ge(posT_done, 1)
            dve.tensor_copy(posT[0:NE, :], ps[0:NE, 7, 0:T]).then_inc(posT_ready, 1)
            dve.wait_ge(posT_ready, 1)
            dve.wait_ge(pad_ready, DEPTH + 2)
            dve.wait_ge(ylo_ready, 1)
            dve.wait_ge(npass_ready, 1)
            n_pass = dve.value_load(npass_i[0:1, 0:1], min_val=1, max_val=3)
            f3 = kt(facc)

            def select(g, q, e):
                for b in range(3):
                    dve.tensor_scalar(pe_sel[:, b * P:(b + 1) * P], cc("iota"), posm[:, bass.ds(e + b * NE, 1)],
                                      None, ALU.is_equal)
                dve.tensor_scalar(pos_e[0:NE, :], posT[0:NE, :], cc("eye8", NE)[:, bass.ds(e, 1)], None, ALU.mult)\
                    .then_inc(psel_ready, 1)

            def gather(g, q, part, bank=7):
                if 2 <= part < 4:
                    cols = slice((part - 2) * 512, (part - 1) * 512)
                    dve.wait_ge(hthi_ready, g * 2 + part - 1)
                    dve.tensor_tensor(ht_lo[q][:, cols], ps[:, bank, :], ht_hi[q][:, cols].bitcast(F32), ALU.subtract)\
                        .then_inc(htlo_ready, 1)
                elif part == 4:
                    dve.wait_ge(gw_done, g + 1)
                    dve.tensor_copy(pslot[q], ps[:, 7, 0:1])
                    dve.tensor_scalar(pt_sel[q][:, :], ps[:, 7, 8:8 + T], cc("ipart"), None, ALU.is_equal)\
                        .then_inc(ptsel_ready, 1)

            def add_output(at_, d, bank):
                dve.wait_ge(scat_done, at_ + d + 1)
                dve.tensor_tensor(f3[:, d], ps[:, bank, 0:T], f3[:, d], ALU.add).then_inc(facc_added, 1)

            with dve.Fori(0, n_pass) as p_:
                select(p_ * (NE + 1), 0, 0)
                for part in range(5):
                    gather(p_ * (NE + 1), 0, part, part)
                with dve.Fori(0, NE // 2) as pair:
                    for q in range(2):
                        it = p_ * NE + pair * 2 + q
                        g = p_ * (NE + 1) + pair * 2 + (q + 1)

                        def rest_hidden(c):
                            dve.wait_ge(eahi_ready, it * FC + c + 1)
                            dve.tensor_tensor(at_lo[:, :], ps[:, 4, :], at_hi[:, :].bitcast(F32), ALU.subtract)\
                                .then_inc(ealo_ready, 1)

                        for k, (kind, c, half) in enumerate(expert_units()):
                            split_lo(U_MOE + k + LEAD, it, PER_EXPERT)
                            if kind == "g" and half and c:
                                rest_hidden(c - 1)
                            if kind == "u" and half:
                                dve.wait_ge(eg_gate, it * FC + c + 1)
                                dve.wait_ge(unit_used, later(U_MOE + k + 1, it, PER_EXPERT))
                                dve.tensor_tensor(ae[c % 2][:, :], ps[:, 2 + c % 2, :], sge[c % 2][:, :], ALU.mult)\
                                    .then_inc(eg_prod, 1)
                            if (kind, c, half) == ("d", FC - 2, 1):
                                rest_hidden(FC - 1)
                            if k - 1 in SCATTER_AT:
                                add_output(it * KD, SCATTER_AT.index(k - 1), 7)
                            if k == GATHER_AT[0] - 1:
                                select(g, 1 - q, pair * 2 + (q + 1))
                            if k - 1 in GATHER_AT:
                                gather(g, 1 - q, GATHER_AT.index(k - 1))
                        dve.wait_ge(facc_added, it * KD + KD)
                        dve.wait_ge(yhi_ready, it + 1)
                        dve.scalar_tensor_tensor(ye_lo[:, :].rearrange("p (a n) -> p a n", a=2), ps[:, 5:7, :], pslot[q],
                                                 ye_hi[:, :].bitcast(F32).rearrange("p (a n) -> p a n", a=2),
                                                 ALU.mult, ALU.subtract).then_inc(ylo_ready, 1)
                dve.tensor_scalar(posm, posm, -128.0, None, ALU.add)
                dve.tensor_scalar(posT[0:NE, :], posT[0:NE, :], -128.0, None, ALU.add).then_inc(pass_step, 1)
                dve.wait_ge(pass_step, p_ + 1)
            end = dve.snap(n_pass * (NE * KD))
            for d in range(KD):
                add_output(end, d, d % 4)
            dve.wait_ge(facc_added, end + KD)
            for d in range(KD):
                add_gated(f3[:, d], mod3[1][:, 5], d, None)
            dve.wait_ge(x_ready, KD * 4)
            dve.wait_ge(rstd_ready, 5)
            step(dve.tensor_tensor(sq3, x3, rstd[:, :].unsqueeze(1).to_broadcast([P, KD, T]), ALU.mult))
            dve.tensor_tensor(hf3, sq3, pc("gf").unsqueeze(2).to_broadcast([P, KD, T]), ALU.mult).then_inc(y_ready, 1)

        @block.tensor
        def _(pe):
            mm = pe.matmul

            def heads(t, rows, n):
                return t[0:rows, 0:H * n].rearrange("p (h n) -> p h n", h=H)

            def bank_heads(bank, rows, n):
                return ps[0:rows, bank, 0:H * n].rearrange("p (h n) -> p h n", h=H)

            def three(out, w_hi, w_lo, x_hi, x_lo, start, stop):
                mm(out, w_hi, x_hi, start=start, stop=False)
                mm(out, w_hi, x_lo, start=False, stop=False)
                return mm(out, w_lo, x_hi, start=False, stop=stop)

            def ada_unit(u, half, bank, it=None):
                pe.wait_ge(lo_split, later(u + 1, it, 6))
                cst3 = cstat[:, :].rearrange("p (k c) -> p k c", k=KD)
                for k in range(4):
                    for i, w in enumerate((whi, wlo)):
                        last = mm(ps[0:2 * NC_, bank, :], cst3[:, 4 * half + k], w[u % NSPLIT][:, k * 512:(k + 1) * 512],
                                  start=(half == 0 and k == 0 and i == 0), stop=(half == 1 and k == 3 and i == 1))
                last.then_inc(unit_used, 1)

            def ada_columns(l, j, rows_at, it=None):
                pe.wait_ge(row_ready, later(rows_at, it, 3))
                for q in range(4):
                    c = (4 * j + q) * NC_
                    cols = slice(c, c + NC_) if it is None else bass.ds(it * (12 * NC_) + c, NC_)
                    last = mm(ps[:, 7, cols], modrow[l][j % 3][0:2 * NC_, q * P:(q + 1) * P], cc("comb", 2 * NC_),
                              start=True, stop=True)
                last.then_inc(modT_ready, 1)

            def sums(src3, n, banks, done):
                for i in range(n):
                    last = mm(ps[:, banks[i], 0:T], cc("ones"), src3[:, i], start=True, stop=True)
                last.then_inc(done, 1)

            def norm(n):
                bank = 0 if n < 4 and n != 2 else 7
                if n % 2:
                    bank, use, _ = tiles[(("out", n // 2), 2, 0)]
                    pe.wait_ge(bank_free[bank], use + 1)
                for k in range(KD):
                    pe.wait_ge(sq_ready, KD * n + k + 1)
                    last = mm(ps[:, bank, 0:T], cc("ones"), kt(sqx[n])[:, k], start=(k == 0), stop=(k == KD - 1))
                last.then_inc(ss_ready, 1)

            def pair(phase, i, u, ready=None, it=None):
                pe.wait_ge(lo_split, later(u + 1, it, 6))
                for s in range(2):
                    bank, use, _ = tiles[(phase, i, s)]
                    if use:
                        pe.wait_ge(bank_free[bank], later(use, it, 3))
                    for k in range(KD):
                        if ready is not None and i == 0 and s == 0 and k % 4 == 0:
                            pe.wait_ge(ready[0], ready[1] + k // 4)
                        w = slice((s * KD + k) * P, (s * KD + k + 1) * P)
                        last = three(ps[:, bank, 0:T], whi[u % NSPLIT][:, w], wlo[u % NSPLIT][:, w], hi3[:, k], lo3[:, k],
                                     k == 0, k == KD - 1)
                    last.then_inc(unit_used if s else tile_done, 1)

            def block_start(l, b, blk_i, n):
                pe.wait_ge(gb_ready, 3 * l + blk_i + 1)
                q3 = kt(qkv, QKV_T)
                cols = slice(blk_i * P, blk_i * P + n)
                for h in range(H):
                    mm(bank_heads(b, P, n)[:, h], heads(blk[b]["MT"], n, P)[:, h], cc("triS" if blk_i == 2 else "tri", n, n),
                       start=True, stop=True)
                for h in range(H):
                    mm(bank_heads(2 + b, n, n)[:, h], q3[:, H + h, cols], q3[:, H + h, cols], start=True, stop=True)
                for h in range(H):
                    last = mm(bank_heads(4 + b, n, n)[:, h], q3[:, H + h, cols], q3[:, h, cols], start=True, stop=True)
                last.then_inc(mm1_done, 1)

            def transpose_a(l, b, blk_i, n):
                pe.wait_ge(A_ready, 3 * l + blk_i + 1)
                for h in range(H):
                    last = pe.transpose(bank_heads(b, n, n)[:, h], heads(blk[b]["da"], n, n)[:, h], cc("ident", n, n))
                last.then_inc(at_done, 1)

            def level_pm(l, b, blk_i, n, q):
                pe.wait_ge(mt_ready, 13 * l + q + 1)
                if q in (0, 1, 12):
                    pe.wait_ge(linit_ready, 3 * l + blk_i + 1)
                else:
                    pe.wait_ge(l_ready, 13 * l + q - 1)
                for h in range(H):
                    last = mm(bank_heads(2 + b, n, n)[:, h], heads(blk[b]["MT"], n, n)[:, h], heads(blk[b]["L"], n, n)[:, h],
                              start=True, stop=True)
                last.then_inc(pm_done, 1)

            def level_q(l, b, blk_i, n, q, s, final):
                half = lambda t, i: t.rearrange("p (g c) -> p g c", c=2 * s)[:, :, i * s:(i + 1) * s]
                pe.wait_ge(pm_copied, 13 * l + q + 1)
                if q in (0, 1, 12):
                    pe.wait_ge(qk_ready, 3 * l + blk_i + 1)
                LT, PM = heads(blk[b]["LT"], n, n), heads(blk[b]["PM"], n, n)
                if not final:
                    for h in range(H):
                        mm(half(bank_heads(4 + b, n, n)[:, h], 0), LT[:, h], half(PM[:, h], 0), start=True, stop=True)
                for h in range(H):
                    last = mm(half(bank_heads(6 + b, n, n)[:, h], 1), PM[:, h], half(LT[:, h], 1), start=True, stop=True)
                last.then_inc(q_done, 1)

            def tokens_kv(l, b, blk_i, n):
                pe.wait_ge(silu_done, H * (l + 1))
                for bank, first in ((b, H), (2 + b, 2 * H)):
                    for h in range(H):
                        last = pe.transpose(bank_heads(bank, n, P)[:, h],
                                            kt(qkv, QKV_T)[:, first + h, blk_i * P:blk_i * P + n], cc("ident"))
                last.then_inc(kv_done, 1)

            def w_rows(l, b, blk_i, n, q):
                pe.wait_ge(kv_ready, 3 * l + blk_i + 1)
                pe.wait_ge(l_ready, 13 * l + q + 1)
                for h in range(H):
                    last = mm(bank_heads(4 + b, P, n)[:, h], heads(blk[b]["da"], n, P)[:, h], heads(blk[b]["LT"], n, n)[:, h],
                              start=True, stop=True)
                last.then_inc(w_done, 1)

            def mixer(l):
                pe.wait_ge(qsq_ready, l + 1)
                pe.wait_ge(ab_copied, l + 1)
                pe.wait_ge(mod_ready, DEPTH)
                for b in range(4):
                    pe.wait_ge(bank_free[b], uses_at[l][b])
                sums(kt(hf)[:, 0:4], 4, range(4), qss_ready)
                sums(kt(hf)[:, 4:8], 4, range(4, 8), qss_ready)
                pe.wait_ge(qrs_ready, 2 * l + 1)
                pe.wait_ge(g_ready, l + 1)
                for mask, maskS, c in (("tri", "triS", 0), ("after", "afterS", 12)):
                    mm(ps[:, 0, c:c + 8], cc(mask), gg[:, 0:8], start=True, stop=True)
                    last = mm(ps[:, 0, c + 8:c + 12], cc(maskS), gg[:, 8:12], start=True, stop=True)
                last.then_inc(cum_ready, 1)
                pe.wait_ge(qn_ready, 2 * l + 2)
                pe.wait_ge(beg_ready, l + 1)
                for b in range(2):
                    block_start(l, b, b, P)
                for b in range(2):
                    transpose_a(l, b, b, P)
                for i in range(len(LEVELS)):
                    for b in range(2):
                        level_pm(l, b, b, P, 2 * i + b)
                    for b in range(2):
                        level_q(l, b, b, P, 2 * i + b, LEVELS[i], i == len(LEVELS) - 1)
                    if i in (2, 4):
                        pe.wait_ge(taps_summed, CT * (l + 1))
                        pe.wait_ge(tap_prompt, CT * CK * (l + 1))
                        if i == 4:
                            pe.wait_ge(crs_ready, 2 * l + 1)
                        sums(kt(yc, CT)[:, i - 2:i], 2, range(2), cmean_done)
                    if i in (3, 5):
                        pe.wait_ge(csq_ready, 2 * l + (i - 3) // 2 + 1)
                        sums(kt(csq, CT)[:, i - 3:i - 1], 2, range(2), css_ready)
                pe.wait_ge(crs_ready, 2 * l + 2)
                for b in range(2):
                    tokens_kv(l, b, b, P)
                for b in range(2):
                    w_rows(l, b, b, P, 10 + b)
                for b in range(2):
                    pe.wait_ge(nw_ready, 3 * l + b + 1)
                    pe.wait_ge(qd_ready, 3 * l + b + 1)
                    if b:
                        pe.wait_ge(s_ready, 2 * l + 1)
                    S3 = heads(S, P, P)
                    for h in range(H):
                        out = bank_heads(6 + b, P, P)[:, h]
                        last = mm(out, heads(blk[b]["LT"], P, P)[:, h], heads(blk[b]["AT"], P, P)[:, h], start=True, stop=(b == 0))
                        if b:
                            last = mm(out, heads(blk[b]["PM"], P, P)[:, h], S3[:, h], start=False, stop=True)
                    last.then_inc(vn_done, 1)
                    pe.wait_ge(vn_ready, 3 * l + b + 1)
                    for h in range(H):
                        out = bank_heads(b, P, P)[:, h]
                        if b:
                            mm(out, S3[:, h], heads(blk[b]["er"], P, P)[:, h], start=True, stop=False)
                        last = mm(out, heads(blk[b]["MT"], P, P)[:, h], heads(blk[b]["dq"], P, P)[:, h], start=(b == 0), stop=True)
                    last.then_inc(o_done, 1)
                    for h in range(H):
                        last = mm(bank_heads(2 + b, P, P)[:, h], heads(blk[b]["L"], P, P)[:, h], heads(blk[b]["MT"], P, P)[:, h],
                                  start=True, stop=True)
                    last.then_inc(s_done, 1)
                pe.wait_ge(o_copied, 3 * l + 2)
                pe.wait_ge(s_ready, 2 * l + 2)
                n = TS
                block_start(l, 0, 2, n)
                transpose_a(l, 0, 2, n)
                level_pm(l, 0, 2, n, 12)
                level_q(l, 0, 2, n, 12, 2, True)
                tokens_kv(l, 0, 2, n)
                w_rows(l, 0, 2, n, 12)
                pe.wait_ge(nw_ready, 3 * l + 3)
                pe.wait_ge(qd_ready, 3 * l + 3)
                pe.wait_ge(sst_in, 64 * (l + 1))
                out5 = ps[:, 6, 0:2 * H * n].rearrange("p (h b s t) -> p h b s t", h=H, b=NB, s=2)
                for h in range(H):
                    mm(out5[:, h, :, 0], heads(blk[0]["AT"], n, P)[:, h], heads(blk[0]["LT"], n, n)[:, h], start=True, stop=True)
                    for b in range(NB):
                        last = mm(ps[:, 6, (h * NB + b) * 2 * TD:(h * NB + b + 1) * 2 * TD], sst[h][:, b * P:(b + 1) * P],
                                  wq[:, (h * NB + b) * 2 * TD:(h * NB + b + 1) * 2 * TD], start=False, stop=True,
                                  skip_group_check=True)
                last.then_inc(swq_done, 1)
                pe.wait_ge(swq_copied, 2 * l + 1)
                for h in range(H):
                    last = pe.transpose(bank_heads(2, n, P)[:, h], swq[:, h * n:(h + 1) * n], cc("ident"))
                last.then_inc(vn_done, 1)
                pe.wait_ge(vn_ready, 3 * l + 3)
                for h in range(H):
                    last = mm(bank_heads(0, P, n)[:, h], heads(blk[1]["er"], n, P)[:, h], heads(blk[0]["dq"], n, n)[:, h],
                              start=True, stop=True)
                last.then_inc(o_done, 1)
                pe.wait_ge(osq_ready, l + 1)
                sums(kt(osq, H), H, range(0, 8, 2), oss_ready)
                pe.wait_ge(ors_ready, l + 1)

            def project_out(l):
                for i in range(N_OUT):
                    u = U_OUT[l] + i
                    pe.wait_ge(lo_split, u + 1)
                    parts = [(0, 4), (1, 4), (0, 0), (1, 0)] if i == 0 else [(0, 4), (0, 0), (1, 4), (1, 0)]
                    for s, first in parts:
                        bank, use, _ = tiles[(("out", l), i, s)]
                        if first:
                            pe.wait_ge(mlo_ready, 2 * l + 1)
                            pe.wait_ge(bank_free[bank], use)
                        else:
                            pe.wait_ge(mlo_ready, 2 * l + 2)
                        for k in range(first, first + 4):
                            w = slice((s * KD + k) * P, (s * KD + k + 1) * P)
                            last = three(ps[:, bank, 0:T], whi[u % NSPLIT][:, w], wlo[u % NSPLIT][:, w], hi3[:, k], lo3[:, k],
                                         k == 4, k == 3)
                        if not first:
                            last.then_inc(unit_used if s else tile_done, 1)
                    pe.wait_ge(vx_ready, H * l + i + 1)
                    if i >= 2:
                        pe.wait_ge(sst_ready, H * l + i - 1)
                    for half in range(2):
                        last = mm(ps[:, 4 + 2 * (i % 2) + half, :], heads(blk[1]["MT"], TS, P)[:, i],
                                  vx[0:TS, half * 512:(half + 1) * 512], start=True, stop=True)
                    last.then_inc(sst_done, 1)

            pe.wait_ge(cstat_ready, 2)
            pe.wait_ge(con_in, 16)
            norm(0)
            with pe.Fori(0, N_ADA // 6) as i:
                for c in range(6):
                    ada_unit(c, c % 2, 4 + c // 2 % 3, i)
                    if c % 2:
                        ada_columns(0, c // 2, c // 2 + 1, i)

            def token_rates(l):
                pe.wait_ge(hf_ready, 4 * l + 2)
                a, _ = PCOL[f"wab{l}"]
                for b in range(3):
                    n = TS if b == 2 else P
                    for k in range(KD):
                        last = mm(ps[0:n, 4, 8 * b:8 * b + 8], hf3[:, k, b * P:b * P + n], par[:, a + 8 * k:a + 8 * k + 8],
                                  start=(k == 0), stop=(k == KD - 1))
                last.then_inc(ab_done, 1)

            for i in range(N_IN):
                pair(("in", 0), i, in_unit(0, i), (hlo_ready, 1))
                if i == 0:
                    token_rates(0)
                    pe.wait_ge(mod_ready, 1)
                    pe.wait_ge(rstd_ready, 1)
                else:
                    ada_columns(1, i - 1, N_IN + i)
                for half in range(2):
                    ada_unit(ada_unit_of(1, 2 * i + half), half, 5 + i % 2)
            ada_columns(1, N_IN - 1, 2 * N_IN)
            mixer(0)
            project_out(0)
            norm(1)
            with pe.Fori(0, N_UP // 6) as i:
                pe.wait_ge(hlo_ready, 4)
                for c in range(6):
                    pair("up", c, U_UP + c, None, i)
            for c in range(N_UP // 6 * 6, N_UP):
                pair("up", c, U_UP + c)
            pe.wait_ge(alo_ready, N_UP)
            for n in range(FT * KD):
                d, f = divmod(n, FT)
                u = U_DOWN + n // 16
                bank, use, _ = tiles[("down", d)]
                if n % 16 == 0:
                    pe.wait_ge(lo_split, u + 1)
                if f == 0:
                    pe.wait_ge(bank_free[bank], use)
                w = slice((n % 16) * P, (n % 16 + 1) * P)
                cols = slice(f * T, (f + 1) * T)
                last = three(ps[:, bank, 0:T], whi[u % NSPLIT][:, w], wlo[u % NSPLIT][:, w], act_hi[:, cols], act_lo[:, cols],
                             f == 0, f == FT - 1)
                if n % 16 == 15:
                    last.then_inc(unit_used, 1)
                elif f == FT - 1:
                    last.then_inc(tile_done, 1)
            norm(2)
            for i in range(N_IN):
                pair(("in", 1), i, in_unit(1, i), (hlo_ready, 5))
                if i == 0:
                    token_rates(1)
            mixer(1)
            project_out(1)
            norm(3)
            pe.wait_ge(hf_ready, 8)
            pe.wait_ge(rstd_ready, 4)
            a, _ = PCOL["wr"]
            for b in range(3):
                n = TS if b == 2 else P
                for k in range(KD):
                    last = mm(ps[0:n, 7, NE * b:NE * b + NE], hf3[:, k, b * P:b * P + n], par[:, a + NE * k:a + NE * k + NE],
                              start=(k == 0), stop=(k == KD - 1))
            last.then_inc(lg_done, 1)
            for b in range(3):
                n = TS if b == 2 else P
                for k in range(KD):
                    last = pe.transpose(ps[0:n, 2 * b + k // 4, (k % 4) * P:(k % 4 + 1) * P], hf3[:, k, b * P:b * P + n],
                                        cc("ident"))
                last.then_inc(tokT_done, 1)
            pe.wait_ge(sel_ready, 1)
            s8 = lambda b: sel[:, NE * b:NE * b + NE]
            for b in range(3):
                for a in range(b):
                    mm(ps[:, 6, NE * b:NE * b + NE], cc("ones"), s8(a), start=(a == 0), stop=False)
                mm(ps[:, 6, NE * b:NE * b + NE], cc("before"), s8(b), start=(b == 0), stop=True)
            for b in range(3):
                last = mm(ps[:, 6, 3 * NE:4 * NE], cc("ones"), s8(b), start=(b == 0), stop=(b == 2))
            last.then_inc(pos_done, 1)
            pe.wait_ge(npass_ready, 1)
            for b in range(3):
                n = TS if b == 2 else P
                last = mm(ps[0:NE, 7, b * P:b * P + n], posm[0:n, NE * b:NE * b + NE], cc("ident", n, n), start=True, stop=True)
            last.then_inc(posT_done, 1)
            pe.wait_ge(tok_lo_ready, 3)
            n_pass = pe.value_load(npass_i[0:1, 0:1], min_val=1, max_val=3)

            def gather(g, q, part, bank=7):
                if part == 0:
                    pe.wait_ge(psel_ready, g + 1)
                elif bank == 7 and part in (1, 3, 4):
                    pe.wait_ge(gx_copied if part == 1 else htlo_ready, g * 2 + (1 if part < 4 else 2))
                if part in (2, 3):
                    pe.wait_ge(gx_copied, g * 2 + part - 1 if bank == part else g * 2 + 2)
                if part < 2:
                    for i, tok in enumerate((tok_hi, tok_lo)):
                        for b in range(3):
                            last = mm(ps[:, bank, :], pe_sel[:, b * P:(b + 1) * P],
                                      tok[:, b * D + part * 512:b * D + (part + 1) * 512],
                                      start=(i == 0 and b == 0), stop=(i == 1 and b == 2))
                    last.then_inc(gx_done, 1)
                elif part < 4:
                    for d in range(4):
                        c = (4 * (part - 2) + d) * P
                        last = pe.transpose(ps[:, bank, d * P:(d + 1) * P], xe[:, c:c + P], cc("ident"))
                    last.then_inc(gt_done, 1)
                else:
                    for b in range(3):
                        mm(ps[:, 7, 0:1], pe_sel[:, b * P:(b + 1) * P].bitcast(F32), wgt[:, bass.ds(q + b * NE, 1)],
                           start=(b == 0), stop=(b == 2))
                    mm(ps[:, 7, 8:8 + T], cc("ones", NE), pos_e[0:NE, :], start=True, stop=True).then_inc(gw_done, 1)

            def scatter(d, q, bank):
                w = slice(d * P, (d + 1) * P)
                mm(ps[:, bank, 0:T], ye_hi[:, w], pt_sel[q][:, :], start=True, stop=False)
                mm(ps[:, bank, 0:T], ye_lo[:, w], pt_sel[q][:, :], start=False, stop=True).then_inc(scat_done, 1)

            with pe.Fori(0, n_pass) as p_:
                for part in range(5):
                    gather(p_ * (NE + 1), 0, part, part if part < 4 else 7)
                with pe.Fori(0, NE // 2) as pair:
                    for q in range(2):
                        it = p_ * NE + pair * 2 + q
                        g = p_ * (NE + 1) + pair * 2 + (q + 1)
                        pe.wait_ge(htlo_ready, g * 2)

                        def hidden_rows(c):
                            pe.wait_ge(eg_prod, it * FC + c + 1)
                            for i in range(4):
                                last = pe.transpose(ps[:, 4, i * P:(i + 1) * P], ae[c % 2][:, i * P:(i + 1) * P], cc("ident"))
                            last.then_inc(eT_done, 1)

                        for k, (kind, c, half) in enumerate(expert_units()):
                            if (kind, half) == ("u", 0) and c:
                                hidden_rows(c - 1)
                            if (kind, c, half) == ("d", FC - 1, 0):
                                hidden_rows(FC - 1)
                            u = U_MOE + k
                            pe.wait_ge(lo_split, later(u + 1, it, PER_EXPERT))
                            if kind == "d":
                                if half == 0:
                                    pe.wait_ge(ealo_ready, it * FC + c + 1)
                                bank, a_hi, a_lo, first, end = 5 + half, at_hi, at_lo, c == 0, c == FC - 1
                                off = 0
                            else:
                                if c >= 2 and half == 0:
                                    pe.wait_ge(eg_gate if kind == "g" else eg_prod, it * FC + c - 1)
                                bank, first, end = (0 if kind == "g" else 2) + c % 2, half == 0, half == 1
                                a_hi, a_lo, off = ht_hi[q], ht_lo[q], 4 * half
                            for i in range(4):
                                a = slice((off + i) * P, (off + i + 1) * P)
                                w = slice(i * 512, (i + 1) * 512)
                                mm(ps[:, bank, :], a_hi[:, a], whi[u % NSPLIT][:, w], start=(first and i == 0), stop=False)
                                mm(ps[:, bank, :], a_hi[:, a], wlo[u % NSPLIT][:, w], start=False, stop=False)
                                last = mm(ps[:, bank, :], a_lo[:, a], whi[u % NSPLIT][:, w], start=False, stop=(end and i == 3))
                            last.then_inc(unit_used, 1)
                            if k in SCATTER_AT:
                                d = SCATTER_AT.index(k)
                                if d:
                                    pe.wait_ge(facc_added, it * KD + d)
                                else:
                                    pe.wait_ge(ylo_ready, it + 1)
                                    pe.wait_ge(ptsel_ready, g)
                                scatter(d, 1 - q, 7)
                            if k in GATHER_AT:
                                if k == GATHER_AT[0]:
                                    pe.wait_ge(facc_added, it * KD + KD)
                                part = GATHER_AT.index(k)
                                gather(g, pair * 2 + (q + 1) if part == 4 else None, part)
            end = pe.snap(n_pass * NE + 1)
            pe.wait_ge(ylo_ready, end)
            end = pe.snap(n_pass * (NE * KD))
            for d in range(KD):
                if d >= 4:
                    pe.wait_ge(facc_added, end + (d - 3))
                scatter(d, 1, d % 4)
            norm(4)


def pack_units(w_ada, w_in, w_out, w_gate, w_up, w_down, e_gate, e_up, e_down):
    out = np.empty((N_UNITS + NRAW, P, UNIT), np.float32)

    def column_units(w, first):
        m = w.shape[1] // 512
        out[first] = w.reshape(2, 4, P, m, 512).transpose(3, 0, 2, 1, 4).reshape(2 * m, P, UNIT)

    def tile_units(w, cols, first):
        t = np.stack([w[:, c:c + P] for c in cols])
        t = t.reshape(len(cols) // 2, 2, KD, P, P).transpose(0, 3, 1, 2, 4)
        out[first] = t.reshape(len(cols) // 2, P, UNIT)

    for l in range(DEPTH):
        column_units(w_ada[l], [ada_unit_of(l, v) for v in range(N_ADA)])
        tile_units(w_in[l], IN_COLS, [in_unit(l, i) for i in range(N_IN)])
        tile_units(w_out[l], [P * d for d in range(KD)], slice(U_OUT[l], U_OUT[l] + N_OUT))
    pair = np.stack([w_gate[0].reshape(D, FT, P), w_up[0].reshape(D, FT, P)], 2).reshape(D, 2 * FT * P)
    tile_units(pair, [P * i for i in range(2 * FT)], slice(U_UP, U_UP + N_UP))
    t = w_down[0].reshape(FT, P, KD, P).transpose(2, 0, 1, 3).reshape(N_DOWN, 16, P, P)
    out[U_DOWN:U_DOWN + N_DOWN] = t.transpose(0, 2, 1, 3).reshape(N_DOWN, P, UNIT)
    for k, (kind, c, half) in enumerate(expert_units()):
        if kind == "d":
            w = e_down[0][:, c * 512:(c + 1) * 512, half * 512:(half + 1) * 512]
        else:
            w = (e_gate if kind == "g" else e_up)[0][:, half * 512:(half + 1) * 512, c * 512:(c + 1) * 512]
        w = w.reshape(NE, 4, P, 512).transpose(0, 2, 1, 3).reshape(NE, P, UNIT)
        out[U_MOE + k:U_MOE + NE * PER_EXPERT:PER_EXPERT] = w
    out[N_UNITS:] = out[U_MOE:U_MOE + NRAW]
    return out


def channel_major(a, tiles_n):
    return a.reshape(a.shape[0], tiles_n, P).transpose(2, 1, 0)


def kernel(**inputs):
    import concourse.bacc as bacc
    from concourse.bass_utils import run_bass_kernel_spmd

    g = {k: np.asarray(v) for k, v in inputs.items()}
    arrays = {}
    arrays["units"] = pack_units(g["w_ada"], g["w_in"], g["w_out"], g["w_ff_gate"], g["w_ff_up"], g["w_ff_down"],
                                 g["w_exp_gate"], g["w_exp_up"], g["w_exp_down"])
    tokens = np.concatenate([g["x_prompt"].reshape(TP, D), g["x_sample"].reshape(TS, D)])
    arrays["x_in"] = channel_major(tokens, KD).reshape(P, KD * T)
    arrays["c_in"] = channel_major(np.concatenate([g["c_prompt"], g["c_sample"]]), KD).reshape(P, KD * NC_)
    par = np.empty((P, NPAR), np.float32)

    def put(name, a):
        lo, hi = PCOL[name]
        par[:, lo:hi] = a.reshape(P, hi - lo)

    for l in range(DEPTH):
        put(f"b_ada{l}", channel_major(g["b_ada"][l][None], MODS * KD))
        put(f"g1{l}", channel_major(g["g_norm1"][l][None], KD))
        put(f"g2{l}", channel_major(g["g_norm2"][l][None], KD))
        put(f"wq{l}", channel_major(g["w_gdn_conv"][l], QKV_T))
        put(f"wc{l}", channel_major(g["w_conf_dw"][l], CT))
        put(f"bc{l}", channel_major(g["b_conf_dw"][l][None], CT))
        put(f"gln{l}", channel_major(g["g_conf_ln"][l][None], CT))
        put(f"bln{l}", channel_major(g["b_conf_ln"][l][None], CT))
        put(f"gout{l}", g["g_gdn_out"][l][:, None])
        put(f"wab{l}", np.ascontiguousarray(g["w_in"][l][:, COL_B:COL_B + 8].reshape(KD, P, 8).transpose(1, 0, 2)))
        put(f"alog{l}", np.broadcast_to(np.tile(g["a_log"][l], 3), (P, 12)))
        put(f"dt{l}", np.broadcast_to(np.tile(g["dt_bias"][l], 3), (P, 12)))
    put("wr", np.ascontiguousarray(g["w_router"][0].reshape(KD, P, NE).transpose(1, 0, 2)))
    put("br", np.broadcast_to(np.tile(g["b_router"][0], 3), (P, 3 * NE)))
    put("gf", channel_major(g["g_final"][None], KD))
    arrays["par_in"] = par
    arrays["const_in"] = constants()
    arrays["gdn_in"] = g["state_gdn"].transpose(0, 2, 3, 1, 4).reshape(DEPTH, H, P, NB * P)

    def pads(state, tiles_n, seg):
        rows = state.shape[2]
        a = np.zeros((DEPTH, P, tiles_n, NB, seg), np.float32)
        a[..., :rows] = state.reshape(DEPTH, NB, rows, tiles_n, P).transpose(0, 4, 3, 1, 2)
        return a.reshape(DEPTH, P, tiles_n * NB * seg)

    arrays["qst_in"] = pads(g["state_gdn_conv"], QKV_T, QSEG)
    arrays["cst_in"] = pads(g["state_conf_conv"], CT, CSEG)
    arrays = {k: np.ascontiguousarray(v, np.float32) for k, v in arrays.items()}

    nc = bacc.Bacc("TRN2", target_bir_lowering=False, num_devices=1, dynamic_dma_scratch_size=4096)
    args = [nc.dram_tensor(k, v.shape, F32, kind="ExternalInput").ap() for k, v in arrays.items()]
    outs = {"y_out": (P, KD * T), "gdnp_out": (DEPTH, P, H * P), "gdns_out": (DEPTH, H, P, NB * P),
            "qst_out": (DEPTH, P, QKV_T * QPAD), "cst_out": (DEPTH, P, CT * CPAD)}
    args += [nc.dram_tensor(k, s, F32, kind="ExternalOutput").ap() for k, s in outs.items()]
    program(nc, *args)
    r = run_bass_kernel_spmd(nc, [arrays], core_ids=[0]).results[0]

    y = r["y_out"].reshape(P, KD, T).transpose(2, 1, 0).reshape(T, D)
    q = r["qst_out"].reshape(DEPTH, P, QKV_T, QPAD)
    c = r["cst_out"].reshape(DEPTH, P, CT, CPAD)

    def rows(a, first, n):
        a = a[..., first:first + n]
        axes = (0, *range(3, a.ndim), 2, 1)
        a = a.transpose(axes)
        return np.ascontiguousarray(a.reshape(*a.shape[:-2], -1))

    return (
        np.ascontiguousarray(y[:TP].reshape(1, TP, D)),
        np.ascontiguousarray(y[TP:].reshape(NB, TD, D)),
        np.ascontiguousarray(r["gdnp_out"].reshape(DEPTH, P, H, P).transpose(0, 2, 1, 3)[:, None]),
        rows(q, QSAMP - (CW - 1), CW - 1)[:, None],
        rows(c, CSAMP - (CK - 1), CK - 1)[:, None],
        np.ascontiguousarray(r["gdns_out"].reshape(DEPTH, H, P, NB, P).transpose(0, 3, 1, 2, 4)),
        rows(q[..., QSAMP:].reshape(DEPTH, P, QKV_T, NB, QSEG), QSEG - (CW - 1), CW - 1),
        rows(c[..., CSAMP:].reshape(DEPTH, P, CT, NB, CSEG), CSEG - (CK - 1), CK - 1),
    )
```
